# Optimizing a Trainium2 kernel written in Bass

```python
import math
import jax, jax.numpy as jnp
from jax import lax
import numpy as np

D_MODEL = 1024
BATCH = 1
SEQ = 512
DEPTH = 2

CHUNK = 64
Q_BLOCK = 128
A_WIDTH = D_MODEL // 2
A_HEADS = 4
A_DK = A_WIDTH // A_HEADS
A_DV = A_WIDTH // A_HEADS
B_WIDTH = D_MODEL - A_WIDTH
B_HEADS = 4
B_HEAD_DIM = B_WIDTH // (2 * B_HEADS)
EVEN_IN = 4 * A_WIDTH + 3 * B_WIDTH
C_HEADS = 16
C_HEAD_DIM = D_MODEL // C_HEADS
ODD_IN = 4 * D_MODEL + C_HEADS
D_FF = -(-8 * D_MODEL // (3 * 256)) * 256
N_EVEN = (DEPTH + 1) // 2
N_ODD = DEPTH // 2
ALPHA = (2 * DEPTH) ** 0.25
BETA = (8 * DEPTH) ** -0.25
MASK_VALUE = -1e30

kernel_name = "hybrid_hgrn2_diffattn_fox_deepnorm"

F32 = jnp.float32

def _layer_norm(x, g, b, eps=1e-5):
    xf = x.astype(F32)
    mu = jnp.mean(xf, axis=-1, keepdims=True)
    var = jnp.mean(jnp.square(xf - mu), axis=-1, keepdims=True)
    return ((xf - mu) * lax.rsqrt(var + eps) * g.astype(F32) + b.astype(F32)).astype(x.dtype)

def _rms_norm(x, g, eps=1e-6):
    xf = x.astype(F32)
    return xf * lax.rsqrt(jnp.mean(xf * xf, axis=-1, keepdims=True) + eps) * g.astype(F32)

def _swiglu(x, w1, w2):
    gate, up = jnp.split(x @ w1, 2, axis=-1)
    return (jax.nn.silu(gate) * up) @ w2

def _hgrn2(q_raw, f_raw, i, lb):
    Bsz, S = q_raw.shape[:2]
    nc = S // CHUNK
    lbh = lb.reshape(A_HEADS, A_DK).astype(F32)
    z = f_raw.astype(F32)
    q = jax.nn.silu(q_raw.astype(F32))
    f = lbh + (1.0 - lbh) * jax.nn.sigmoid(z)
    k = 1.0 - f
    logf = jnp.log(f)

    def to_chunks(t):
        return t.reshape(Bsz, nc, CHUNK, A_HEADS, -1).transpose(1, 0, 3, 2, 4)

    qc, kc, ic, lc = to_chunks(q), to_chunks(k), to_chunks(i.astype(F32)), to_chunks(logf)
    causal = jnp.tril(jnp.ones((CHUNK, CHUNK), bool))[:, :, None]

    def step(state, inp):
        qt, kt, it, lt = inp
        b = jnp.cumsum(lt, axis=2)
        o_inter = jnp.einsum('bhtk,bhkv->bhtv', qt * jnp.exp(b), state)
        rel = b[:, :, :, None, :] - b[:, :, None, :, :]
        decay = jnp.where(causal, jnp.exp(jnp.minimum(rel, 0.0)), 0.0)
        scores = jnp.einsum('bhtk,bhsk,bhtsk->bhts', qt, kt, decay)
        o_intra = jnp.einsum('bhts,bhsv->bhtv', scores, it)
        b_last = b[:, :, -1, :]
        state = jnp.exp(b_last)[..., None] * state + jnp.einsum(
            'bhsk,bhsv->bhkv', kt * jnp.exp(b_last[:, :, None, :] - b), it)
        return state, o_inter + o_intra

    s0 = jnp.zeros((Bsz, A_HEADS, A_DK, A_DV), F32)
    _, o = lax.scan(step, s0, (qc, kc, ic, lc))
    return o.transpose(1, 0, 3, 2, 4).reshape(Bsz, S, A_HEADS, A_DV)

def _diff_attention(q, k, v, lam):
    Bsz, H, _, S, d = q.shape
    scale = d ** -0.5
    k_chunk = jnp.arange(S) // CHUNK

    def block(bi):
        start = bi * Q_BLOCK
        qb = lax.dynamic_slice_in_dim(q, start, Q_BLOCK, axis=3)
        s = jnp.einsum('bhcqd,bhckd->bhcqk', qb, k) * scale
        q_chunk = (start + jnp.arange(Q_BLOCK)) // CHUNK
        mask = k_chunk[None, :] <= q_chunk[:, None]
        p = jax.nn.softmax(jnp.where(mask, s, MASK_VALUE), axis=-1)
        attn = p[:, :, 0] - lam * p[:, :, 1]
        return jnp.einsum('bhqk,bhkv->bhqv', attn, v)

    o = lax.map(block, jnp.arange(S // Q_BLOCK))
    return o.transpose(1, 0, 3, 2, 4).reshape(Bsz, S, H, -1)

def _fox_attention(q, k, v, c):
    Bsz, H, S, d = q.shape
    scale = d ** -0.5
    k_pos = jnp.arange(S)

    def block(bi):
        start = bi * Q_BLOCK
        qb = lax.dynamic_slice_in_dim(q, start, Q_BLOCK, axis=2)
        cb = lax.dynamic_slice_in_dim(c, start, Q_BLOCK, axis=2)
        s = jnp.einsum('bhqd,bhkd->bhqk', qb, k) * scale + (cb[..., :, None] - c[..., None, :])
        q_pos = start + jnp.arange(Q_BLOCK)
        mask = k_pos[None, :] <= q_pos[:, None]
        p = jax.nn.softmax(jnp.where(mask, s, MASK_VALUE), axis=-1)
        return jnp.einsum('bhqk,bhkd->bhqd', p, v)

    o = lax.map(block, jnp.arange(S // Q_BLOCK))
    return o.transpose(1, 0, 3, 2, 4).reshape(Bsz, S, H, d)

def _even_mixer(x, w_in, w_out, lb, lq1, lk1, lq2, lk2, hgrn_g, diff_g, layer_idx):
    Bsz, S, _ = x.shape
    proj = x @ w_in
    cuts = [A_WIDTH, 2 * A_WIDTH, 3 * A_WIDTH, 4 * A_WIDTH,
            4 * A_WIDTH + B_WIDTH, 4 * A_WIDTH + 2 * B_WIDTH]
    a_q, a_f, a_i, a_g, b_q, b_k, b_v = jnp.split(proj, cuts, axis=-1)
    heads_a = lambda t: t.reshape(Bsz, S, A_HEADS, -1)
    o_a = _hgrn2(heads_a(a_q), heads_a(a_f), heads_a(a_i), lb)
    o_a = _rms_norm(o_a, hgrn_g) * jax.nn.silu(heads_a(a_g).astype(F32))
    lam_init = 0.8 - 0.6 * math.exp(-0.3 * layer_idx)
    lam = (jnp.exp(jnp.sum(lq1.astype(F32) * lk1.astype(F32)))
           - jnp.exp(jnp.sum(lq2.astype(F32) * lk2.astype(F32))) + lam_init)
    qd = b_q.reshape(Bsz, S, B_HEADS, 2, B_HEAD_DIM).transpose(0, 2, 3, 1, 4).astype(F32)
    kd = b_k.reshape(Bsz, S, B_HEADS, 2, B_HEAD_DIM).transpose(0, 2, 3, 1, 4).astype(F32)
    vd = b_v.reshape(Bsz, S, B_HEADS, 2 * B_HEAD_DIM).transpose(0, 2, 1, 3).astype(F32)
    o_b = _diff_attention(qd, kd, vd, lam)
    o_b = _rms_norm(o_b, diff_g) * (1.0 - lam_init)
    o = jnp.concatenate([o_a.reshape(Bsz, S, A_WIDTH), o_b.reshape(Bsz, S, B_WIDTH)], axis=-1)
    return o.astype(x.dtype) @ w_out

def _odd_mixer(x, w_in, w_out, b_f, qn_g, kn_g):
    Bsz, S, _ = x.shape
    proj = x @ w_in
    q, k, v, g, f_logit = jnp.split(proj, [D_MODEL, 2 * D_MODEL, 3 * D_MODEL, 4 * D_MODEL], axis=-1)
    heads = lambda t: t.reshape(Bsz, S, C_HEADS, C_HEAD_DIM).transpose(0, 2, 1, 3)
    qh = _rms_norm(heads(q), qn_g)
    kh = _rms_norm(heads(k), kn_g)
    vh = heads(v).astype(F32)
    logf = jax.nn.log_sigmoid(f_logit.astype(F32) + b_f.astype(F32))
    c = jnp.cumsum(logf, axis=1).transpose(0, 2, 1)
    o = _fox_attention(qh, kh, vh, c).reshape(Bsz, S, D_MODEL)
    o = o * jax.nn.sigmoid(g.astype(F32))
    return o.astype(x.dtype) @ w_out

def setup_inputs(seed: int = 0) -> dict:
    key = jax.random.key(seed)
    ks = jax.random.split(key, 21)
    nrm = lambda k, shape, s: jax.random.normal(k, shape, F32) * s
    d_in = D_MODEL ** -0.5
    return {
        "x": nrm(ks[0], (BATCH, SEQ, D_MODEL), 1.0),
        "even_w_in": nrm(ks[1], (N_EVEN, D_MODEL, EVEN_IN), d_in),
        "even_w_out": nrm(ks[2], (N_EVEN, D_MODEL, D_MODEL), d_in * BETA),
        "hgrn_lb_logits": nrm(ks[3], (N_EVEN, A_WIDTH), 0.1),
        "diff_lq1": nrm(ks[4], (N_EVEN, B_HEAD_DIM), 0.1),
        "diff_lk1": nrm(ks[5], (N_EVEN, B_HEAD_DIM), 0.1),
        "diff_lq2": nrm(ks[6], (N_EVEN, B_HEAD_DIM), 0.1),
        "diff_lk2": nrm(ks[7], (N_EVEN, B_HEAD_DIM), 0.1),
        "hgrn_norm_g": 1.0 + nrm(ks[8], (N_EVEN, A_DV), 0.02),
        "diff_norm_g": 1.0 + nrm(ks[9], (N_EVEN, 2 * B_HEAD_DIM), 0.02),
        "fox_w_in": nrm(ks[10], (N_ODD, D_MODEL, ODD_IN), d_in),
        "fox_w_out": nrm(ks[11], (N_ODD, D_MODEL, D_MODEL), d_in * BETA),
        "fox_b_f": 2.0 + nrm(ks[12], (N_ODD, C_HEADS), 0.1),
        "fox_qnorm_g": 1.0 + nrm(ks[13], (N_ODD, C_HEAD_DIM), 0.02),
        "fox_knorm_g": 1.0 + nrm(ks[14], (N_ODD, C_HEAD_DIM), 0.02),
        "ffn_w1": nrm(ks[15], (DEPTH, D_MODEL, 2 * D_FF), d_in),
        "ffn_w2": nrm(ks[16], (DEPTH, D_FF, D_MODEL), D_FF ** -0.5 * BETA),
        "ln1_g": 1.0 + nrm(ks[17], (DEPTH, D_MODEL), 0.02),
        "ln1_b": nrm(ks[18], (DEPTH, D_MODEL), 0.02),
        "ln2_g": 1.0 + nrm(ks[19], (DEPTH, D_MODEL), 0.02),
        "ln2_b": nrm(ks[20], (DEPTH, D_MODEL), 0.02),
    }

def reference(x, even_w_in, even_w_out, hgrn_lb_logits, diff_lq1, diff_lk1, diff_lq2, diff_lk2,
              hgrn_norm_g, diff_norm_g, fox_w_in, fox_w_out, fox_b_f, fox_qnorm_g, fox_knorm_g,
              ffn_w1, ffn_w2, ln1_g, ln1_b, ln2_g, ln2_b):
    lb_soft = jax.nn.softmax(hgrn_lb_logits.astype(F32), axis=0)
    lb_all = jnp.cumsum(lb_soft, axis=0) - lb_soft[0]
    for l in range(DEPTH):
        j = l // 2
        if l % 2 == 0:
            h = _even_mixer(x, even_w_in[j], even_w_out[j], lb_all[j],
                            diff_lq1[j], diff_lk1[j], diff_lq2[j], diff_lk2[j],
                            hgrn_norm_g[j], diff_norm_g[j], l)
        else:
            h = _odd_mixer(x, fox_w_in[j], fox_w_out[j], fox_b_f[j], fox_qnorm_g[j], fox_knorm_g[j])
        x = _layer_norm(ALPHA * x + h, ln1_g[l], ln1_b[l])
        x = _layer_norm(ALPHA * x + _swiglu(x, ffn_w1[l], ffn_w2[l]), ln2_g[l], ln2_b[l])
    return x


_drawn_inputs = setup_inputs


def setup_inputs(seed=0):
    import zlib

    import numpy as np

    out = dict(_drawn_inputs(seed))
    spreads = {}
    factors = {'diff_lq1': 3.054,
     'diff_lk1': 8.0,
     'diff_lq2': 8.0,
     'diff_lk2': 3.491,
     'hgrn_norm_g': 8.0,
     'diff_norm_g': 8.0,
     'fox_b_f': 64.0,
     'fox_qnorm_g': 8.0,
     'fox_knorm_g': 8.0}
    for name, (base, spread) in spreads.items():
        noise = np.random.default_rng([zlib.crc32(name.encode()), seed]).standard_normal(out[name].shape)
        drawn = base * np.exp(spread * noise) if base else spread * noise
        out[name] = __import__('jax').numpy.asarray(drawn.astype(out[name].dtype))
    for name, factor in factors.items():
        out[name] = (out[name] * factor).astype(out[name].dtype)
    return out
```

```python
import math
from contextlib import ExitStack

import concourse.bass as bass
from concourse import mybir

F32 = mybir.dt.float32
F32R = mybir.dt.float32r
BF16 = mybir.dt.bfloat16
U16 = mybir.dt.uint16
ALU = mybir.AluOpType
ACT = mybir.ActivationFunctionType
AX_X = mybir.AxisListType.X

P = 128
D = 1024
TS = 512
NT = TS // P
KD = D // P
DEPTH = 2
AH = 4
FH = 16
HD = 64
CHUNK = 64
HA = HD + 2
D_FF = 2816
NF = D_FF // P
ALPHA = (2 * DEPTH) ** 0.25
LAM_INIT = 0.8 - 0.6 * math.exp(-0.3 * 0)
LEVELS = [64, 32, 16, 8, 4, 2, 1]
SLOT = 2048
RAW = 2
RING = 3
PIECES = 4
TINY = 2.0 ** -64


def weight_chunks(w):
    out = []

    def feature_major(stage, m, n0):
        out.append((stage, [(0, m[:, n0:n0 + 256].rearrange("(k p) n -> p k n", p=P), KD, 256)], KD * 256))

    def token_major(stage, m, n0, k0, nk, width=512):
        src = m[k0 * P:(k0 + nk) * P, n0:n0 + width].rearrange("(k p) n -> p k n", p=P)
        out.append((stage, [(0, src, nk, width)], nk * width))

    def columns(stage, m, n0):
        token_major(stage, m, n0, 0, 4)
        token_major(stage, m, n0, 4, 4)

    def tail(l, mixer_out):
        for half in range(2):
            columns(f"out{l}", mixer_out, half * 512)
        for j in range(NF):
            w1 = w["ffn_w1"][l].rearrange("(k p) n -> p k n", p=P)
            out.append((f"up{l}", [(0, w1[:, :, j * P:(j + 1) * P], KD, P),
                                   (KD * P, w1[:, :, D_FF + j * P:D_FF + (j + 1) * P], KD, P)], SLOT))
        for half in range(2):
            k0 = 0
            for nk in [2, 4, 4, 4, 4, 4]:
                token_major(f"down{l}", w["ffn_w2"][l], half * 512, k0, nk)
                k0 += nk

    we = w["even_w_in"][0]
    for stage, n0 in (("a_f", 512), ("a_q", 0)):
        for i in range(2):
            feature_major(stage, we, n0 + 256 * i)
    columns("a_g", we, 1536)
    columns("a_i", we, 1024)
    for stage, n0 in (("b_q", 2048), ("b_k", 2560)):
        for i in range(2):
            feature_major(stage, we, n0 + 256 * i)
    columns("b_v", we, 3072)
    tail(0, w["even_w_out"][0])
    wf = w["fox_w_in"][0]
    token_major("fox_f", wf, 4 * D, 0, KD, FH)
    for half in range(2):
        for n in range(4):
            columns(f"fox{'qkvg'[n]}{half}", wf, n * D + half * 512)
    tail(1, w["fox_w_out"][0])
    return out


def build(nc, w, out):
    chunks = weight_chunks(w)
    stage_chunks = {}
    for c, (stage, _, _) in enumerate(chunks):
        stage_chunks.setdefault(stage, []).append(c)

    with ExitStack() as ctx:
        top = [-(-nc.sbuf_base // 32) * 32]

        def at(name, shape, dt, offset):
            return nc.alloc_sbuf_tensor_at(name, shape, dt, offset=offset)

        def place(name, free, dt, size):
            t = at(name, [P, *free], dt, top[0])
            n = size
            for f in free:
                n *= f
            top[0] += -(-n // 32) * 32
            return t

        x_res = place("x_res", [NT, D], F32, 4)
        xT_hi = place("xT_hi", [KD, TS], F32R, 4)
        xT_lo = place("xT_lo", [KD, TS], F32R, 4)
        w_raw = [place(f"w_raw{i}", [SLOT], F32, 4) for i in range(RAW)]
        w_hi = [place(f"w_hi{i}", [SLOT], F32R, 4) for i in range(RING)]
        w_lo = [place(f"w_lo{i}", [SLOT], F32R, 4) for i in range(RING)]
        ident = place("ident", [P], F32, 4)
        ident_bf = place("ident_bf", [P], BF16, 2)
        fox_mask = place("fox_mask", [P], BF16, 2)
        diff_mask = place("diff_mask", [P], BF16, 2)
        level_mask = place("level_mask", [len(LEVELS), P], BF16, 2)
        ln_rows = place("ln_rows", [D], F32, 4)
        stats = place("stats", [NT, 20], F32, 4)
        small = place("small", [48], F32, 4)
        gains = place("gains", [12], F32, 4)
        arena = top[0]

        def take(name, free, dt, at_el):
            t = at(name, [P, *free], dt, arena + 4 * at_el)
            n = 1
            for f in free:
                n *= f
            return t, at_el + n

        hT_hi, e = take("hT_hi", [NF, TS], F32R, 0)
        hT_lo, _ = take("hT_lo", [NF, TS], F32R, e)
        silu_g = at("silu_g", [P, NF, TS], F32, arena + 4 * NF * TS)
        qT, e = take("qT", [AH, TS], F32, 0)
        kT, e = take("kT", [AH, TS], F32, e)
        bT, e = take("bT", [AH, TS], F32, e)
        q_dec, e = take("q_dec", [TS], F32, e)
        k_dec, e = take("k_dec", [TS], F32, e)
        k_dec2, e = take("k_dec2", [3, P], F32, e)
        scT, e = take("scT", [2, 10, P], F32, e)
        iv, e = take("iv", [NT, 512], F32, e)
        bqT, e = take("bqT", [AH, TS], F32, e)
        bkT, e = take("bkT", [AH, TS], F32, e)
        bv, e = take("bv", [NT, 512], F32, e)
        o_even, e = take("o_even", [NT, D], F32, e)
        junk, e = take("junk", [P], F32, e)
        assert e <= 2 * NF * TS, e
        p_map, e2 = take("p_map", [3, 2, TS], F32, 0)
        pT_diff, e2 = take("pT_diff", [2, TS], F32, e2)
        assert e2 <= 3 * AH * TS
        qA, e = take("qA", [8, TS], F32, 0)
        kA, e = take("kA", [8, TS], F32, e)
        v_all, e = take("v_all", [NT, 512], F32, e)
        o_fox, e = take("o_fox", [NT, D], F32, e)
        p_fox, e = take("p_fox", [3, TS], F32, e)
        pT_fox, e = take("pT_fox", [2, TS], F32, e)
        qn, e = take("qn", [2, 8, HA], F32, e)
        sq, e = take("sq", [2, 512], F32, e)
        tri, e = take("tri", [P], F32, e)
        ones, e = take("ones", [P], F32, e)
        gate, e = take("gate", [5, NT, FH], F32, e)
        fox_ms, e = take("fox_ms", [2, 3, 8], F32, e)
        bf_row, e = take("bf_row", [FH], F32, e)
        assert e <= 2 * NF * TS, e
        top[0] = arena + 2 * NF * TS * 4
        assert top[0] <= nc.sbuf_top, (top[0], nc.sbuf_top)

        psum = [ctx.enter_context(nc.psum_tensor(f"bank{b}", [P, 512], F32)) for b in range(8)]

        def sem(name):
            return ctx.enter_context(nc.semaphore(name))

        w_loaded = [sem(f"w_loaded{i}") for i in range(RAW)]
        hi_ready, lo_ready, w_used = sem("hi_ready"), sem("lo_ready"), sem("w_used")
        consts_in, fox_in, x_in, out_done = sem("consts_in"), sem("fox_in"), sem("x_in"), sem("out_done")
        lam_in = sem("lam_in")
        bank_full = [sem(f"bank{b}_full") for b in range(8)]
        freed = {"act": [sem(f"bank{b}_read_act") for b in range(8)],
                 "dve": [sem(f"bank{b}_read_dve") for b in range(8)]}
        act_step, dve_step = sem("act_step"), sem("dve_step")
        T_hi, T_lo = sem("T_hi"), sem("T_lo")
        S = {}

        def named(*names):
            for n in names:
                S[n] = sem(n)

        named("norm_done", "o_ready", "var_ready", "root_ready", "silu_done", "h_hi", "h_lo", "h_mul",
              "arena_free", "sig_done", "q_done", "gate_done", "i_done", "bq_done", "bk_done", "bv_done",
              "ln_arg", "ln_done", "k_done", "e_arg", "e_done", "dec_done", "sc_used", "merge_done",
              "ms_done", "max_done", "exp_done", "mix_done", "turned", "pT_done", "pv_done",
              "lam_arg", "lam_exp", "o_dve",
              "f_arg", "f_exp", "f_ln", "logf_done", "c_done", "sq_done", "qvar", "qroot", "qn_done", "qn_used",
              "qA_done", "v_done", "g_done", "act_free", "fmax", "fexp", "fturn", "fpT", "fpv", "ffin")

        chunk_used = {}
        PAIR = {(t, t): t for t in range(NT)} | {(0, 1): 4, (1, 2): 5, (2, 3): 6, (0, 2): 7, (1, 3): 8, (0, 3): 9}

        uses, bank_count, last = {}, [0] * 8, [None] * 8
        read_count = {"act": [0] * 8, "dve": [0] * 8}

        rows = [w[n][l:l + 1, :] for l in range(DEPTH) for n in ("ln1_g", "ln1_b", "ln2_g", "ln2_b")]
        n_masks = 2 + len(LEVELS)
        masks_f32 = bkT[:, :, :].rearrange("p h n -> p (h n)")[:, 0:n_masks * P].rearrange("p (m n) -> p m n", n=P)
        consts = [(ident[:, :], w["c_ident"]), (masks_f32, w["c_masks"]),
                  (gains[:, 0:1], w["hgrn_norm_g"].rearrange("o d -> d o")),
                  (gains[:, 1:2], w["diff_norm_g"].rearrange("o d -> d o")),
                  (gains[0:HD, 4:5], w["fox_qnorm_g"].rearrange("o d -> d o")),
                  (gains[0:HD, 5:6], w["fox_knorm_g"].rearrange("o d -> d o")),
                  (gains[HD:P, 4:6], w["c_ones"][0:P - HD, 0:2]),
                  ]
        consts += [(gains[:, 8 + h:9 + h], w["hgrn_lb_logits"][:, h * P:(h + 1) * P].rearrange("o d -> d o"))
                   for h in range(AH)]
        consts += [(ln_rows[i:i + 1, :], row) for i, row in enumerate(rows)]
        lam_loads = [(bv[:, 0, i * HD:(i + 1) * HD], w[n][0:1, :].to_broadcast([P, HD]))
                     for i, n in enumerate(("diff_lq1", "diff_lk1", "diff_lq2", "diff_lk2"))]
        fox_loads = [(tri[:, :], w["c_tri"]), (ones[:, :], w["c_ones"]),
                     (bf_row[:, :], w["fox_b_f"][0:1, :].to_broadcast([P, FH]))]
        N_CONSTS, N_FOX = len(consts), len(fox_loads)

        block = ctx.enter_context(nc.Block())

        def chunk_at(stage, i=0):
            return stage_chunks[stage][i]

        def hi(c, a, n):
            return w_hi[c % RING][:, a:a + n]

        def lo(c, a, n):
            return w_lo[c % RING][:, a:a + n]

        units = [("prep", h, 0) for h in range(AH)]
        for h in range(AH):
            units += [("diag", h, 0)] + [("level", h, n) for n in range(len(LEVELS))]
            units += [("qdec", h, 0), ("kdec", h, 0), ("kdec2", h, 0)]
            if h:
                units.insert(len(units) - 7, ("value", h - 1, 0))
        units += [("none", 0, 0)] * 3 + [("value", AH - 1, 0)] + [("none", 0, 0)] * 3
        mixed = [c for s in ("a_i", "b_q", "b_k", "b_v") for c in stage_chunks[s]]
        even_seq = []
        n = 0
        for c in mixed:
            for p in range(PIECES):
                even_seq.append(("piece", c, p))
                if n < len(units):
                    even_seq.append(("unit", n, 0))
                    n += 1
                if p == 3 or p == 1:
                    even_seq.append(("unit", n, 0))
                    n += 1
        while n < len(units):
            even_seq.append(("unit", n, 0))
            n += 1

        def nth(kinds, u):
            return sum(1 for k, _, _ in units[:u] if k in kinds)

        MM = ("diag", "level", "kdec", "kdec2")
        ARG = ("level", "kdec")
        EXP = ("level", "qdec", "kdec")
        DEC = ("level", "qdec", "kdec", "kdec2")

        def groups_of(c):
            stage = chunks[c][0]
            i = stage_chunks[stage].index(c)
            if stage in ("a_f", "a_q", "b_q", "b_k"):
                return [(stage, 2 * i), (stage, 2 * i + 1)]
            if stage == "fox_f" or i % 2 == 1:
                return [(stage, t) for t in range(NT)]
            return []

        def dec_buf(n):
            return o_even[:, 2 + n % 2, 512:D]

        def exp_buf(n):
            return o_even[:, n % 2, 512:D]

        def silu_buf(j):
            return silu_g[:, j, :]

        def h_buf(j):
            return psum[4 + j % 2][:, :]

        @block.tensor
        def _(pe):
            mm = nc.tensor.matmul

            def open_bank(key, bank, reader):
                if last[bank]:
                    who, count = last[bank]
                    pe.wait_ge(freed[who][bank], count)
                read_count[reader][bank] += 1
                bank_count[bank] += 1
                last[bank] = (reader, read_count[reader][bank])
                uses[key] = (bank, bank_count[bank], reader)
                return psum[bank]

            def close_bank(key, ins):
                ins.then_inc(bank_full[uses[key][0]], 1)

            def used_with_bank(c, key):
                chunk_used[c] = (bank_full[uses[key][0]], uses[key][1])

            alone = [0]

            def used_alone(c, ins):
                ins.then_inc(w_used, 1)
                alone[0] += 1
                chunk_used[c] = (w_used, alone[0])

            gid = [0]

            def next_gemm_bank():
                gid[0] += 1
                return (gid[0] - 1) % 4

            def products(acc, l_hi, l_lo, r_hi, r_lo, first, final):
                mm(acc, l_hi, r_lo, start=first, stop=False)
                mm(acc, l_lo, r_hi, start=False, stop=False)
                return mm(acc, l_hi, r_hi, start=False, stop=final)

            def weights_in(c):
                pe.wait_ge(hi_ready, c + 1)
                pe.wait_ge(lo_ready, c + 1)

            def feature_chunk(c, reader):
                stage, _, _ = chunks[c]
                weights_in(c)
                for j, key in enumerate(groups_of(c)):
                    acc = open_bank(key, next_gemm_bank(), reader)
                    for k in range(KD):
                        a = k * 256 + j * P
                        ins = products(acc[:, :], hi(c, a, P), lo(c, a, P), xT_hi[:, k, :], xT_lo[:, k, :],
                                       k == 0, k == KD - 1)
                        if k == KD // 2 - 1:
                            yield
                    close_bank(key, ins)
                    if j == 1:
                        used_with_bank(c, key)
                    yield

            def token_chunk(c, reader, src_hi, src_lo, k_base, first, final, width=512):
                stage, _, size = chunks[c]
                nk = size // width
                weights_in(c)
                for t in range(NT):
                    key = (stage, t) if not isinstance(final, tuple) else (*final, t)
                    if first:
                        open_bank((stage, "acc", t, c), next_gemm_bank(), reader)
                        acc_bank[t] = uses[(stage, "acc", t, c)]
                    acc = psum[acc_bank[t][0]][:, 0:width]
                    for k in range(nk):
                        tok = slice(t * P, (t + 1) * P)
                        ins = products(acc, src_hi[:, k_base + k, tok], src_lo[:, k_base + k, tok],
                                       hi(c, k * width, width), lo(c, k * width, width),
                                       first and k == 0, bool(final) and k == nk - 1)
                    if final:
                        uses[key] = acc_bank[t]
                        close_bank(key, ins)
                    if t == NT - 1:
                        if final:
                            used_with_bank(c, key)
                        else:
                            used_alone(c, ins)
                    yield

            acc_bank = [None] * NT

            def columns(stage, reader, src_hi=xT_hi, src_lo=xT_lo):
                a, b = stage_chunks[stage]
                yield from token_chunk(a, reader, src_hi, src_lo, 0, True, False)
                yield from token_chunk(b, reader, src_hi, src_lo, 4, False, True)

            def drain(pieces):
                for _ in pieces:
                    pass

            turns = [0]

            def turn_tile(tag, t, src, ready):
                for r in range(2):
                    if r == 0:
                        ready()
                    key = (tag, t, r)
                    acc = open_bank(key, t, "dve")
                    for j in range(4):
                        f = (4 * r + j) * P
                        ins = nc.tensor.transpose(acc[:, j * P:(j + 1) * P], src[:, t, f:f + P], ident[:, :])
                    close_bank(key, ins)

            def wait_tiles(n):
                pe.wait_ge(T_hi, 2 * n)
                pe.wait_ge(T_lo, 2 * n)

            pe.wait_ge(consts_in, 16 * N_CONSTS)

            for t in range(NT):
                turn_tile("x", t, x_res, lambda: pe.wait_ge(x_in, 16))
            turned_tiles = [NT]

            def norm_tail(tag, step, src_tiles):
                for t in range(NT + 2):
                    if t < NT:
                        src_tiles(t)
                    if t >= 2:
                        n = step * NT + t - 1
                        turn_tile(tag, t - 2, x_res, lambda: pe.wait_ge(S["norm_done"], n))
                turned_tiles[0] += NT

            def mixer_out(l):
                o = o_even if l == 0 else o_fox
                pe.wait_ge(S["o_ready"], l + 1)
                for t in range(NT):
                    turn_tile(f"o{l}", t, o, lambda: None)
                turned_tiles[0] += NT
                wait_tiles(turned_tiles[0])
                a, b, c2, d2 = stage_chunks[f"out{l}"]
                drain(token_chunk(a, "dve", xT_hi, xT_lo, 0, True, False))
                drain(token_chunk(b, "dve", xT_hi, xT_lo, 4, False, (f"out{l}", 0)))
                tail_products((f"out{l}", 1), [(c2, 0), (d2, 4)], xT_hi, xT_lo, f"n1_{l}", 2 * l)

            def tail_products(name, parts, src_hi, src_lo, tag, step, acc_open=False):
                def tile(t):
                    key = (*name, t)
                    if not acc_open:
                        open_bank((*name, "acc", t), next_gemm_bank(), "dve")
                        acc_bank[t] = uses[(*name, "acc", t)]
                    acc = psum[acc_bank[t][0]][:, :]
                    tok = slice(t * P, (t + 1) * P)
                    for n, (c, k0) in enumerate(parts):
                        if t == 0:
                            weights_in(c)
                        nk = chunks[c][2] // 512
                        for k in range(nk):
                            ins = products(acc, src_hi[:, k0 + k, tok], src_lo[:, k0 + k, tok],
                                           hi(c, k * 512, 512), lo(c, k * 512, 512),
                                           not acc_open and n == 0 and k == 0,
                                           n == len(parts) - 1 and k == nk - 1)
                        if t == NT - 1:
                            if n < len(parts) - 1:
                                used_alone(c, ins)
                            else:
                                uses[key] = acc_bank[t]
                                close_bank(key, ins)
                                used_with_bank(c, key)
                        elif n == len(parts) - 1:
                            uses[key] = acc_bank[t]
                            close_bank(key, ins)

                norm_tail(tag, step, tile)

            def swiglu(l):
                wait_tiles(turned_tiles[0])
                for j, c in enumerate(stage_chunks[f"up{l}"]):
                    weights_in(c)
                    for part in range(2):
                        key = (f"up{l}", j, part)
                        acc = open_bank(key, next_gemm_bank(), "act" if part == 0 else "dve")
                        for k in range(KD):
                            a = part * KD * P + k * P
                            ins = products(acc[:, :], hi(c, a, P), lo(c, a, P), xT_hi[:, k, :],
                                           xT_lo[:, k, :], k == 0, k == KD - 1)
                        close_bank(key, ins)
                    used_with_bank(c, key)
                cs = stage_chunks[f"down{l}"]
                pe.wait_ge(S["h_lo"], (l + 1) * NF)
                spread_rows(2 * l + 1)
                k0 = 0
                for i in range(6):
                    drain(token_chunk(cs[i], "dve", hT_hi, hT_lo, k0, i == 0, (f"down{l}", 0) if i == 5 else False))
                    k0 += chunks[cs[i]][2] // 512
                k0 = 0
                for i in range(6, 9):
                    drain(token_chunk(cs[i], "dve", hT_hi, hT_lo, k0, i == 6, False))
                    k0 += chunks[cs[i]][2] // 512
                parts = []
                for i in range(9, 12):
                    parts.append((cs[i], k0))
                    k0 += chunks[cs[i]][2] // 512
                tail_products((f"down{l}", 1), parts, hT_hi, hT_lo, f"n2_{l}", 2 * l + 1, acc_open=True)

            def spread_rows(n):
                for i in range(4):
                    key = ("rows", n, i)
                    acc = open_bank(key, 4 + i, "dve")
                    row = 2 * n + i // 2
                    sel = ident[0:8, row:row + 1].to_broadcast([8, P])
                    close_bank(key, mm(acc[:, :], sel, ln_rows[0:8, (i % 2) * 512:(i % 2) * 512 + 512],
                                       start=True, stop=True))

            wait_tiles(NT)
            for c in stage_chunks["a_f"] + stage_chunks["a_q"]:
                drain(feature_chunk(c, "act"))
            drain(columns("a_g", "act"))

            def unit_products(u):
                kind, h, n = units[u]
                if kind in MM:
                    m = nth(MM, u)
                    acc = open_bank(("unit", u), 4 + m % 2, "dve")
                if kind == "diag":
                    pe.wait_ge(S["k_done"], h + 1)
                    for t in range(NT):
                        ins = mm(acc[:, t * P:(t + 1) * P], kT[:, h, t * P:(t + 1) * P],
                                 qT[:, h, t * P:(t + 1) * P], start=True, stop=True)
                if kind == "level":
                    pe.wait_ge(S["dec_done"], nth(DEC, u) + 1)
                    d = dec_buf(nth(("level",), u))
                    for t in range(NT):
                        ins = mm(acc[:, t * P:(t + 1) * P], d[:, t * P:(t + 1) * P], d[:, t * P:(t + 1) * P],
                                 start=True, stop=True)
                if kind == "kdec":
                    pe.wait_ge(S["dec_done"], nth(DEC, u) + 1)
                    for i in range(3):
                        ins = mm(acc[:, i * P:(i + 1) * P], k_dec[:, i * P:(i + 1) * P],
                                 q_dec[:, (i + 1) * P:(i + 2) * P], start=True, stop=True)
                if kind == "kdec2":
                    pe.wait_ge(S["dec_done"], nth(DEC, u) + 1)
                    for i, t in enumerate((2, 3, 3)):
                        ins = mm(acc[:, i * P:(i + 1) * P], k_dec2[:, i, :], q_dec[:, t * P:(t + 1) * P],
                                 start=True, stop=True)
                if kind in MM:
                    close_bank(("unit", u), ins)
                if kind == "value":
                    acc = open_bank(("value", h), 6 + h % 2, "dve")
                    pe.wait_ge(S["merge_done"], 10 * (h + 1))
                    pe.wait_ge(S["i_done"], NT)
                    for t in range(NT):
                        for s in range(t + 1):
                            ins = mm(acc[:, t * P:(t + 1) * P], scT[:, h % 2, PAIR[(s, t)], :],
                                     iv[:, s, h * P:(h + 1) * P], start=s == 0, stop=s == t)
                    close_bank(("value", h), ins)

            pieces = {}
            for kind, a, b in even_seq:
                if kind == "unit":
                    unit_products(a)
                    continue
                stage = chunks[a][0]
                if stage not in pieces:
                    if stage in ("a_i", "b_v"):
                        pieces[stage] = columns(stage, "act")
                    else:
                        x0, x1 = stage_chunks[stage]
                        pieces[stage] = (y for c in (x0, x1) for y in feature_chunk(c, "act"))
                next(pieces[stage], None)
            for stage in ("a_i", "b_q", "b_k", "b_v"):
                drain(pieces[stage])

            pe.wait_ge(S["bq_done"], 4)
            pe.wait_ge(S["bk_done"], 4)
            pe.wait_ge(S["bv_done"], 4)
            N = AH * NT
            for s in range(N + 3):
                if s < N:
                    h, i = s // NT, s % NT
                    for m in range(2):
                        key = ("score", s, m)
                        acc = open_bank(key, 2 * (s % 2) + m, "act")
                        n = (i + 1) * P
                        rows = slice(m * HD, (m + 1) * HD)
                        mm(acc[:, 0:n], bqT[rows, h, i * P:(i + 1) * P], bkT[rows, h, 0:n], start=True, stop=False)
                        close_bank(key, mm(acc[:, n - P:n], ident_bf[:, :], diff_mask[:, :], start=False, stop=True))
                if 2 <= s < N + 2:
                    u = s - 2
                    i = u % NT
                    pe.wait_ge(S["mix_done"], u + 1)
                    acc = open_bank(("pT", u), 4 + u % 2, "act")
                    for j in range(i + 1):
                        ins = nc.tensor.transpose(acc[:, j * P:(j + 1) * P], p_map[:, u % 3, 0, j * P:(j + 1) * P],
                                                  ident[:, :])
                    close_bank(("pT", u), ins)
                if s >= 3:
                    u = s - 3
                    h, i = u // NT, u % NT
                    pe.wait_ge(S["pT_done"], u + 1)
                    acc = open_bank(("diff", u), 6 + u % 2, "dve")
                    for j in range(i + 1):
                        ins = mm(acc[:, 0:P], pT_diff[:, u % 2, j * P:(j + 1) * P], bv[:, j, h * P:(h + 1) * P],
                                 start=j == 0, stop=j == i)
                    close_bank(("diff", u), ins)

            spread_rows(0)
            mixer_out(0)
            swiglu(0)

            wait_tiles(turned_tiles[0])
            drain(token_chunk(stage_chunks["fox_f"][0], "dve", xT_hi, xT_lo, 0, True, True, FH))
            pe.wait_ge(fox_in, 16 * N_FOX)

            def turn_heads(part, half, t):
                n = (2 * half + part) * NT + t
                pe.wait_ge(S["qn_done"], n + 1)
                for r in range(2):
                    key = ("heads", part, half, t, r)
                    acc = open_bank(key, 4 + r, "act")
                    for j in range(4):
                        ins = nc.tensor.transpose(acc[0:HA, j * P:(j + 1) * P], qn[:, n % 2, 4 * r + j, :],
                                                  ident[:, :])
                    close_bank(key, ins)

            def gates():
                acc = open_bank("cum", 6, "dve")
                pe.wait_ge(S["logf_done"], 1)
                for t in range(NT):
                    for s in range(t + 1):
                        ins = mm(acc[:, t * FH:(t + 1) * FH], (tri if s == t else ones)[:, :], gate[:, 2, s, :],
                                 start=s == 0, stop=s == t)
                close_bank("cum", ins)

            for half in range(2):
                drain(columns(f"foxq{half}", "dve"))
                if half == 0:
                    gates()
                gen = columns(f"foxk{half}", "dve")
                for i, _ in enumerate(gen):
                    if 1 <= i <= NT:
                        turn_heads(0, half, i - 1)
                gen = columns(f"foxv{half}", "act")
                for i, _ in enumerate(gen):
                    if 1 <= i <= NT:
                        turn_heads(1, half, i - 1)
                drain(columns(f"foxg{half}", "act"))
                pe.wait_ge(S["qA_done"], 2 * NT * (half + 1))
                pe.wait_ge(S["v_done"], NT * (half + 1))
                N = 8 * NT
                for s in range(N + 3):
                    base = half * N
                    if s < N:
                        h, i = s // NT, s % NT
                        n = (i + 1) * P
                        key = ("fs", half, s)
                        acc = open_bank(key, s % 3, "act")
                        mm(acc[:, 0:n], qA[0:HA, h, i * P:(i + 1) * P], kA[0:HA, h, 0:n], start=True, stop=False)
                        close_bank(key, mm(acc[:, n - P:n], ident_bf[:, :], fox_mask[:, :], start=False, stop=True))
                    if 2 <= s < N + 2:
                        u = s - 2
                        i = u % NT
                        pe.wait_ge(S["fexp"], base + u + 1)
                        acc = open_bank(("fT", half, u), 3 + u % 2, "act")
                        for j in range(i + 1):
                            ins = nc.tensor.transpose(acc[:, j * P:(j + 1) * P],
                                                      p_fox[:, u % 3, j * P:(j + 1) * P], ident[:, :])
                        close_bank(("fT", half, u), ins)
                    if s >= 3:
                        u = s - 3
                        h, i = u // NT, u % NT
                        pe.wait_ge(S["fpT"], base + u + 1)
                        acc = open_bank(("fv", half, u), 5 + u % 3, "dve")
                        for j in range(i + 1):
                            ins = mm(acc[:, 0:HD], pT_fox[:, u % 2, j * P:(j + 1) * P],
                                     v_all[:, j, h * HD:(h + 1) * HD], start=j == 0, stop=j == i)
                        close_bank(("fv", half, u), ins)
            spread_rows(2)
            mixer_out(1)
            swiglu(1)

        @block.sync
        def _(sp):
            sp.dma_start(x_res[:, :, :], w["x"][0].rearrange("(t p) d -> p t d", p=P)).then_inc(x_in, 16)

            def load(c):
                if c >= RAW:
                    sp.wait_ge(lo_ready, c - RAW + 1)
                for off, src, a, b in chunks[c][1]:
                    dst = w_raw[c % RAW][:, off:off + a * b].rearrange("p (a b) -> p a b", a=a)
                    sp.dma_start(dst, src).then_inc(w_loaded[c % RAW], 16)

            load(0)
            for dst, src in consts:
                sp.dma_start(dst, src).then_inc(consts_in, 16)
            for dst, src in lam_loads:
                sp.dma_start(dst, src).then_inc(lam_in, 16)
            for c in range(1, len(chunks)):
                if chunks[c][0] == "fox_f":
                    sp.wait_ge(S["norm_done"], 2 * NT)
                    for dst, src in fox_loads:
                        sp.dma_start(dst, src).then_inc(fox_in, 16)
                load(c)
            o = out[0].rearrange("(t p) d -> p t d", p=P)
            for t in range(NT):
                sp.wait_ge(S["norm_done"], 3 * NT + t + 1)
                sp.dma_start(o[:, t, :], x_res[:, t, :]).then_inc(out_done, 16)
            sp.wait_ge(out_done, 16 * NT)

        @block.gpsimd
        def _(pool):
            for c, (_, _, size) in enumerate(chunks):
                pool.wait_ge(hi_ready, c + 1)
                if c >= RING:
                    pool.wait_ge(*chunk_used[c - RING])
                for a in range(0, size, 1024):
                    n = min(1024, size - a)
                    ins = nc.gpsimd.tensor_tensor(w_lo[c % RING][:, a:a + n], w_raw[c % RAW][:, a:a + n],
                                                  w_hi[c % RING][:, a:a + n].bitcast(F32), ALU.subtract)
                ins.then_inc(lo_ready, 1)

        def reader_of(eng, counts):
            def full(key):
                bank, n, _ = uses[key]
                eng.wait_ge(bank_full[bank], n)
                return psum[bank]

            def chain(ins, s):
                ins.then_inc(s, 1)
                counts[id(s)] = counts.get(id(s), 0) + 1
                eng.wait_ge(s, counts[id(s)])

            return full, chain

        @block.scalar
        def _(act):
            counts = {}
            full, chain = reader_of(act, counts)
            step = lambda ins: chain(ins, act_step)
            release = lambda ins, key: chain(ins, freed["act"][uses[key][0]])
            fn = nc.scalar.activation
            rounded = [0]
            loaded = {0: 0, 1: 0}
            need = []
            for c, (_, loads, _) in enumerate(chunks):
                loaded[c % RAW] += 16 * len(loads)
                need.append(loaded[c % RAW])

            def hi_upto(n):
                while rounded[0] < min(n, len(chunks)):
                    c = rounded[0]
                    act.wait_ge(w_loaded[c % RAW], need[c])
                    if c >= RING:
                        act.wait_ge(*chunk_used[c - RING])
                    size = chunks[c][2]
                    chain(fn(w_hi[c % RING][:, 0:size], w_raw[c % RAW][:, 0:size], ACT.Copy), hi_ready)
                    rounded[0] += 1

            def split_hi(tag, t):
                for r in range(2):
                    acc = full((tag, t, r))
                    dst = xT_hi[:, 4 * r:4 * r + 4, t * P:(t + 1) * P]
                    src = acc[:, :].rearrange("p (k n) -> p k n", k=4)
                    if tag == "o0":
                        chain(fn(dst, src, ACT.Copy, scale=gains[:, r:r + 1]), T_hi)
                    else:
                        chain(fn(dst, src, ACT.Copy), T_hi)

            roots = [0]

            def root(dst, src, arg_sem, n, done):
                act.wait_ge(arg_sem, n)
                step(fn(dst, src, ACT.Ln))
                chain(fn(dst, dst, ACT.Exp, scale=-0.5), done)

            def evac(key, dst, src_fn, func=ACT.Copy):
                acc = full(key)
                release(fn(dst, src_fn(acc), func), key)

            whole = lambda acc: acc[:, :]

            hi_upto(2)
            for t in range(NT):
                split_hi("x", t)
                hi_upto(3)
            for stage, dst, func in (("a_f", kT, ACT.Sigmoid), ("a_q", qT, ACT.Silu)):
                for h in range(AH):
                    c = stage_chunks[stage][h // 2]
                    hi_upto(c + 3)
                    evac((stage, h), dst[:, h, :], whole, func)
                    if h == 3:
                        act.sem_inc(S["sig_done"], 1)
            hi_upto(stage_chunks["a_g"][1] + 2)
            for t in range(NT):
                evac(("a_g", t), o_even[:, t, 0:512], whole, ACT.Silu)
            act.sem_inc(S["gate_done"], 1)
            act.wait_ge(S["lam_arg"], 1)
            chain(fn(small[:, 0:2], small[:, 0:2], ACT.Exp), S["lam_exp"])
            chain(fn(small[:, 16:20], small[:, 16:20], ACT.Exp), S["lam_exp"])

            def unit_act(u):
                if u >= 3 and units[u - 3][0] == "value":
                    h = units[u - 3][1]
                    root(stats[:, :, 8 + h], stats[:, :, 4 + h], S["var_ready"], h + 1, S["root_ready"])
                kind, h, n = units[u]
                if kind == "prep":
                    act.wait_ge(S["ln_arg"], h + 1)
                    step(fn(q_dec[:, :], q_dec[:, :], ACT.Ln))
                    chain(fn(k_dec[:, :], k_dec[:, :], ACT.Ln), S["ln_done"])
                if kind in EXP:
                    buf = exp_buf(nth(EXP, u))
                    if kind == "qdec":
                        act.wait_ge(S["k_done"], h + 1)
                        e = nth(DEC, u)
                        act.wait_ge(S["dec_done"], e - 1)
                        chain(fn(buf, bT[:, h, :], ACT.Exp), S["e_done"])
                    else:
                        act.wait_ge(S["e_arg"], nth(ARG, u) + 1)
                        chain(fn(buf, buf, ACT.Exp), S["e_done"])
                if kind == "value":
                    acc = full(("value", h))
                    for t in range(NT):
                        ins = fn(junk[:, :], acc[:, t * P:(t + 1) * P], ACT.Square, accum_out=stats[:, t, h:h + 1])
                        if t < NT - 1:
                            step(ins)
                        else:
                            chain(ins, S["ms_done"])

            due = []
            finished = {}
            for kind, a, b in even_seq:
                if kind == "unit":
                    unit_act(a)
                    continue
                for key in due:
                    dst = {"a_i": iv, "b_v": bv, "b_q": bqT, "b_k": bkT}[key[0]]
                    if key[0] == "b_v" and key[1] == 0:
                        act.wait_ge(S["lam_arg"], 1)
                    evac(key, dst[:, key[1], :], whole)
                    act.sem_inc(S[{"a_i": "i_done", "b_v": "bv_done", "b_q": "bq_done", "b_k": "bk_done"}[key[0]]], 1)
                due = []
                hi_upto(a + 2 if b < 2 else a + 3) if b == 1 or b == 3 else None
                g = groups_of(a)
                if len(g) == 2:
                    due = [g[0]] if b == 1 else [g[1]] if b == 3 else []
                elif g:
                    due = [g[b]]
            for key in due:
                evac(key, bv[:, key[1], :], whole)
                act.sem_inc(S["bv_done"], 1)

            N = AH * NT
            for s in range(N + 4):
                if s < N:
                    i = s % NT
                    n = (i + 1) * P
                    if s == 0:
                        act.wait_ge(S["act_free"], 1)
                    if s >= 2:
                        act.wait_ge(S["mix_done"], s - 1)
                    if s >= 3:
                        bank, cnt, _ = uses[("pT", s - 3)]
                        act.wait_ge(bank_full[bank], cnt)
                    for m in range(2):
                        act.wait_ge(S["max_done"], 2 * s + m + 1)
                        key = ("score", s, m)
                        acc = full(key)
                        ins = fn(p_map[:, s % 3, m, 0:n], acc[:, 0:n], ACT.Exp, bias=small[:, 24 + 4 * (s % 2) + m:25 + 4 * (s % 2) + m],
                                 scale=HD ** -0.5, accum_out=small[:, 26 + 4 * (s % 2) + m:27 + 4 * (s % 2) + m])
                        release(ins, key)
                    act.sem_inc(S["exp_done"], 1)
                if 2 <= s < N + 2:
                    u = s - 2
                    n = (u % NT + 1) * P
                    acc = full(("pT", u))
                    if u >= 2:
                        bank, cnt, _ = uses[("diff", u - 2)]
                        act.wait_ge(bank_full[bank], cnt)
                    release(fn(pT_diff[:, u % 2, 0:n], acc[:, 0:n], ACT.Copy), ("pT", u))
                    act.sem_inc(S["pT_done"], 1)
                if 4 <= s:
                    u = s - 4
                    acc = full(("diff", u))
                    chain(fn(junk[:, :], acc[:, 0:P], ACT.Square, accum_out=stats[:, u % NT, u // NT:u // NT + 1]),
                          S["ms_done"])
                    if u % NT == NT - 1:
                        h = u // NT
                        root(stats[:, :, 8 + h], stats[:, :, 4 + h], S["var_ready"], AH + h + 1, S["root_ready"])
                if s in (1, 3):
                    hi_upto(chunk_at("out0") + 1 + s // 2)

            def mixer_tail(l):
                for t in range(NT):
                    split_hi(f"o{l}", t)
                hi_upto(stage_chunks[f"out{l}"][0] + 3)
                hi_upto(stage_chunks[f"out{l}"][2] + 2)
                hi_upto(stage_chunks[f"up{l}"][0] + 1)
                norm_act(f"n1_{l}", 2 * l, stage_chunks[f"up{l}"][0])

            def norm_act(tag, step_n, after):
                for t in range(NT):
                    root(stats[:, t, 14:15], stats[:, t, 13:14], S["ln_arg"], AH + step_n * NT + t + 1, S["ln_done"])
                    if t >= 1:
                        if t == NT - 1:
                            hi_upto(after + 1)
                        split_hi(tag, t - 1)
                hi_upto(after + 2)
                split_hi(tag, NT - 1)
                hi_upto(after + 3)

            def swiglu_act(l):
                for j, c in enumerate(stage_chunks[f"up{l}"]):
                    hi_upto(c + 2)
                    acc = full((f"up{l}", j, 0))
                    release(fn(silu_buf(j), acc[:, :], ACT.Silu), (f"up{l}", j, 0))
                    act.sem_inc(S["silu_done"], 1)
                    hi_upto(c + 3)
                    if j >= 1:
                        act.wait_ge(S["h_mul"], l * NF + j)
                        chain(fn(hT_hi[:, j - 1, :], h_buf(j - 1), ACT.Copy), S["h_hi"])
                act.wait_ge(S["h_mul"], l * NF + NF)
                chain(fn(hT_hi[:, NF - 1, :], h_buf(NF - 1), ACT.Copy), S["h_hi"])
                cs = stage_chunks[f"down{l}"]
                hi_upto(cs[-1] + 1)
                norm_act(f"n2_{l}", 2 * l + 1, cs[-1] + 1)

            mixer_tail(0)
            swiglu_act(0)

            act.wait_ge(S["f_arg"], 1)
            chain(fn(gate[:, 1, :, :], gate[:, 1, :, :], ACT.Exp), S["f_exp"])
            act.wait_ge(S["f_arg"], 2)
            chain(fn(gate[:, 1, :, :], gate[:, 1, :, :], ACT.Ln), S["f_ln"])

            def heads_act(part, half, t):
                n = (2 * half + part) * NT + t
                for r in range(2):
                    acc = full(("heads", part, half, t, r))
                    dst = (qA if part == 0 else kA)[0:HA, 4 * r:4 * r + 4, t * P:(t + 1) * P]
                    src = acc[0:HA, :].rearrange("p (k n) -> p k n", k=4)
                    release(fn(dst, src, ACT.Copy, scale=gains[0:HA, 4 + part:5 + part]), ("heads", part, half, t, r))
                act.sem_inc(S["qA_done"], 1)

            def square(part, half, t):
                n = (2 * half + part) * NT + t
                acc = full((f"fox{'qk'[part]}{half}", t))
                if n >= 2:
                    act.wait_ge(S["qvar"], n - 1)
                chain(fn(sq[:, n % 2, :], acc[:, :], ACT.Square), S["sq_done"])
                root(fox_ms[:, n % 2, 1, :], fox_ms[:, n % 2, 0, :], S["qvar"], n + 1, S["qroot"])

            for half in range(2):
                st = stage_chunks[f"foxq{half}"][0]
                hi_upto(st + 3)
                for t in range(NT):
                    square(0, half, t)
                    if t == 1:
                        hi_upto(st + 4)
                hi_upto(st + 5)
                for t in range(NT):
                    heads_act(0, half, t)
                hi_upto(st + 6)
                for t in range(NT):
                    square(1, half, t)
                hi_upto(st + 7)
                for t in range(NT):
                    heads_act(1, half, t)
                hi_upto(st + 8)
                for t in range(NT):
                    evac((f"foxv{half}", t), v_all[:, t, :], whole)
                    act.sem_inc(S["v_done"], 1)
                hi_upto(st + 9)
                for t in range(NT):
                    evac((f"foxg{half}", t), o_fox[:, t, half * 512:(half + 1) * 512], whole, ACT.Sigmoid)
                    act.sem_inc(S["g_done"], 1)
                hi_upto(st + 11)
                N = 8 * NT
                base = half * N
                for s in range(N + 2):
                    if s < N:
                        n = (s % NT + 1) * P
                        act.wait_ge(S["fmax"], base + s + 1)
                        if s >= 3:
                            bank, cnt, _ = uses[("fT", half, s - 3)]
                            act.wait_ge(bank_full[bank], cnt)
                        if s >= 4:
                            act.wait_ge(S["ffin"], base + s - 3)
                        key = ("fs", half, s)
                        ins = fn(p_fox[:, s % 3, 0:n], full(key)[:, 0:n], ACT.Exp, bias=small[:, 32 + s % 4:33 + s % 4],
                                 accum_out=small[:, 36 + s % 4:37 + s % 4])
                        release(ins, key)
                        act.sem_inc(S["fexp"], 1)
                    if s >= 2:
                        u = s - 2
                        n = (u % NT + 1) * P
                        key = ("fT", half, u)
                        acc = full(key)
                        if u >= 2:
                            bank, cnt, _ = uses[("fv", half, u - 2)]
                            act.wait_ge(bank_full[bank], cnt)
                        release(fn(pT_fox[:, u % 2, 0:n], acc[:, 0:n], ACT.Copy), key)
                        act.sem_inc(S["fpT"], 1)
            mixer_tail(1)
            swiglu_act(1)

        @block.vector
        def _(dve):
            counts = {}
            full, chain = reader_of(dve, counts)
            step = lambda ins: chain(ins, dve_step)
            release = lambda ins, key: chain(ins, freed["dve"][uses[key][0]])
            v = nc.vector
            tt, ts, stt = v.tensor_tensor, v.tensor_scalar, v.scalar_tensor_tensor
            split = [0]

            def split_lo(tag, t):
                for r in range(2):
                    split[0] += 1
                    acc = full((tag, t, r))
                    dve.wait_ge(T_hi, split[0])
                    tok = slice(t * P, (t + 1) * P)
                    dst = xT_lo[:, 4 * r:4 * r + 4, tok]
                    high = xT_hi[:, 4 * r:4 * r + 4, tok].bitcast(F32)
                    src = acc[:, :].rearrange("p (k n) -> p k n", k=4)
                    if tag == "o0":
                        ins = stt(dst, src, gains[:, r:r + 1], high, ALU.mult, ALU.subtract)
                    else:
                        ins = tt(dst, src, high, ALU.subtract)
                    release(ins, (tag, t, r))
                    dve.sem_inc(T_lo, 1)

            def refine(r, var, tmp):
                step(tt(tmp, r, r, ALU.mult))
                step(tt(tmp, tmp, var, ALU.mult))
                step(ts(tmp, tmp, -0.5, 1.5, ALU.mult, ALU.add))
                step(tt(r, r, tmp, ALU.mult))

            dve.wait_ge(consts_in, 16 * N_CONSTS)
            dve.wait_ge(lam_in, 16 * len(lam_loads))
            step(v.tensor_copy(ident_bf[:, :], ident[:, :]))
            step(v.tensor_copy(fox_mask[:, :], masks_f32[:, 0, :]))
            step(v.tensor_copy(diff_mask[:, :], masks_f32[:, 1, :]))
            step(v.tensor_copy(level_mask[:, :, :], masks_f32[:, 2:n_masks, :]))
            lam_rows = bv[:, 0, 0:4 * HD].rearrange("p (a b) -> p a b", a=4)
            for m in range(2):
                step(tt(bv[:, 1, m * HD:(m + 1) * HD], lam_rows[:, 2 * m, :], lam_rows[:, 2 * m + 1, :], ALU.mult))
                step(v.tensor_reduce(small[:, m:m + 1], bv[:, 1, m * HD:(m + 1) * HD], AX_X, ALU.add))
            lg = gains[:, 8:12]
            step(tt(small[:, 16:20], lg, lg, ALU.subtract))
            dve.sem_inc(S["lam_arg"], 1)
            step(ts(gains[:, 1:2], gains[:, 1:2], 1.0 - LAM_INIT, None, ALU.mult))
            step(ts(gains[0:HD, 4:5], gains[0:HD, 4:5], HD ** -0.5, None, ALU.mult))
            for t in range(NT):
                split_lo("x", t)

            dve.wait_ge(S["lam_exp"], 2)
            step(tt(small[:, 2:3], small[:, 1:2], small[:, 0:1], ALU.subtract))
            step(ts(small[:, 2:3], small[:, 2:3], -LAM_INIT, None, ALU.add))
            step(v.reciprocal(small[:, 20:24], small[:, 16:20]))
            step(tt(small[:, 16:20], small[:, 16:20], small[:, 20:24], ALU.mult))
            step(tt(small[:, 8:12], small[:, 16:20], small[:, 16:20], ALU.subtract))
            step(ts(small[:, 12:16], small[:, 8:12], -1.0, 1.0, ALU.mult, ALU.add))
            dve.wait_ge(S["sig_done"], 2)
            dve.wait_ge(S["gate_done"], 1)

            def halves(ap, b):
                return ap.rearrange("p (n two b) -> p n two b", two=2, b=b)

            def before(u):
                kind, h, n = units[u]
                if kind == "prep":
                    k = kT[:, h, :]
                    if h:
                        dve.wait_ge(S["ln_done"], h)
                    step(ts(k, k, small[:, 12 + h:13 + h], small[:, 8 + h:9 + h], ALU.mult, ALU.add))
                    step(ts(q_dec[:, :], k, TINY, None, ALU.max))
                    step(ts(k_dec[:, :], k, 1.0 / TINY, 1.0, ALU.mult, ALU.min))
                    chain(ts(k, k, -1.0, 1.0, ALU.mult, ALU.add), S["ln_arg"])
                    dve.wait_ge(S["ln_done"], h + 1)
                    for t in range(NT):
                        tok = slice(t * P, (t + 1) * P)
                        ins = v.tensor_tensor_scan(bT[:, h, tok], q_dec[:, tok], k_dec[:, tok], 0.0, ALU.add, ALU.add)
                        if t < NT - 1:
                            step(ins)
                    chain(ins, S["k_done"])
                if kind in ARG:
                    x = nth(EXP, u)
                    buf = exp_buf(x)
                    b = bT[:, h, :]
                    if kind == "level":
                        z = LEVELS[n]
                        bb, ee = halves(b, z), halves(buf, z)
                        mid = bb[:, :, 0, z - 1:z].to_broadcast([P, TS // (2 * z), z])
                        step(tt(ee[:, :, 1, :], bb[:, :, 1, :], mid, ALU.subtract))
                        chain(tt(ee[:, :, 0, :], mid, bb[:, :, 0, :], ALU.subtract), S["e_arg"])
                    else:
                        bb = b.rearrange("p (t n) -> p t n", t=NT)
                        ee = buf.rearrange("p (t n) -> p t n", t=NT)
                        end = bb[:, :, P - 1:P].to_broadcast([P, NT, P])
                        chain(tt(ee, end, bb, ALU.subtract), S["e_arg"])

            def after(u):
                kind, h, n = units[u]
                if kind in EXP:
                    dve.wait_ge(S["e_done"], nth(EXP, u) + 1)
                    buf = exp_buf(nth(EXP, u))
                if kind == "level":
                    m = nth(("level",), u)
                    if m >= 2:
                        prev = [x for x in range(u) if units[x][0] == "level"][-2]
                        bank, cnt, _ = uses[("unit", prev)]
                        dve.wait_ge(bank_full[bank], cnt)
                    z = LEVELS[n]
                    d, ee = halves(dec_buf(m), z), halves(buf, z)
                    qq, kk = halves(qT[:, h, :], z), halves(kT[:, h, :], z)
                    step(tt(d[:, :, 1, :], qq[:, :, 1, :], ee[:, :, 1, :], ALU.mult))
                    chain(tt(d[:, :, 0, :], kk[:, :, 0, :], ee[:, :, 0, :], ALU.mult), S["dec_done"])
                if kind in ("qdec", "kdec") and h:
                    prev = [x for x in range(u) if units[x][0] == "kdec2"][-1]
                    bank, cnt, _ = uses[("unit", prev)]
                    dve.wait_ge(bank_full[bank], cnt)
                if kind == "qdec":
                    step(v.tensor_copy(small[:, 3:7], buf.rearrange("p (t n) -> p t n", t=NT)[:, :, P - 1]))
                    chain(tt(q_dec[:, :], qT[:, h, :], buf, ALU.mult), S["dec_done"])
                if kind == "kdec":
                    chain(tt(k_dec[:, :], kT[:, h, :], buf, ALU.mult), S["dec_done"])
                if kind == "kdec2":
                    step(ts(k_dec2[:, 0, :], k_dec[:, 0:P], small[:, 4:5], None, ALU.mult))
                    step(ts(k_dec2[:, 1, :], k_dec[:, P:2 * P], small[:, 5:6], None, ALU.mult))
                    chain(ts(k_dec2[:, 2, :], k_dec2[:, 0, :], small[:, 5:6], None, ALU.mult), S["dec_done"])

            def merge(u):
                kind, h, n = units[u]
                if kind in MM:
                    acc = full(("unit", u))
                    dst = scT[:, h % 2, 0:4, :]
                    src = acc[:, :].rearrange("p (t n) -> p t n", t=NT)
                    if kind == "diag":
                        if h >= 2:
                            bank, cnt, _ = uses[("value", h - 2)]
                            dve.wait_ge(bank_full[bank], cnt)
                        ins = tt(dst, src, ident[:, None, :].to_broadcast([P, NT, P]), ALU.mult)
                    elif kind == "level":
                        ins = v.copy_predicated(dst, level_mask[:, n:n + 1, :].bitcast(U16).to_broadcast([P, NT, P]), src)
                    else:
                        o = 4 if kind == "kdec" else 7
                        ins = v.tensor_copy(scT[:, h % 2, o:o + 3, :], src[:, 0:3, :])
                    release(ins, ("unit", u))
                    dve.sem_inc(S["merge_done"], 1)
                if kind == "value":
                    norm_head(h, 0)

            def norm_head(h, part):
                n = part * AH + h
                dve.wait_ge(S["ms_done"], h + 1 if part == 0 else AH + NT * (h + 1))
                var, r = stats[:, :, 4 + h], stats[:, :, 8 + h]
                chain(ts(var, stats[:, :, h], 1.0 / P, 1e-6, ALU.mult, ALU.add), S["var_ready"])
                dve.wait_ge(S["root_ready"], n + 1)
                refine(r, var, stats[:, :, 12])
                for t in range(NT):
                    if part == 0:
                        o = o_even[:, t, h * P:(h + 1) * P]
                        key = ("value", h)
                        ins = stt(o, full(key)[:, t * P:(t + 1) * P], r[:, t:t + 1], o, ALU.mult, ALU.mult)
                        (release(ins, key) if t == NT - 1 else step(ins))
                    else:
                        o = o_even[:, t, 512 + h * P:512 + (h + 1) * P]
                        step(ts(o, o, r[:, t:t + 1], None, ALU.mult))

            U = len(units)
            for u in range(U + 3):
                if 0 <= u - 3 < U:
                    merge(u - 3)
                if u < U:
                    before(u)
                if 0 <= u - 1 < U:
                    after(u - 1)
            dve.sem_inc(S["act_free"], 1)

            N = AH * NT
            for s in range(N + 5):
                if s < N:
                    n = (s % NT + 1) * P
                    if s >= 2:
                        dve.wait_ge(S["exp_done"], s - 1)
                    for m in range(2):
                        acc = full(("score", s, m))
                        c = 24 + 4 * (s % 2) + m
                        step(v.tensor_reduce(small[:, c:c + 1], acc[:, 0:n], AX_X, ALU.max))
                        chain(ts(small[:, c:c + 1], small[:, c:c + 1], -(HD ** -0.5), None, ALU.mult), S["max_done"])
                if 1 <= s <= N:
                    u = s - 1
                    n = (u % NT + 1) * P
                    c = 26 + 4 * (u % 2)
                    dve.wait_ge(S["exp_done"], u + 1)
                    step(v.reciprocal(small[:, 40:42], small[:, c:c + 2]))
                    step(tt(small[:, 41:42], small[:, 41:42], small[:, 2:3], ALU.mult))
                    a, b = p_map[:, u % 3, 0, 0:n], p_map[:, u % 3, 1, 0:n]
                    step(ts(b, b, small[:, 41:42], None, ALU.mult))
                    chain(stt(a, a, small[:, 40:41], b, ALU.mult, ALU.add), S["mix_done"])
                if s >= 5:
                    u = s - 5
                    h, i = u // NT, u % NT
                    dve.wait_ge(S["ms_done"], AH + u + 1)
                    key = ("diff", u)
                    release(v.tensor_copy(o_even[:, i, 512 + h * P:512 + (h + 1) * P], full(key)[:, 0:P]), key)
                    if i == NT - 1:
                        norm_head(h, 1)
            dve.sem_inc(S["o_ready"], 1)

            def add_left(key, t, half):
                xs = x_res[:, t, half * 512:(half + 1) * 512]
                release(stt(xs, xs, ALPHA, full(key)[:, :], ALU.mult, ALU.add), key)
                step(v.bn_stats(stats[:, t, 6 * half:6 * half + 6], xs))

            def norm(tag, name, n):
                for t in range(NT):
                    add_left((*name, 1, t), t, 1)
                    st = stats[:, t, :]
                    step(v.bn_aggr(st[:, 12:14], st[:, 0:12]))
                    chain(ts(st[:, 13:14], st[:, 13:14], 1e-5, None, ALU.add), S["ln_arg"])
                    dve.wait_ge(S["ln_done"], AH + n * NT + t + 1)
                    refine(st[:, 14:15], st[:, 13:14], st[:, 15:16])
                    step(ts(x_res[:, t, :], x_res[:, t, :], st[:, 12:13], st[:, 14:15], ALU.subtract, ALU.mult))
                    for i in range(2):
                        xs = x_res[:, t, i * 512:(i + 1) * 512]
                        ga, be = full(("rows", n, i)), full(("rows", n, 2 + i))
                        ins = tt(xs, xs, ga[:, :], ALU.mult)
                        (release(ins, ("rows", n, i)) if t == NT - 1 else step(ins))
                        ins = tt(xs, xs, be[:, :], ALU.add)
                        (release(ins, ("rows", n, 2 + i)) if t == NT - 1 else step(ins))
                    dve.sem_inc(S["norm_done"], 1)
                    if t >= 1:
                        split_lo(tag, t - 1)
                split_lo(tag, NT - 1)

            def mixer_tail(l):
                for t in range(NT):
                    split_lo(f"o{l}", t)
                for t in range(NT):
                    add_left((f"out{l}", 0, t), t, 0)
                norm(f"n1_{l}", (f"out{l}",), 2 * l)

            def swiglu_dve(l):
                for j in range(NF):
                    dve.wait_ge(S["silu_done"], l * NF + j + 1)
                    if j >= 2:
                        dve.wait_ge(S["h_hi"], l * NF + j - 1)
                    acc = full((f"up{l}", j, 1))
                    release(tt(h_buf(j), silu_buf(j), acc[:, :], ALU.mult), (f"up{l}", j, 1))
                    dve.sem_inc(S["h_mul"], 1)
                    if j >= 1:
                        lo_h(l, j - 1)
                lo_h(l, NF - 1)
                for t in range(NT):
                    add_left((f"down{l}", 0, t), t, 0)
                norm(f"n2_{l}", (f"down{l}",), 2 * l + 1)

            def lo_h(l, j):
                dve.wait_ge(S["h_hi"], l * NF + j + 1)
                chain(tt(hT_lo[:, j, :], h_buf(j), hT_hi[:, j, :].bitcast(F32), ALU.subtract), S["h_lo"])

            mixer_tail(0)
            swiglu_dve(0)

            dve.wait_ge(fox_in, 16 * N_FOX)
            for t in range(NT):
                key = ("fox_f", t)
                release(tt(gate[:, 0, t, :], full(key)[:, 0:FH], bf_row[:, :], ALU.add), key)
            step(ts(gate[:, 1, :, :], gate[:, 0, :, :], -1.0, None, ALU.mult))
            chain(tt(gate[:, 1, :, :], gate[:, 1, :, :], gate[:, 0, :, :], ALU.min), S["f_arg"])
            dve.wait_ge(S["f_exp"], 1)
            chain(ts(gate[:, 1, :, :], gate[:, 1, :, :], 1.0, None, ALU.add), S["f_arg"])
            dve.wait_ge(S["f_ln"], 1)
            step(ts(gate[:, 0, :, :], gate[:, 0, :, :], 0.0, None, ALU.min))
            chain(tt(gate[:, 2, :, :], gate[:, 0, :, :], gate[:, 1, :, :], ALU.subtract), S["logf_done"])
            step(v.memset(qn[:, :, :, HD:HA], 1.0))

            def fox_heads(part, half, t):
                n = (2 * half + part) * NT + t
                key = (f"fox{'qk'[part]}{half}", t)
                dve.wait_ge(S["sq_done"], n + 1)
                m = fox_ms[:, n % 2, :, :]
                step(v.tensor_reduce(m[:, 0, :], sq[:, n % 2, :].rearrange("p (h d) -> p h d", h=8), AX_X, ALU.add))
                chain(ts(m[:, 0, :], m[:, 0, :], 1.0 / HD, 1e-6, ALU.mult, ALU.add), S["qvar"])
                dve.wait_ge(S["qroot"], n + 1)
                refine(m[:, 1, :], m[:, 0, :], m[:, 2, :])
                if n >= 2:
                    p2, h2, t2 = (n - 2) // NT % 2, (n - 2) // (2 * NT), (n - 2) % NT
                    bank, cnt, _ = uses[("heads", p2, h2, t2, 1)]
                    dve.wait_ge(bank_full[bank], cnt)
                q = qn[:, n % 2, :, :]
                release(tt(q[:, :, 0:HD], full(key)[:, :].rearrange("p (h d) -> p h d", h=8),
                           m[:, 1, :].unsqueeze(2).to_broadcast([P, 8, HD]), ALU.mult), key)
                hs = slice(half * 8, half * 8 + 8)
                if n == 0:
                    step(v.tensor_copy(gate[:, 3, :, :], full("cum")[:, 0:NT * FH].rearrange("p (t h) -> p t h", t=NT)))
                    release(ts(gate[:, 4, :, :], full("cum")[:, 0:NT * FH].rearrange("p (t h) -> p t h", t=NT),
                               -1.0, None, ALU.mult), "cum")
                if part == 0:
                    step(v.tensor_copy(q[:, :, HD], gate[:, 3, t, hs]))
                    chain(v.memset(q[:, :, HD + 1], 1.0), S["qn_done"])
                else:
                    step(v.tensor_copy(q[:, :, HD + 1], gate[:, 4, t, hs]))
                    chain(v.memset(q[:, :, HD], 1.0), S["qn_done"])

            for half in range(2):
                for part in range(2):
                    for t in range(NT):
                        fox_heads(part, half, t)
                N = 8 * NT
                base = half * N
                for s in range(N + 3):
                    if s < N:
                        n = (s % NT + 1) * P
                        c = 32 + s % 4
                        acc = full(("fs", half, s))
                        if s >= 4:
                            dve.wait_ge(S["fexp"], base + s - 3)
                        chain(v.tensor_reduce(small[:, c:c + 1], acc[:, 0:n], AX_X, ALU.max, negate=True), S["fmax"])
                    if s >= 3:
                        u = s - 3
                        h, i = u // NT, u % NT
                        key = ("fv", half, u)
                        acc = full(key)
                        if u == 0:
                            dve.wait_ge(S["g_done"], NT * (half + 1))
                        step(v.reciprocal(small[:, 40:41], small[:, 36 + u % 4:37 + u % 4]))
                        o = o_fox[:, i, (half * 8 + h) * HD:(half * 8 + h + 1) * HD]
                        release(stt(o, acc[:, 0:HD], small[:, 40:41], o, ALU.mult, ALU.mult), key)
                        dve.sem_inc(S["ffin"], 1)
            dve.sem_inc(S["o_ready"], 1)
            mixer_tail(1)
            swiglu_dve(1)


_INS = ["x", "even_w_in", "even_w_out", "hgrn_lb_logits", "diff_lq1", "diff_lk1", "diff_lq2", "diff_lk2",
        "hgrn_norm_g", "diff_norm_g", "fox_w_in", "fox_w_out", "fox_b_f", "fox_qnorm_g", "fox_knorm_g",
        "ffn_w1", "ffn_w2", "ln1_g", "ln1_b", "ln2_g", "ln2_b"]


def _constants():
    import numpy as np

    i = np.arange(P)
    masks = np.zeros((P, 2 + len(LEVELS), P), np.float32)
    masks[:, 0, :] = np.where(i[None, :] > i[:, None], -1e30, 0.0)
    masks[:, 1, :] = np.where(i[None, :] // CHUNK > i[:, None] // CHUNK, -1e30, 0.0)
    for n, z in enumerate(LEVELS):
        same = i[:, None] // (2 * z) == i[None, :] // (2 * z)
        masks[:, 2 + n, :] = same & (i[:, None] % (2 * z) < z) & (i[None, :] % (2 * z) >= z)
    return {
        "c_ident": np.eye(P, dtype=np.float32),
        "c_masks": masks,
        "c_tri": (i[:, None] <= i[None, :]).astype(np.float32),
        "c_ones": np.ones((P, P), np.float32),
    }


def kernel(**inputs):
    import numpy as _np
    import concourse.bacc as _bacc
    from concourse import mybir as _mybir
    from concourse.bass_utils import run_bass_kernel_spmd as _run

    nc = _bacc.Bacc("TRN2", target_bir_lowering=False, num_devices=1)
    arrays, args = {}, {}
    for name, a in [(n, inputs[n]) for n in _INS] + list(_constants().items()):
        a = _np.ascontiguousarray(a)
        arrays[f"in_{name}_dram"] = a
        args[name] = nc.dram_tensor(f"in_{name}_dram", a.shape, _mybir.dt.from_np(a.dtype),
                                    kind="ExternalInput").ap()
    out = nc.dram_tensor("out_0_dram", (1, TS, D), F32, kind="ExternalOutput").ap()
    build(nc, args, out)
    r = _run(nc, [arrays], core_ids=[0])
    return r.results[0]["out_0_dram"]
```

```python
import math
from contextlib import ExitStack

import concourse.bass as bass
from concourse import mybir

F32 = mybir.dt.float32
F32R = mybir.dt.float32r
BF16 = mybir.dt.bfloat16
U16 = mybir.dt.uint16
ALU = mybir.AluOpType
ACT = mybir.ActivationFunctionType
AX_X = mybir.AxisListType.X

P = 128
D = 1024
TS = 512
NT = TS // P
KD = D // P
DEPTH = 2
AH = 4
FH = 16
HD = 64
CHUNK = 64
HA = HD + 2
D_FF = 2816
NF = D_FF // P
ALPHA = (2 * DEPTH) ** 0.25
LAM_INIT = 0.8 - 0.6 * math.exp(-0.3 * 0)
LEVELS = [64, 32, 16, 8, 4, 2, 1]
SLOT = 2048
RAW = 2
RING = 3
PIECES = 4
FOX_PARTS = [[("q", 0), ("k", 0), ("v", 0), ("g", 0)], [("q", 1), ("k", 1), ("v", 1)],
             [("q", 2), ("k", 2), ("g", 1)], [("q", 3), ("k", 3)]]
FOX_ORDER = [x for part in FOX_PARTS for x in part]
QUARTER = 4 * NT
TINY = 2.0 ** -64
LN_EXP = "natural_log_exp_and_others"


def weight_chunks(w):
    out = []

    def feature_major(stage, m, n0):
        out.append((stage, [(0, m[:, n0:n0 + 256].rearrange("(k p) n -> p k n", p=P), KD, 256)], KD * 256))

    def token_major(stage, m, n0, k0, nk, width=512):
        src = m[k0 * P:(k0 + nk) * P, n0:n0 + width].rearrange("(k p) n -> p k n", p=P)
        out.append((stage, [(0, src, nk, width)], nk * width))

    def columns(stage, m, n0):
        token_major(stage, m, n0, 0, 4)
        token_major(stage, m, n0, 4, 4)

    def tail(l, mixer_out):
        for half in range(2):
            columns(f"out{l}", mixer_out, half * 512)
        for j in range(NF):
            w1 = w["ffn_w1"][l].rearrange("(k p) n -> p k n", p=P)
            out.append((f"up{l}", [(0, w1[:, :, j * P:(j + 1) * P], KD, P),
                                   (KD * P, w1[:, :, D_FF + j * P:D_FF + (j + 1) * P], KD, P)], SLOT))
        for half in range(2):
            k0 = 0
            for nk in [2, 4, 4, 4, 4, 4]:
                token_major(f"down{l}", w["ffn_w2"][l], half * 512, k0, nk)
                k0 += nk

    we = w["even_w_in"][0]
    for stage, n0 in (("a_f", 512), ("a_q", 0)):
        for i in range(2):
            feature_major(stage, we, n0 + 256 * i)
    columns("a_i", we, 1024)
    for stage, n0 in (("b_q", 2048), ("b_k", 2560)):
        for i in range(2):
            feature_major(stage, we, n0 + 256 * i)
    columns("b_v", we, 3072)
    columns("a_g", we, 1536)
    tail(0, w["even_w_out"][0])
    wf = w["fox_w_in"][0]
    token_major("fox_f", wf, 4 * D, 0, KD, FH)
    for name, i in FOX_ORDER:
        n0 = "qkvg".index(name) * D
        if name in "qk":
            token_major(f"fox{name}{i}", wf, n0 + 256 * i, 0, KD, 256)
        else:
            columns(f"fox{name}{i}", wf, n0 + 512 * i)
    tail(1, w["fox_w_out"][0])
    return out


def build(nc, w, out):
    chunks = weight_chunks(w)
    stage_chunks = {}
    for c, (stage, _, _) in enumerate(chunks):
        stage_chunks.setdefault(stage, []).append(c)

    with ExitStack() as ctx:
        top = [-(-nc.sbuf_base // 32) * 32]

        def at(name, shape, dt, offset):
            return nc.alloc_sbuf_tensor_at(name, shape, dt, offset=offset)

        def place(name, free, dt, size):
            t = at(name, [P, *free], dt, top[0])
            n = size
            for f in free:
                n *= f
            top[0] += -(-n // 32) * 32
            return t

        x_res = place("x_res", [NT, D], F32, 4)
        xT_hi = place("xT_hi", [KD, TS], F32R, 4)
        xT_lo = place("xT_lo", [KD, TS], F32R, 4)
        w_raw = [place(f"w_raw{i}", [SLOT], F32, 4) for i in range(RAW)]
        w_hi = [place(f"w_hi{i}", [SLOT], F32R, 4) for i in range(RING)]
        w_lo = [place(f"w_lo{i}", [SLOT], F32R, 4) for i in range(RING)]
        ident = place("ident", [P], F32, 4)
        ident_bf = place("ident_bf", [P], BF16, 2)
        fox_mask = place("fox_mask", [P], BF16, 2)
        diff_mask = place("diff_mask", [P], BF16, 2)
        level_mask = place("level_mask", [len(LEVELS), P], BF16, 2)
        ln_rows = place("ln_rows", [D], F32, 4)
        stats = place("stats", [NT, 20], F32, 4)
        small = place("small", [48], F32, 4)
        gains = place("gains", [12], F32, 4)
        arena = top[0]

        def take(name, free, dt, at_el):
            t = at(name, [P, *free], dt, arena + 4 * at_el)
            n = 1
            for f in free:
                n *= f
            return t, at_el + n

        hT_hi, e = take("hT_hi", [NF, TS], F32R, 0)
        hT_lo, _ = take("hT_lo", [NF, TS], F32R, e)
        silu_g = at("silu_g", [P, NF, TS], F32, arena + 4 * NF * TS)
        qT, e = take("qT", [AH, TS], F32, 0)
        kT, e = take("kT", [AH, TS], F32, e)
        bT, e = take("bT", [AH, TS], F32, e)
        q_dec, e = take("q_dec", [TS], F32, e)
        k_dec, e = take("k_dec", [TS], F32, e)
        k_dec2, e = take("k_dec2", [3, P], F32, e)
        scT, e = take("scT", [2, 10, P], F32, e)
        iv, e = take("iv", [NT, 512], F32, e)
        bqT, e = take("bqT", [AH, TS], F32, e)
        bkT, e = take("bkT", [AH, TS], F32, e)
        bv, e = take("bv", [NT, 512], F32, e)
        o_even, e = take("o_even", [NT, D], F32, e)
        junk, e = take("junk", [P], F32, e)
        assert e <= 2 * NF * TS, e
        p_map, e2 = take("p_map", [3, 2, TS], F32, 0)
        pT_diff, e2 = take("pT_diff", [2, TS], F32, e2)
        a_gate, e2 = take("a_gate", [NT, 512], F32, e2)
        assert e2 <= 3 * AH * TS
        qA, e = take("qA", [2, 4, TS], F32, 0)
        kA, e = take("kA", [2, 4, TS], F32, e)
        v_all, e = take("v_all", [NT, D], F32, e)
        o_fox, e = take("o_fox", [NT, D], F32, e)
        p_fox, e = take("p_fox", [3, TS], F32, e)
        pT_fox, e = take("pT_fox", [2, TS], F32, e)
        qn, e = take("qn", [2, 4, HA], F32, e)
        sq, e = take("sq", [2, 256], F32, e)
        tri, e = take("tri", [P], F32, e)
        ones, e = take("ones", [P], F32, e)
        gate, e = take("gate", [5, NT, FH], F32, e)
        fox_ms, e = take("fox_ms", [2, 3, 4], F32, e)
        bf_row, e = take("bf_row", [FH], F32, e)
        assert e <= 2 * NF * TS, e
        top[0] = arena + 2 * NF * TS * 4
        assert top[0] <= nc.sbuf_top, (top[0], nc.sbuf_top)

        banks = ctx.enter_context(nc.psum_tensor("banks", [P, 8, 512], F32))
        psum = [banks[:, b, :] for b in range(8)]

        def sem(name):
            return ctx.enter_context(nc.semaphore(name))

        w_loaded = [sem(f"w_loaded{i}") for i in range(RAW)]
        hi_ready, lo_ready, w_used = sem("hi_ready"), sem("lo_ready"), sem("w_used")
        consts_in, fox_in, x_in, out_done = sem("consts_in"), sem("fox_in"), sem("x_in"), sem("out_done")
        lam_in = sem("lam_in")
        bank_full = [sem(f"bank{b}_full") for b in range(8)]
        freed = {"act": [sem(f"bank{b}_read_act") for b in range(8)],
                 "dve": [sem(f"bank{b}_read_dve") for b in range(8)]}
        act_step, dve_step = sem("act_step"), sem("dve_step")
        T_hi, T_lo = sem("T_hi"), sem("T_lo")
        S = {}

        def named(*names):
            for n in names:
                S[n] = sem(n)

        named("norm_done", "o_ready", "var_ready", "root_ready", "silu_done", "h_hi", "h_lo", "h_mul",
              "arena_free", "sig_done", "q_done", "gate_done", "i_done", "bq_done", "bk_done", "bv_done",
              "ln_arg", "ln_done", "k_done", "e_arg", "e_done", "dec_done", "sc_used", "merge_done",
              "ms_done", "max_done", "exp_done", "mix_done", "turned", "pT_done", "pv_done",
              "lam_arg", "lam_exp", "o_dve",
              "f_arg", "f_exp", "f_ln", "logf_done", "c_done", "sq_done", "qvar", "qroot", "qn_done", "qn_used",
              "qA_done", "v_done", "g_done", "act_free", "fmax", "fexp", "fturn", "fpT", "fpv", "ffin")

        chunk_used = {}
        PAIR = {(t, t): t for t in range(NT)} | {(0, 1): 4, (1, 2): 5, (2, 3): 6, (0, 2): 7, (1, 3): 8, (0, 3): 9}

        uses, bank_count, last = {}, [0] * 8, [None] * 8
        read_count = {"act": [0] * 8, "dve": [0] * 8}

        rows = [w[n][l:l + 1, :] for l in range(DEPTH) for n in ("ln1_g", "ln1_b", "ln2_g", "ln2_b")]
        n_masks = 2 + len(LEVELS)
        masks_f32 = bkT[:, :, :].rearrange("p h n -> p (h n)")[:, 0:n_masks * P].rearrange("p (m n) -> p m n", n=P)
        consts = [(ident[:, :], w["c_ident"]), (masks_f32, w["c_masks"]),
                  (gains[:, 0:1], w["hgrn_norm_g"].rearrange("o d -> d o")),
                  (gains[:, 1:2], w["diff_norm_g"].rearrange("o d -> d o")),
                  (gains[0:HD, 4:5], w["fox_qnorm_g"].rearrange("o d -> d o")),
                  (gains[0:HD, 5:6], w["fox_knorm_g"].rearrange("o d -> d o")),
                  (gains[HD:P, 4:6], w["c_ones"][0:P - HD, 0:2]),
                  ]
        consts += [(gains[:, 8 + h:9 + h], w["hgrn_lb_logits"][:, h * P:(h + 1) * P].rearrange("o d -> d o"))
                   for h in range(AH)]
        consts += [(ln_rows[i:i + 1, :], row) for i, row in enumerate(rows)]
        lam_loads = [(bv[:, 0, i * HD:(i + 1) * HD], w[n][0:1, :].to_broadcast([P, HD]))
                     for i, n in enumerate(("diff_lq1", "diff_lk1", "diff_lq2", "diff_lk2"))]
        fox_loads = [(tri[:, :], w["c_tri"]), (ones[:, :], w["c_ones"]),
                     (bf_row[:, :], w["fox_b_f"][0:1, :].to_broadcast([P, FH]))]
        N_CONSTS, N_FOX = len(consts), len(fox_loads)

        block = ctx.enter_context(nc.Block())

        def chunk_at(stage, i=0):
            return stage_chunks[stage][i]

        def hi(c, a, n):
            return w_hi[c % RING][:, a:a + n]

        def lo(c, a, n):
            return w_lo[c % RING][:, a:a + n]

        units = []
        for h in range(AH):
            units += [("diag", h, 0)] + [("level", h, n) for n in range(len(LEVELS))]
            units += [("qdec", h, 0), ("kdec", h, 0), ("kdec2", h, 0)]
            if h:
                units.insert(len(units) - 7, ("value", h - 1, 0))
        units += [("none", 0, 0)] * 3 + [("value", AH - 1, 0)] + [("none", 0, 0)] * 3
        mixed = [c for s in ("a_i", "b_q", "b_k", "b_v") for c in stage_chunks[s]]
        even_seq = []
        n = 0
        for c in mixed:
            for p in range(PIECES):
                even_seq.append(("piece", c, p))
                if n < len(units):
                    even_seq.append(("unit", n, 0))
                    n += 1
                if p == 3 or p == 1:
                    even_seq.append(("unit", n, 0))
                    n += 1
        while n < len(units):
            even_seq.append(("unit", n, 0))
            n += 1

        D_UNITS = AH * NT
        gate_pieces = [(c, p) for c in stage_chunks["a_g"] for p in range(PIECES)]
        GATE_AT = len(gate_pieces) + 1

        def pieces_of(names):
            return [(c, p) for name, i in names for c in stage_chunks[f"fox{name}{i}"] for p in range(PIECES)]

        fox_slots = [(piece, None) for piece in pieces_of(FOX_PARTS[0])]
        F_UNITS = 4 * QUARTER
        for j in range(4):
            between = pieces_of(FOX_PARTS[j + 1]) if j < 3 else []
            span = max(len(between), QUARTER - 4)
            for i in range(QUARTER):
                a, b = (min(n * len(between) // span, len(between)) for n in (i, i + 1))
                assert b - a <= 1
                fox_slots.append((between[a] if b > a else None, QUARTER * j + i))
        fox_slots += [(None, F_UNITS + i) for i in range(3)]

        def heads_at(i):
            if not 0 <= i < len(fox_slots) or fox_slots[i][0] is None:
                return None
            c, p = fox_slots[i][0]
            stage = chunks[c][0]
            if stage[3] not in "qk":
                return None
            part, j = "qk".index(stage[3]), int(stage[4])
            return part, j, p, (2 * j + part) * NT + p

        def group_at(i):
            if not 0 <= i < len(fox_slots) or fox_slots[i][0] is None:
                return None
            c, p = fox_slots[i][0]
            stage = chunks[c][0]
            return (stage, p) if stage[3] in "vg" and stage_chunks[stage][1] == c else None

        def nth(kinds, u):
            return sum(1 for k, _, _ in units[:u] if k in kinds)

        MM = ("diag", "level", "kdec", "kdec2")
        ARG = ("level", "kdec")
        EXP = ("level", "qdec", "kdec")
        DEC = ("level", "qdec", "kdec", "kdec2")

        def groups_of(c):
            stage = chunks[c][0]
            i = stage_chunks[stage].index(c)
            if stage in ("a_f", "a_q", "b_q", "b_k"):
                return [(stage, 2 * i), (stage, 2 * i + 1)]
            if stage == "fox_f" or i % 2 == 1:
                return [(stage, t) for t in range(NT)]
            return []

        def dec_buf(n):
            return o_even[:, 2 + n % 2, 512:D]

        def exp_buf(n):
            return o_even[:, n % 2, 512:D]

        def silu_buf(j):
            return silu_g[:, j, :]

        def h_buf(j):
            return psum[4 + j % 2]

        @block.tensor
        def _(pe):
            mm = nc.tensor.matmul

            def open_bank(key, bank, reader):
                if last[bank]:
                    who, count = last[bank]
                    pe.wait_ge(freed[who][bank], count)
                read_count[reader][bank] += 1
                bank_count[bank] += 1
                last[bank] = (reader, read_count[reader][bank])
                uses[key] = (bank, bank_count[bank], reader)
                return psum[bank]

            def close_bank(key, ins):
                ins.then_inc(bank_full[uses[key][0]], 1)

            def used_with_bank(c, key):
                chunk_used[c] = (bank_full[uses[key][0]], uses[key][1])

            alone = [0]

            def used_alone(c, ins):
                ins.then_inc(w_used, 1)
                alone[0] += 1
                chunk_used[c] = (w_used, alone[0])

            gid = [0]

            def next_gemm_bank():
                gid[0] += 1
                return (gid[0] - 1) % 4

            def products(acc, l_hi, l_lo, r_hi, r_lo, first, final):
                mm(acc, l_hi, r_lo, start=first, stop=False)
                mm(acc, l_lo, r_hi, start=False, stop=False)
                return mm(acc, l_hi, r_hi, start=False, stop=final)

            def weights_in(c):
                pe.wait_ge(hi_ready, c + 1)
                pe.wait_ge(lo_ready, c + 1)

            def feature_chunk(c, reader):
                stage, _, _ = chunks[c]
                weights_in(c)
                for j, key in enumerate(groups_of(c)):
                    acc = open_bank(key, next_gemm_bank(), reader)
                    for k in range(KD):
                        a = k * 256 + j * P
                        ins = products(acc[:, :], hi(c, a, P), lo(c, a, P), xT_hi[:, k, :], xT_lo[:, k, :],
                                       k == 0, k == KD - 1)
                        if k == KD // 2 - 1:
                            yield
                    close_bank(key, ins)
                    if j == 1:
                        used_with_bank(c, key)
                    yield

            def token_chunk(c, reader, src_hi, src_lo, k_base, first, final, width=512):
                stage, _, size = chunks[c]
                nk = size // width
                weights_in(c)
                for t in range(NT):
                    key = (stage, t) if not isinstance(final, tuple) else (*final, t)
                    if first:
                        open_bank((stage, "acc", t, c), next_gemm_bank(), reader)
                        acc_bank[t] = uses[(stage, "acc", t, c)]
                    acc = psum[acc_bank[t][0]][:, 0:width]
                    for k in range(nk):
                        tok = slice(t * P, (t + 1) * P)
                        ins = products(acc, src_hi[:, k_base + k, tok], src_lo[:, k_base + k, tok],
                                       hi(c, k * width, width), lo(c, k * width, width),
                                       first and k == 0, bool(final) and k == nk - 1)
                    if final:
                        uses[key] = acc_bank[t]
                        close_bank(key, ins)
                    if t == NT - 1:
                        if final:
                            used_with_bank(c, key)
                        else:
                            used_alone(c, ins)
                    yield

            acc_bank = [None] * NT

            def columns(stage, reader, src_hi=xT_hi, src_lo=xT_lo):
                a, b = stage_chunks[stage]
                yield from token_chunk(a, reader, src_hi, src_lo, 0, True, False)
                yield from token_chunk(b, reader, src_hi, src_lo, 4, False, True)

            def drain(pieces):
                for _ in pieces:
                    pass

            turns = [0]

            def turn_tile(tag, t, src, ready):
                for r in range(2):
                    if r == 0:
                        ready()
                    key = (tag, t, r)
                    acc = open_bank(key, t, "dve")
                    for j in range(4):
                        f = (4 * r + j) * P
                        ins = nc.tensor.transpose(acc[:, j * P:(j + 1) * P], src[:, t, f:f + P], ident[:, :])
                    close_bank(key, ins)

            def wait_tiles(n):
                pe.wait_ge(T_hi, 2 * n)
                pe.wait_ge(T_lo, 2 * n)

            pe.wait_ge(consts_in, 16 * N_CONSTS)

            for t in range(NT):
                turn_tile("x", t, x_res, lambda: pe.wait_ge(x_in, 16))
            turned_tiles = [NT]

            def norm_tail(tag, step, src_tiles):
                for t in range(NT + 2):
                    if t < NT:
                        src_tiles(t)
                    if t >= 2:
                        n = step * NT + t - 1
                        turn_tile(tag, t - 2, x_res, lambda: pe.wait_ge(S["norm_done"], n))
                turned_tiles[0] += NT

            def mixer_out(l):
                o = o_even if l == 0 else o_fox
                pe.wait_ge(S["o_ready"], l + 1)
                for t in range(NT):
                    turn_tile(f"o{l}", t, o, lambda: None)
                turned_tiles[0] += NT
                wait_tiles(turned_tiles[0])
                a, b, c2, d2 = stage_chunks[f"out{l}"]
                drain(token_chunk(a, "dve", xT_hi, xT_lo, 0, True, False))
                drain(token_chunk(b, "dve", xT_hi, xT_lo, 4, False, (f"out{l}", 0)))
                tail_products((f"out{l}", 1), [(c2, 0), (d2, 4)], xT_hi, xT_lo, f"n1_{l}", 2 * l)

            def tail_products(name, parts, src_hi, src_lo, tag, step, acc_open=False):
                def tile(t):
                    key = (*name, t)
                    if not acc_open:
                        open_bank((*name, "acc", t), next_gemm_bank(), "dve")
                        acc_bank[t] = uses[(*name, "acc", t)]
                    acc = psum[acc_bank[t][0]][:, :]
                    tok = slice(t * P, (t + 1) * P)
                    for n, (c, k0) in enumerate(parts):
                        if t == 0:
                            weights_in(c)
                        nk = chunks[c][2] // 512
                        for k in range(nk):
                            ins = products(acc, src_hi[:, k0 + k, tok], src_lo[:, k0 + k, tok],
                                           hi(c, k * 512, 512), lo(c, k * 512, 512),
                                           not acc_open and n == 0 and k == 0,
                                           n == len(parts) - 1 and k == nk - 1)
                        if t == NT - 1:
                            if n < len(parts) - 1:
                                used_alone(c, ins)
                            else:
                                uses[key] = acc_bank[t]
                                close_bank(key, ins)
                                used_with_bank(c, key)
                        elif n == len(parts) - 1:
                            uses[key] = acc_bank[t]
                            close_bank(key, ins)

                norm_tail(tag, step, tile)

            def swiglu(l):
                wait_tiles(turned_tiles[0])
                for j, c in enumerate(stage_chunks[f"up{l}"]):
                    weights_in(c)
                    for part in range(2):
                        key = (f"up{l}", j, part)
                        acc = open_bank(key, next_gemm_bank(), "act" if part == 0 else "dve")
                        for k in range(KD):
                            a = part * KD * P + k * P
                            ins = products(acc[:, :], hi(c, a, P), lo(c, a, P), xT_hi[:, k, :],
                                           xT_lo[:, k, :], k == 0, k == KD - 1)
                        close_bank(key, ins)
                    used_with_bank(c, key)
                cs = stage_chunks[f"down{l}"]
                pe.wait_ge(S["h_lo"], (l + 1) * NF)
                spread_rows(2 * l + 1)
                k0 = 0
                for i in range(6):
                    drain(token_chunk(cs[i], "dve", hT_hi, hT_lo, k0, i == 0, (f"down{l}", 0) if i == 5 else False))
                    k0 += chunks[cs[i]][2] // 512
                k0 = 0
                for i in range(6, 9):
                    drain(token_chunk(cs[i], "dve", hT_hi, hT_lo, k0, i == 6, False))
                    k0 += chunks[cs[i]][2] // 512
                parts = []
                for i in range(9, 12):
                    parts.append((cs[i], k0))
                    k0 += chunks[cs[i]][2] // 512
                tail_products((f"down{l}", 1), parts, hT_hi, hT_lo, f"n2_{l}", 2 * l + 1, acc_open=True)

            def spread_rows(n):
                for i in range(4):
                    key = ("rows", n, i)
                    acc = open_bank(key, 4 + i, "dve")
                    row = 2 * n + i // 2
                    sel = ident[0:8, row:row + 1].to_broadcast([8, P])
                    close_bank(key, mm(acc[:, :], sel, ln_rows[0:8, (i % 2) * 512:(i % 2) * 512 + 512],
                                       start=True, stop=True))

            wait_tiles(NT)
            for c in stage_chunks["a_f"] + stage_chunks["a_q"]:
                drain(feature_chunk(c, "act"))

            def unit_products(u):
                kind, h, n = units[u]
                if kind in MM:
                    m = nth(MM, u)
                    acc = open_bank(("unit", u), 4 + m % 2, "dve")
                if kind == "diag":
                    pe.wait_ge(S["k_done"], h + 1)
                    for t in range(NT):
                        ins = mm(acc[:, t * P:(t + 1) * P], kT[:, h, t * P:(t + 1) * P],
                                 qT[:, h, t * P:(t + 1) * P], start=True, stop=True)
                if kind == "level":
                    pe.wait_ge(S["dec_done"], nth(DEC, u) + 1)
                    d = dec_buf(nth(("level",), u))
                    for t in range(NT):
                        ins = mm(acc[:, t * P:(t + 1) * P], d[:, t * P:(t + 1) * P], d[:, t * P:(t + 1) * P],
                                 start=True, stop=True)
                if kind == "kdec":
                    pe.wait_ge(S["dec_done"], nth(DEC, u) + 1)
                    for i in range(3):
                        ins = mm(acc[:, i * P:(i + 1) * P], k_dec[:, i * P:(i + 1) * P],
                                 q_dec[:, (i + 1) * P:(i + 2) * P], start=True, stop=True)
                if kind == "kdec2":
                    pe.wait_ge(S["dec_done"], nth(DEC, u) + 1)
                    for i, t in enumerate((2, 3, 3)):
                        ins = mm(acc[:, i * P:(i + 1) * P], k_dec2[:, i, :], q_dec[:, t * P:(t + 1) * P],
                                 start=True, stop=True)
                if kind in MM:
                    close_bank(("unit", u), ins)
                if kind == "value":
                    acc = open_bank(("value", h), 6 + h % 2, "dve")
                    pe.wait_ge(S["merge_done"], 10 * (h + 1))
                    pe.wait_ge(S["i_done"], NT)
                    for t in range(NT):
                        for s in range(t + 1):
                            ins = mm(acc[:, t * P:(t + 1) * P], scT[:, h % 2, PAIR[(s, t)], :],
                                     iv[:, s, h * P:(h + 1) * P], start=s == 0, stop=s == t)
                    close_bank(("value", h), ins)

            pieces = {}
            for kind, a, b in even_seq:
                if kind == "unit":
                    unit_products(a)
                    continue
                stage = chunks[a][0]
                if stage not in pieces:
                    if stage in ("a_i", "b_v"):
                        pieces[stage] = columns(stage, "act")
                    else:
                        x0, x1 = stage_chunks[stage]
                        pieces[stage] = (y for c in (x0, x1) for y in feature_chunk(c, "act"))
                next(pieces[stage], None)
            for stage in ("a_i", "b_q", "b_k", "b_v"):
                drain(pieces[stage])

            pe.wait_ge(S["bq_done"], 4)
            pe.wait_ge(S["bk_done"], 4)
            pe.wait_ge(S["bv_done"], 4)
            N = D_UNITS
            gen = columns("a_g", "act")
            for s in range(N + 3):
                if s < len(gate_pieces):
                    next(gen)
                if s == GATE_AT - 1:
                    drain(gen)
                wide = s >= GATE_AT
                if s < N:
                    h, i = s // NT, s % NT
                    for m in range(2):
                        key = ("score", s, m)
                        acc = open_bank(key, (0 if wide and s % 2 else 4) + m, "act")
                        n = (i + 1) * P
                        rows = slice(m * HD, (m + 1) * HD)
                        mm(acc[:, 0:n], bqT[rows, h, i * P:(i + 1) * P], bkT[rows, h, 0:n], start=True, stop=False)
                        close_bank(key, mm(acc[:, n - P:n], ident_bf[:, :], diff_mask[:, :], start=False, stop=True))
                if 2 <= s < N + 2:
                    u = s - 2
                    i = u % NT
                    pe.wait_ge(S["mix_done"], u + 1)
                    acc = open_bank(("pT", u), 2 if wide and u % 2 else 6, "act")
                    for j in range(i + 1):
                        ins = nc.tensor.transpose(acc[:, j * P:(j + 1) * P], p_map[:, u % 3, 0, j * P:(j + 1) * P],
                                                  ident[:, :])
                    close_bank(("pT", u), ins)
                if s >= 3:
                    u = s - 3
                    h, i = u // NT, u % NT
                    pe.wait_ge(S["pT_done"], u + 1)
                    acc = open_bank(("diff", u), 3 if wide and u % 2 else 7, "dve")
                    for j in range(i + 1):
                        ins = mm(acc[:, 0:P], pT_diff[:, u % 2, j * P:(j + 1) * P], bv[:, j, h * P:(h + 1) * P],
                                 start=j == 0, stop=j == i)
                    close_bank(("diff", u), ins)

            spread_rows(0)
            mixer_out(0)
            swiglu(0)

            wait_tiles(turned_tiles[0])
            drain(token_chunk(stage_chunks["fox_f"][0], "dve", xT_hi, xT_lo, 0, True, True, FH))
            pe.wait_ge(fox_in, 16 * N_FOX)

            def turn_heads(part, j, t, n):
                pe.wait_ge(S["qn_done"], n + 1)
                key = ("heads", n)
                acc = open_bank(key, 7, "act")
                for i in range(4):
                    ins = nc.tensor.transpose(acc[0:HA, i * P:(i + 1) * P], qn[:, n % 2, i, :], ident[:, :])
                close_bank(key, ins)

            def gates():
                acc = open_bank("cum", 6, "dve")
                pe.wait_ge(S["logf_done"], 1)
                for t in range(NT):
                    for s in range(t + 1):
                        ins = mm(acc[:, t * FH:(t + 1) * FH], (tri if s == t else ones)[:, :], gate[:, 2, s, :],
                                 start=s == 0, stop=s == t)
                close_bank("cum", ins)

            running = {}
            for i, (piece, s) in enumerate(fox_slots):
                if piece:
                    stage = chunks[piece[0]][0]
                    if stage not in running:
                        if stage[3] in "qk":
                            running[stage] = token_chunk(piece[0], "dve", xT_hi, xT_lo, 0, True, True, 256)
                        else:
                            running[stage] = columns(stage, "act")
                    next(running[stage])
                if i == 1:
                    gates()
                if heads_at(i - 2):
                    turn_heads(*heads_at(i - 2))
                if s is None:
                    continue
                wide = s >= 3 * QUARTER + 1
                if s < F_UNITS:
                    h, i = s // NT, s % NT
                    n = (i + 1) * P
                    j = s // QUARTER
                    if s % QUARTER == 0:
                        pe.wait_ge(S["qA_done"], 2 * NT * (j + 1))
                        pe.wait_ge(S["v_done"], NT * (j // 2 + 1))
                    acc = open_bank(("fs", s), (4, 0, 1)[s % 3] if wide else 4, "act")
                    mm(acc[:, 0:n], qA[0:HA, j % 2, h % 4, i * P:(i + 1) * P], kA[0:HA, j % 2, h % 4, 0:n],
                       start=True, stop=False)
                    close_bank(("fs", s), mm(acc[:, n - P:n], ident_bf[:, :], fox_mask[:, :], start=False, stop=True))
                if 2 <= s < F_UNITS + 2:
                    u = s - 2
                    i = u % NT
                    pe.wait_ge(S["fexp"], u + 1)
                    acc = open_bank(("fT", u), 2 if wide and u % 2 else 5, "act")
                    for j in range(i + 1):
                        ins = nc.tensor.transpose(acc[:, j * P:(j + 1) * P], p_fox[:, u % 3, j * P:(j + 1) * P],
                                                  ident[:, :])
                    close_bank(("fT", u), ins)
                if s >= 3:
                    u = s - 3
                    h, i = u // NT, u % NT
                    pe.wait_ge(S["fpT"], u + 1)
                    acc = open_bank(("fv", u), 3 if wide and u % 2 else 6, "dve")
                    for j in range(i + 1):
                        ins = mm(acc[:, 0:HD], pT_fox[:, u % 2, j * P:(j + 1) * P], v_all[:, j, h * HD:(h + 1) * HD],
                                 start=j == 0, stop=j == i)
                    close_bank(("fv", u), ins)
            for gen in running.values():
                drain(gen)
            spread_rows(2)
            mixer_out(1)
            swiglu(1)

        @block.sync
        def _(sp):
            sp.dma_start(x_res[:, :, :], w["x"][0].rearrange("(t p) d -> p t d", p=P)).then_inc(x_in, 16)

            def load(c):
                if c >= RAW:
                    sp.wait_ge(lo_ready, c - RAW + 1)
                for off, src, a, b in chunks[c][1]:
                    dst = w_raw[c % RAW][:, off:off + a * b].rearrange("p (a b) -> p a b", a=a)
                    sp.dma_start(dst, src).then_inc(w_loaded[c % RAW], 16)

            load(0)
            for dst, src in consts:
                sp.dma_start(dst, src).then_inc(consts_in, 16)
            for dst, src in lam_loads:
                sp.dma_start(dst, src).then_inc(lam_in, 16)
            for c in range(1, len(chunks)):
                if chunks[c][0] == "fox_f":
                    sp.wait_ge(S["norm_done"], 2 * NT)
                    for dst, src in fox_loads:
                        sp.dma_start(dst, src).then_inc(fox_in, 16)
                load(c)
            o = out[0].rearrange("(t p) d -> p t d", p=P)
            for t in range(NT):
                sp.wait_ge(S["norm_done"], 3 * NT + t + 1)
                sp.dma_start(o[:, t, :], x_res[:, t, :]).then_inc(out_done, 16)
            sp.wait_ge(out_done, 16 * NT)

        @block.gpsimd
        def _(pool):
            for c, (_, _, size) in enumerate(chunks):
                pool.wait_ge(hi_ready, c + 1)
                if c >= RING:
                    pool.wait_ge(*chunk_used[c - RING])
                for a in range(0, size, 1024):
                    n = min(1024, size - a)
                    ins = nc.gpsimd.tensor_tensor(w_lo[c % RING][:, a:a + n], w_raw[c % RAW][:, a:a + n],
                                                  w_hi[c % RING][:, a:a + n].bitcast(F32), ALU.subtract)
                ins.then_inc(lo_ready, 1)

        def reader_of(eng, counts):
            def full(key):
                bank, n, _ = uses[key]
                eng.wait_ge(bank_full[bank], n)
                return psum[bank]

            def chain(ins, s):
                ins.then_inc(s, 1)
                counts[id(s)] = counts.get(id(s), 0) + 1
                eng.wait_ge(s, counts[id(s)])

            return full, chain

        @block.scalar
        def _(act):
            counts = {}
            full, chain = reader_of(act, counts)
            step = lambda ins: chain(ins, act_step)
            release = lambda ins, key: chain(ins, freed["act"][uses[key][0]])
            fn = nc.scalar.activation
            rounded = [0]
            loaded = {0: 0, 1: 0}
            need = []
            for c, (_, loads, _) in enumerate(chunks):
                loaded[c % RAW] += 16 * len(loads)
                need.append(loaded[c % RAW])

            def hi_upto(n):
                while rounded[0] < min(n, len(chunks)):
                    c = rounded[0]
                    act.wait_ge(w_loaded[c % RAW], need[c])
                    if c >= RING:
                        act.wait_ge(*chunk_used[c - RING])
                    size = chunks[c][2]
                    chain(fn(w_hi[c % RING][:, 0:size], w_raw[c % RAW][:, 0:size], ACT.Copy), hi_ready)
                    rounded[0] += 1

            def split_hi(tag, t):
                for r in range(2):
                    acc = full((tag, t, r))
                    dst = xT_hi[:, 4 * r:4 * r + 4, t * P:(t + 1) * P]
                    src = acc[:, :].rearrange("p (k n) -> p k n", k=4)
                    if tag == "o0":
                        chain(fn(dst, src, ACT.Copy, scale=gains[:, r:r + 1]), T_hi)
                    else:
                        chain(fn(dst, src, ACT.Copy), T_hi)

            roots = [0]

            def root(dst, src, arg_sem, n, done):
                act.wait_ge(arg_sem, n)
                step(fn(dst, src, ACT.Ln))
                chain(fn(dst, dst, ACT.Exp, scale=-0.5), done)

            def evac(key, dst, src_fn, func=ACT.Copy):
                acc = full(key)
                release(fn(dst, src_fn(acc), func), key)

            whole = lambda acc: acc[:, :]

            hi_upto(2)
            act.wait_ge(S["lam_arg"], 1)
            chain(fn(small[:, 0:2], small[:, 0:2], ACT.Exp), S["lam_exp"])
            chain(fn(small[:, 16:20], small[:, 16:20], ACT.Exp), S["lam_exp"])
            for t in range(NT):
                split_hi("x", t)
                hi_upto(3)
            def projected(stage, dst, func):
                for h in range(AH):
                    hi_upto(stage_chunks[stage][h // 2] + 3)
                    evac((stage, h), dst[:, h, :], whole, func)

            projected("a_f", kT, ACT.Sigmoid)
            act.sem_inc(S["sig_done"], 1)
            nc.scalar.preload_act_table_set("natural_log")
            for h in range(AH):
                act.wait_ge(S["ln_arg"], h + 1)
                step(fn(q_dec[:, :], q_dec[:, :], ACT.Ln))
                chain(fn(k_dec[:, :], k_dec[:, :], ACT.Ln), S["ln_done"])
                if h == 1:
                    hi_upto(stage_chunks["a_q"][0] + 3)
            projected("a_q", qT, ACT.Silu)
            act.sem_inc(S["q_done"], 1)
            nc.scalar.preload_act_table_set(LN_EXP)

            def unit_act(u):
                if u >= 3 and units[u - 3][0] == "value":
                    h = units[u - 3][1]
                    root(stats[:, :, 8 + h], stats[:, :, 4 + h], S["var_ready"], h + 1, S["root_ready"])
                kind, h, n = units[u]
                if kind in EXP:
                    buf = exp_buf(nth(EXP, u))
                    if kind == "qdec":
                        act.wait_ge(S["k_done"], h + 1)
                        e = nth(DEC, u)
                        act.wait_ge(S["dec_done"], e - 1)
                        chain(fn(buf, bT[:, h, :], ACT.Exp), S["e_done"])
                    else:
                        act.wait_ge(S["e_arg"], nth(ARG, u) + 1)
                        chain(fn(buf, buf, ACT.Exp), S["e_done"])
                if kind == "value":
                    acc = full(("value", h))
                    for t in range(NT):
                        ins = fn(junk[:, :], acc[:, t * P:(t + 1) * P], ACT.Square, accum_out=stats[:, t, h:h + 1])
                        if t < NT - 1:
                            step(ins)
                        else:
                            chain(ins, S["ms_done"])

            due = []
            finished = {}
            for kind, a, b in even_seq:
                if kind == "unit":
                    unit_act(a)
                    continue
                for key in due:
                    dst = {"a_i": iv, "b_v": bv, "b_q": bqT, "b_k": bkT}[key[0]]
                    if key[0] == "b_v" and key[1] == 0:
                        act.wait_ge(S["lam_arg"], 1)
                    evac(key, dst[:, key[1], :], whole)
                    act.sem_inc(S[{"a_i": "i_done", "b_v": "bv_done", "b_q": "bq_done", "b_k": "bk_done"}[key[0]]], 1)
                due = []
                hi_upto(a + 2 if b < 2 else a + 3) if b == 1 or b == 3 else None
                g = groups_of(a)
                if len(g) == 2:
                    due = [g[0]] if b == 1 else [g[1]] if b == 3 else []
                elif g:
                    due = [g[b]]
            for key in due:
                evac(key, bv[:, key[1], :], whole)
                act.sem_inc(S["bv_done"], 1)

            N = D_UNITS
            for s in range(N + 4):
                if s == GATE_AT:
                    for t in range(NT):
                        evac(("a_g", t), a_gate[:, t, :], whole, ACT.Silu)
                    act.sem_inc(S["gate_done"], 1)
                    nc.scalar.preload_act_table_set(LN_EXP)
                if s in (1, 5, 9):
                    hi_upto(stage_chunks["a_g"][0] + 2 + s // 4)
                if s < N:
                    i = s % NT
                    n = (i + 1) * P
                    if s == 0:
                        act.wait_ge(S["act_free"], 1)
                    if s >= 2:
                        act.wait_ge(S["mix_done"], s - 1)
                    if s >= 3:
                        bank, cnt, _ = uses[("pT", s - 3)]
                        act.wait_ge(bank_full[bank], cnt)
                    for m in range(2):
                        act.wait_ge(S["max_done"], 2 * s + m + 1)
                        key = ("score", s, m)
                        acc = full(key)
                        ins = fn(p_map[:, s % 3, m, 0:n], acc[:, 0:n], ACT.Exp, bias=small[:, 24 + 4 * (s % 2) + m:25 + 4 * (s % 2) + m],
                                 scale=HD ** -0.5, accum_out=small[:, 26 + 4 * (s % 2) + m:27 + 4 * (s % 2) + m])
                        release(ins, key)
                    act.sem_inc(S["exp_done"], 1)
                if 2 <= s < N + 2:
                    u = s - 2
                    n = (u % NT + 1) * P
                    acc = full(("pT", u))
                    if u >= 2:
                        bank, cnt, _ = uses[("diff", u - 2)]
                        act.wait_ge(bank_full[bank], cnt)
                    release(fn(pT_diff[:, u % 2, 0:n], acc[:, 0:n], ACT.Copy), ("pT", u))
                    act.sem_inc(S["pT_done"], 1)
                if 4 <= s:
                    u = s - 4
                    acc = full(("diff", u))
                    chain(fn(junk[:, :], acc[:, 0:P], ACT.Square, accum_out=stats[:, u % NT, u // NT:u // NT + 1]),
                          S["ms_done"])
                    if u % NT == NT - 1:
                        h = u // NT
                        root(stats[:, :, 8 + h], stats[:, :, 4 + h], S["var_ready"], AH + h + 1, S["root_ready"])

            def mixer_tail(l):
                for t in range(NT):
                    split_hi(f"o{l}", t)
                hi_upto(stage_chunks[f"out{l}"][0] + 3)
                hi_upto(stage_chunks[f"out{l}"][2] + 2)
                hi_upto(stage_chunks[f"up{l}"][0] + 1)
                norm_act(f"n1_{l}", 2 * l, stage_chunks[f"up{l}"][0])

            def norm_act(tag, step_n, after):
                nc.scalar.preload_act_table_set(LN_EXP)
                for t in range(NT):
                    root(stats[:, t, 14:15], stats[:, t, 13:14], S["ln_arg"], AH + step_n * NT + t + 1, S["ln_done"])
                    if t >= 1:
                        if t == NT - 1:
                            hi_upto(after + 1)
                        split_hi(tag, t - 1)
                hi_upto(after + 2)
                split_hi(tag, NT - 1)
                hi_upto(after + 3)

            def swiglu_act(l):
                for j, c in enumerate(stage_chunks[f"up{l}"]):
                    hi_upto(c + 2)
                    acc = full((f"up{l}", j, 0))
                    release(fn(silu_buf(j), acc[:, :], ACT.Silu), (f"up{l}", j, 0))
                    act.sem_inc(S["silu_done"], 1)
                    hi_upto(c + 3)
                    if j >= 1:
                        act.wait_ge(S["h_mul"], l * NF + j)
                        chain(fn(hT_hi[:, j - 1, :], h_buf(j - 1), ACT.Copy), S["h_hi"])
                act.wait_ge(S["h_mul"], l * NF + NF)
                chain(fn(hT_hi[:, NF - 1, :], h_buf(NF - 1), ACT.Copy), S["h_hi"])
                cs = stage_chunks[f"down{l}"]
                hi_upto(cs[-1] + 1)
                norm_act(f"n2_{l}", 2 * l + 1, cs[-1] + 1)

            mixer_tail(0)
            swiglu_act(0)

            act.wait_ge(S["f_arg"], 1)
            chain(fn(gate[:, 1, :, :], gate[:, 1, :, :], ACT.Exp), S["f_exp"])
            act.wait_ge(S["f_arg"], 2)
            nc.scalar.preload_act_table_set("natural_log")
            chain(fn(gate[:, 1, :, :], gate[:, 1, :, :], ACT.Ln), S["f_ln"])

            nc.scalar.preload_act_table_set(LN_EXP)
            for i, (piece, s) in enumerate(fox_slots):
                if i == 0:
                    continue
                if piece and piece[1] == 1:
                    hi_upto(piece[0] + 3)
                if group_at(i - 1):
                    stage, t = group_at(i - 1)
                    if stage[3] == "v":
                        half = int(stage[4])
                        evac((stage, t), v_all[:, t, 512 * half:512 * half + 512], whole)
                        act.sem_inc(S["v_done"], 1)
                    elif t == NT - 1:
                        half = int(stage[4])
                        for t in range(NT):
                            evac((stage, t), o_fox[:, t, 512 * half:512 * half + 512], whole, ACT.Sigmoid)
                        act.sem_inc(S["g_done"], 1)
                        nc.scalar.preload_act_table_set(LN_EXP)
                if heads_at(i - 1):
                    part, j, t, n = heads_at(i - 1)
                    acc = full((f"fox{'qk'[part]}{j}", t))
                    if n >= 2:
                        act.wait_ge(S["qvar"], n - 1)
                    chain(fn(sq[:, n % 2, :], acc[:, 0:256], ACT.Square), S["sq_done"])
                if s is not None and s < F_UNITS:
                    n = (s % NT + 1) * P
                    act.wait_ge(S["fmax"], s + 1)
                    if s >= 3:
                        full(("fT", s - 3))
                    if s >= 4:
                        act.wait_ge(S["ffin"], s - 3)
                    key = ("fs", s)
                    ins = fn(p_fox[:, s % 3, 0:n], full(key)[:, 0:n], ACT.Exp, bias=small[:, 32 + s % 4:33 + s % 4],
                             accum_out=small[:, 36 + s % 4:37 + s % 4])
                    release(ins, key)
                    act.sem_inc(S["fexp"], 1)
                if heads_at(i - 1):
                    part, j, t, n = heads_at(i - 1)
                    root(fox_ms[:, n % 2, 1, :], fox_ms[:, n % 2, 0, :], S["qvar"], n + 1, S["qroot"])
                if s is not None and 2 <= s < F_UNITS + 2:
                    u = s - 2
                    n = (u % NT + 1) * P
                    key = ("fT", u)
                    acc = full(key)
                    if u >= 2:
                        full(("fv", u - 2))
                    release(fn(pT_fox[:, u % 2, 0:n], acc[:, 0:n], ACT.Copy), key)
                    act.sem_inc(S["fpT"], 1)
                if heads_at(i - 2):
                    part, j, t, n = heads_at(i - 2)
                    acc = full(("heads", n))
                    dst = (qA, kA)[part][0:HA, j % 2, :, t * P:(t + 1) * P]
                    src = acc[0:HA, :].rearrange("p (k n) -> p k n", k=4)
                    release(fn(dst, src, ACT.Copy, scale=gains[0:HA, 4 + part:5 + part]), ("heads", n))
                    act.sem_inc(S["qA_done"], 1)
            hi_upto(stage_chunks["out1"][0] + 2)
            mixer_tail(1)
            swiglu_act(1)

        @block.vector
        def _(dve):
            counts = {}
            full, chain = reader_of(dve, counts)
            step = lambda ins: chain(ins, dve_step)
            release = lambda ins, key: chain(ins, freed["dve"][uses[key][0]])
            v = nc.vector
            tt, ts, stt = v.tensor_tensor, v.tensor_scalar, v.scalar_tensor_tensor
            split = [0]

            def split_lo(tag, t):
                for r in range(2):
                    split[0] += 1
                    acc = full((tag, t, r))
                    dve.wait_ge(T_hi, split[0])
                    tok = slice(t * P, (t + 1) * P)
                    dst = xT_lo[:, 4 * r:4 * r + 4, tok]
                    high = xT_hi[:, 4 * r:4 * r + 4, tok].bitcast(F32)
                    src = acc[:, :].rearrange("p (k n) -> p k n", k=4)
                    if tag == "o0":
                        ins = stt(dst, src, gains[:, r:r + 1], high, ALU.mult, ALU.subtract)
                    else:
                        ins = tt(dst, src, high, ALU.subtract)
                    release(ins, (tag, t, r))
                    dve.sem_inc(T_lo, 1)

            def free_now(key):
                s = freed["dve"][uses[key][0]]
                counts[id(s)] = counts.get(id(s), 0) + 1
                dve.sem_inc(s, 1)

            def refine(r, var, tmp):
                step(tt(tmp, r, r, ALU.mult))
                step(tt(tmp, tmp, var, ALU.mult))
                step(ts(tmp, tmp, -0.5, 1.5, ALU.mult, ALU.add))
                step(tt(r, r, tmp, ALU.mult))

            dve.wait_ge(consts_in, 16 * N_CONSTS)
            dve.wait_ge(lam_in, 16 * len(lam_loads))
            step(v.tensor_copy(ident_bf[:, :], ident[:, :]))
            step(v.tensor_copy(fox_mask[:, :], masks_f32[:, 0, :]))
            step(v.tensor_copy(diff_mask[:, :], masks_f32[:, 1, :]))
            step(v.tensor_copy(level_mask[:, :, :], masks_f32[:, 2:n_masks, :]))
            lam_rows = bv[:, 0, 0:4 * HD].rearrange("p (a b) -> p a b", a=4)
            for m in range(2):
                step(tt(bv[:, 1, m * HD:(m + 1) * HD], lam_rows[:, 2 * m, :], lam_rows[:, 2 * m + 1, :], ALU.mult))
                step(v.tensor_reduce(small[:, m:m + 1], bv[:, 1, m * HD:(m + 1) * HD], AX_X, ALU.add))
            lg = gains[:, 8:12]
            step(tt(small[:, 16:20], lg, lg, ALU.subtract))
            step(ts(gains[:, 1:2], gains[:, 1:2], 1.0 - LAM_INIT, None, ALU.mult))
            step(ts(gains[0:HD, 4:5], gains[0:HD, 4:5], HD ** -0.5, None, ALU.mult))
            dve.sem_inc(S["lam_arg"], 1)
            for t in range(NT):
                split_lo("x", t)

            dve.wait_ge(S["lam_exp"], 2)
            step(tt(small[:, 2:3], small[:, 1:2], small[:, 0:1], ALU.subtract))
            step(ts(small[:, 2:3], small[:, 2:3], -LAM_INIT, None, ALU.add))
            step(v.reciprocal(small[:, 20:24], small[:, 16:20]))
            step(tt(small[:, 16:20], small[:, 16:20], small[:, 20:24], ALU.mult))
            step(tt(small[:, 8:12], small[:, 16:20], small[:, 16:20], ALU.subtract))
            step(ts(small[:, 12:16], small[:, 8:12], -1.0, 1.0, ALU.mult, ALU.add))
            dve.wait_ge(S["sig_done"], 1)
            for h in range(AH):
                k = kT[:, h, :]
                step(ts(k, k, small[:, 12 + h:13 + h], small[:, 8 + h:9 + h], ALU.mult, ALU.add))
                step(ts(q_dec[:, :], k, TINY, None, ALU.max))
                step(ts(k_dec[:, :], k, 1.0 / TINY, 1.0, ALU.mult, ALU.min))
                chain(ts(k, k, -1.0, 1.0, ALU.mult, ALU.add), S["ln_arg"])
                dve.wait_ge(S["ln_done"], h + 1)
                for t in range(NT):
                    tok = slice(t * P, (t + 1) * P)
                    ins = v.tensor_tensor_scan(bT[:, h, tok], q_dec[:, tok], k_dec[:, tok], 0.0, ALU.add, ALU.add)
                    if t < NT - 1:
                        step(ins)
                chain(ins, S["k_done"])
            dve.wait_ge(S["q_done"], 1)

            def halves(ap, b):
                return ap.rearrange("p (n two b) -> p n two b", two=2, b=b)

            def before(u):
                kind, h, n = units[u]
                if kind in ARG:
                    x = nth(EXP, u)
                    buf = exp_buf(x)
                    b = bT[:, h, :]
                    if kind == "level":
                        z = LEVELS[n]
                        bb, ee = halves(b, z), halves(buf, z)
                        mid = bb[:, :, 0, z - 1:z].to_broadcast([P, TS // (2 * z), z])
                        step(tt(ee[:, :, 1, :], bb[:, :, 1, :], mid, ALU.subtract))
                        chain(tt(ee[:, :, 0, :], mid, bb[:, :, 0, :], ALU.subtract), S["e_arg"])
                    else:
                        bb = b.rearrange("p (t n) -> p t n", t=NT)
                        ee = buf.rearrange("p (t n) -> p t n", t=NT)
                        end = bb[:, :, P - 1:P].to_broadcast([P, NT, P])
                        chain(tt(ee, end, bb, ALU.subtract), S["e_arg"])

            def after(u):
                kind, h, n = units[u]
                if kind in EXP:
                    dve.wait_ge(S["e_done"], nth(EXP, u) + 1)
                    buf = exp_buf(nth(EXP, u))
                if kind == "level":
                    m = nth(("level",), u)
                    if m >= 2:
                        prev = [x for x in range(u) if units[x][0] == "level"][-2]
                        bank, cnt, _ = uses[("unit", prev)]
                        dve.wait_ge(bank_full[bank], cnt)
                    z = LEVELS[n]
                    d, ee = halves(dec_buf(m), z), halves(buf, z)
                    qq, kk = halves(qT[:, h, :], z), halves(kT[:, h, :], z)
                    step(tt(d[:, :, 1, :], qq[:, :, 1, :], ee[:, :, 1, :], ALU.mult))
                    chain(tt(d[:, :, 0, :], kk[:, :, 0, :], ee[:, :, 0, :], ALU.mult), S["dec_done"])
                if kind in ("qdec", "kdec") and h:
                    prev = [x for x in range(u) if units[x][0] == "kdec2"][-1]
                    bank, cnt, _ = uses[("unit", prev)]
                    dve.wait_ge(bank_full[bank], cnt)
                if kind == "qdec":
                    step(v.tensor_copy(small[:, 3:7], buf.rearrange("p (t n) -> p t n", t=NT)[:, :, P - 1]))
                    chain(tt(q_dec[:, :], qT[:, h, :], buf, ALU.mult), S["dec_done"])
                if kind == "kdec":
                    chain(tt(k_dec[:, :], kT[:, h, :], buf, ALU.mult), S["dec_done"])
                if kind == "kdec2":
                    step(ts(k_dec2[:, 0, :], k_dec[:, 0:P], small[:, 4:5], None, ALU.mult))
                    step(ts(k_dec2[:, 1, :], k_dec[:, P:2 * P], small[:, 5:6], None, ALU.mult))
                    chain(ts(k_dec2[:, 2, :], k_dec2[:, 0, :], small[:, 5:6], None, ALU.mult), S["dec_done"])

            def merge(u):
                kind, h, n = units[u]
                if kind in MM:
                    acc = full(("unit", u))
                    dst = scT[:, h % 2, 0:4, :]
                    src = acc[:, :].rearrange("p (t n) -> p t n", t=NT)
                    if kind == "diag":
                        if h >= 2:
                            bank, cnt, _ = uses[("value", h - 2)]
                            dve.wait_ge(bank_full[bank], cnt)
                        ins = tt(dst, src, ident[:, None, :].to_broadcast([P, NT, P]), ALU.mult)
                    elif kind == "level":
                        ins = v.copy_predicated(dst, level_mask[:, n:n + 1, :].bitcast(U16).to_broadcast([P, NT, P]), src)
                    else:
                        o = 4 if kind == "kdec" else 7
                        ins = v.tensor_copy(scT[:, h % 2, o:o + 3, :], src[:, 0:3, :])
                    release(ins, ("unit", u))
                    dve.sem_inc(S["merge_done"], 1)
                if kind == "value":
                    norm_head(h, 0)

            def norm_head(h, part):
                n = part * AH + h
                dve.wait_ge(S["ms_done"], h + 1 if part == 0 else AH + NT * (h + 1))
                var, r = stats[:, :, 4 + h], stats[:, :, 8 + h]
                chain(ts(var, stats[:, :, h], 1.0 / P, 1e-6, ALU.mult, ALU.add), S["var_ready"])
                dve.wait_ge(S["root_ready"], n + 1)
                refine(r, var, stats[:, :, 12])
                for t in range(NT):
                    if part == 0:
                        o = o_even[:, t, h * P:(h + 1) * P]
                        key = ("value", h)
                        ins = ts(o, full(key)[:, t * P:(t + 1) * P], r[:, t:t + 1], None, ALU.mult)
                        (release(ins, key) if t == NT - 1 else step(ins))
                    else:
                        o = o_even[:, t, 512 + h * P:512 + (h + 1) * P]
                        step(ts(o, o, r[:, t:t + 1], None, ALU.mult))

            U = len(units)
            for u in range(U + 3):
                if 0 <= u - 3 < U:
                    merge(u - 3)
                if u < U:
                    before(u)
                if 0 <= u - 1 < U:
                    after(u - 1)
            dve.sem_inc(S["act_free"], 1)

            N = D_UNITS
            for s in range(N + 4):
                if GATE_AT + 1 <= s <= GATE_AT + NT:
                    t = s - GATE_AT - 1
                    dve.wait_ge(S["gate_done"], 1)
                    step(tt(o_even[:, t, 0:512], o_even[:, t, 0:512], a_gate[:, t, :], ALU.mult))
                if s < N:
                    n = (s % NT + 1) * P
                    if s >= 2:
                        dve.wait_ge(S["exp_done"], s - 1)
                    for m in range(2):
                        acc = full(("score", s, m))
                        c = 24 + 4 * (s % 2) + m
                        step(v.tensor_reduce(small[:, c:c + 1], acc[:, 0:n], AX_X, ALU.max))
                        chain(ts(small[:, c:c + 1], small[:, c:c + 1], -(HD ** -0.5), None, ALU.mult), S["max_done"])
                if 1 <= s <= N:
                    u = s - 1
                    n = (u % NT + 1) * P
                    c = 26 + 4 * (u % 2)
                    dve.wait_ge(S["exp_done"], u + 1)
                    step(v.reciprocal(small[:, 40:42], small[:, c:c + 2]))
                    step(tt(small[:, 41:42], small[:, 41:42], small[:, 2:3], ALU.mult))
                    a, b = p_map[:, u % 3, 0, 0:n], p_map[:, u % 3, 1, 0:n]
                    step(ts(b, b, small[:, 41:42], None, ALU.mult))
                    chain(stt(a, a, small[:, 40:41], b, ALU.mult, ALU.add), S["mix_done"])
                if s >= 4:
                    u = s - 4
                    h, i = u // NT, u % NT
                    dve.wait_ge(S["ms_done"], AH + u + 1)
                    key = ("diff", u)
                    release(v.tensor_copy(o_even[:, i, 512 + h * P:512 + (h + 1) * P], full(key)[:, 0:P]), key)
                    if i == NT - 1:
                        norm_head(h, 1)
            dve.sem_inc(S["o_ready"], 1)

            def add_left(key, t, half):
                xs = x_res[:, t, half * 512:(half + 1) * 512]
                release(stt(xs, xs, ALPHA, full(key)[:, :], ALU.mult, ALU.add), key)
                step(v.bn_stats(stats[:, t, 6 * half:6 * half + 6], xs))

            def norm(tag, name, n):
                for t in range(NT):
                    add_left((*name, 1, t), t, 1)
                    st = stats[:, t, :]
                    step(v.bn_aggr(st[:, 12:14], st[:, 0:12]))
                    chain(ts(st[:, 13:14], st[:, 13:14], 1e-5, None, ALU.add), S["ln_arg"])
                    dve.wait_ge(S["ln_done"], AH + n * NT + t + 1)
                    r, tmp = st[:, 14:15], st[:, 15:16]
                    step(stt(tmp, r, r, st[:, 13:14], ALU.mult, ALU.mult))
                    step(ts(tmp, tmp, -0.5, 1.5, ALU.mult, ALU.add))
                    step(tt(r, r, tmp, ALU.mult))
                    for i in range(4):
                        full(("rows", n, i))
                    xs = x_res[:, t, :].rearrange("p (a b) -> p a b", a=2)
                    step(stt(xs, xs, st[:, 12:13], banks[:, 4:6, :], ALU.subtract, ALU.mult))
                    chain(stt(xs, xs, r, banks[:, 6:8, :], ALU.mult, ALU.add), S["norm_done"])
                    if t == NT - 1:
                        for i in range(4):
                            free_now(("rows", n, i))
                    if t >= 1:
                        split_lo(tag, t - 1)
                split_lo(tag, NT - 1)

            def mixer_tail(l):
                for t in range(NT):
                    split_lo(f"o{l}", t)
                for t in range(NT):
                    add_left((f"out{l}", 0, t), t, 0)
                norm(f"n1_{l}", (f"out{l}",), 2 * l)

            def swiglu_dve(l):
                for j in range(NF):
                    dve.wait_ge(S["silu_done"], l * NF + j + 1)
                    if j >= 2:
                        dve.wait_ge(S["h_hi"], l * NF + j - 1)
                    acc = full((f"up{l}", j, 1))
                    release(tt(h_buf(j), silu_buf(j), acc[:, :], ALU.mult), (f"up{l}", j, 1))
                    dve.sem_inc(S["h_mul"], 1)
                    if j >= 1:
                        lo_h(l, j - 1)
                lo_h(l, NF - 1)
                for t in range(NT):
                    add_left((f"down{l}", 0, t), t, 0)
                norm(f"n2_{l}", (f"down{l}",), 2 * l + 1)

            def lo_h(l, j):
                dve.wait_ge(S["h_hi"], l * NF + j + 1)
                chain(tt(hT_lo[:, j, :], h_buf(j), hT_hi[:, j, :].bitcast(F32), ALU.subtract), S["h_lo"])

            mixer_tail(0)
            swiglu_dve(0)

            dve.wait_ge(fox_in, 16 * N_FOX)
            for t in range(NT):
                key = ("fox_f", t)
                release(tt(gate[:, 0, t, :], full(key)[:, 0:FH], bf_row[:, :], ALU.add), key)
            step(ts(gate[:, 1, :, :], gate[:, 0, :, :], -1.0, None, ALU.mult))
            chain(tt(gate[:, 1, :, :], gate[:, 1, :, :], gate[:, 0, :, :], ALU.min), S["f_arg"])
            dve.wait_ge(S["f_exp"], 1)
            chain(ts(gate[:, 1, :, :], gate[:, 1, :, :], 1.0, None, ALU.add), S["f_arg"])
            dve.wait_ge(S["f_ln"], 1)
            step(ts(gate[:, 0, :, :], gate[:, 0, :, :], 0.0, None, ALU.min))
            chain(tt(gate[:, 2, :, :], gate[:, 0, :, :], gate[:, 1, :, :], ALU.subtract), S["logf_done"])
            step(v.memset(qn[:, :, :, HD:HA], 1.0))

            def square_sums(part, j, t, n):
                dve.wait_ge(S["sq_done"], n + 1)
                m = fox_ms[:, n % 2, :, :]
                step(v.tensor_reduce(m[:, 0, :], sq[:, n % 2, :].rearrange("p (h d) -> p h d", h=4), AX_X, ALU.add))
                chain(ts(m[:, 0, :], m[:, 0, :], 1.0 / HD, 1e-6, ALU.mult, ALU.add), S["qvar"])

            def fox_heads(part, j, t, n):
                key = (f"fox{'qk'[part]}{j}", t)
                m = fox_ms[:, n % 2, :, :]
                dve.wait_ge(S["qroot"], n + 1)
                refine(m[:, 1, :], m[:, 0, :], m[:, 2, :])
                if n >= 2:
                    full(("heads", n - 2))
                q = qn[:, n % 2, :, :]
                release(tt(q[:, :, 0:HD], full(key)[:, 0:256].rearrange("p (h d) -> p h d", h=4),
                           m[:, 1, :].unsqueeze(2).to_broadcast([P, 4, HD]), ALU.mult), key)
                if n == 0:
                    cum = full("cum")[:, 0:NT * FH].rearrange("p (t h) -> p t h", t=NT)
                    step(v.tensor_copy(gate[:, 3, :, :], cum))
                    release(ts(gate[:, 4, :, :], cum, -1.0, None, ALU.mult), "cum")
                hs = slice(4 * j, 4 * j + 4)
                step(v.tensor_copy(q[:, :, HD + part], gate[:, 3 + part, t, hs]))
                chain(v.memset(q[:, :, HD + 1 - part], 1.0), S["qn_done"])

            for i, (piece, s) in enumerate(fox_slots):
                if heads_at(i - 1):
                    square_sums(*heads_at(i - 1))
                if s is not None and s < F_UNITS:
                    n = (s % NT + 1) * P
                    c = 32 + s % 4
                    if s >= 4:
                        dve.wait_ge(S["fexp"], s - 3)
                    chain(v.tensor_reduce(small[:, c:c + 1], full(("fs", s))[:, 0:n], AX_X, ALU.max, negate=True),
                          S["fmax"])
                if heads_at(i - 1):
                    fox_heads(*heads_at(i - 1))
                if s is not None and s >= 3:
                    u = s - 3
                    h, i = u // NT, u % NT
                    key = ("fv", u)
                    acc = full(key)
                    if h % 8 == 0 and i == 0:
                        dve.wait_ge(S["g_done"], h // 8 + 1)
                    step(v.reciprocal(small[:, 40:41], small[:, 36 + u % 4:37 + u % 4]))
                    o = o_fox[:, i, h * HD:(h + 1) * HD]
                    release(stt(o, acc[:, 0:HD], small[:, 40:41], o, ALU.mult, ALU.mult), key)
                    dve.sem_inc(S["ffin"], 1)
            dve.sem_inc(S["o_ready"], 1)
            mixer_tail(1)
            swiglu_dve(1)


_INS = ["x", "even_w_in", "even_w_out", "hgrn_lb_logits", "diff_lq1", "diff_lk1", "diff_lq2", "diff_lk2",
        "hgrn_norm_g", "diff_norm_g", "fox_w_in", "fox_w_out", "fox_b_f", "fox_qnorm_g", "fox_knorm_g",
        "ffn_w1", "ffn_w2", "ln1_g", "ln1_b", "ln2_g", "ln2_b"]


def _constants():
    import numpy as np

    i = np.arange(P)
    masks = np.zeros((P, 2 + len(LEVELS), P), np.float32)
    masks[:, 0, :] = np.where(i[None, :] > i[:, None], -1e30, 0.0)
    masks[:, 1, :] = np.where(i[None, :] // CHUNK > i[:, None] // CHUNK, -1e30, 0.0)
    for n, z in enumerate(LEVELS):
        same = i[:, None] // (2 * z) == i[None, :] // (2 * z)
        masks[:, 2 + n, :] = same & (i[:, None] % (2 * z) < z) & (i[None, :] % (2 * z) >= z)
    return {
        "c_ident": np.eye(P, dtype=np.float32),
        "c_masks": masks,
        "c_tri": (i[:, None] <= i[None, :]).astype(np.float32),
        "c_ones": np.ones((P, P), np.float32),
    }


def kernel(**inputs):
    import numpy as _np
    import concourse.bacc as _bacc
    from concourse import mybir as _mybir
    from concourse.bass_utils import run_bass_kernel_spmd as _run

    nc = _bacc.Bacc("TRN2", target_bir_lowering=False, num_devices=1)
    arrays, args = {}, {}
    for name, a in [(n, inputs[n]) for n in _INS] + list(_constants().items()):
        a = _np.ascontiguousarray(a)
        arrays[f"in_{name}_dram"] = a
        args[name] = nc.dram_tensor(f"in_{name}_dram", a.shape, _mybir.dt.from_np(a.dtype),
                                    kind="ExternalInput").ap()
    out = nc.dram_tensor("out_0_dram", (1, TS, D), F32, kind="ExternalOutput").ap()
    build(nc, args, out)
    r = _run(nc, [arrays], core_ids=[0])
    return r.results[0]["out_0_dram"]
```

```python
import math
from contextlib import ExitStack

import concourse.bass as bass
from concourse import mybir

F32 = mybir.dt.float32
F32R = mybir.dt.float32r
BF16 = mybir.dt.bfloat16
U16 = mybir.dt.uint16
ALU = mybir.AluOpType
ACT = mybir.ActivationFunctionType
AX_X = mybir.AxisListType.X

P = 128
D = 1024
TS = 512
NT = TS // P
KD = D // P
DEPTH = 2
AH = 4
FH = 16
HD = 64
CHUNK = 64
HA = HD + 2
D_FF = 2816
NF = D_FF // P
ALPHA = (2 * DEPTH) ** 0.25
LAM_INIT = 0.8 - 0.6 * math.exp(-0.3 * 0)
LEVELS = [64, 32, 16, 8, 4, 2, 1]
SLOT = 2048
RAW = 2
RING = 3
PIECES = 4
FOX_PARTS = [[("q", 0), ("k", 0), ("v", 0)], [("q", 1), ("k", 1), ("v", 1)], [("q", 2), ("k", 2), ("g", 1)],
             [("q", 3), ("k", 3)], [("g", 0)]]
FOX_ORDER = [x for part in FOX_PARTS for x in part]
QUARTER = 4 * NT
TINY = 2.0 ** -64
LN_EXP = "natural_log_exp_and_others"


def weight_chunks(w):
    out = []

    def feature_major(stage, m, n0):
        out.append((stage, [(0, m[:, n0:n0 + 256].rearrange("(k p) n -> p k n", p=P), KD, 256)], KD * 256))

    def token_major(stage, m, n0, k0, nk, width=512):
        src = m[k0 * P:(k0 + nk) * P, n0:n0 + width].rearrange("(k p) n -> p k n", p=P)
        out.append((stage, [(0, src, nk, width)], nk * width))

    def columns(stage, m, n0):
        token_major(stage, m, n0, 0, 4)
        token_major(stage, m, n0, 4, 4)

    def tail(l, mixer_out):
        for half in range(2):
            columns(f"out{l}", mixer_out, half * 512)
        for j in range(NF):
            w1 = w["ffn_w1"][l].rearrange("(k p) n -> p k n", p=P)
            out.append((f"up{l}", [(0, w1[:, :, j * P:(j + 1) * P], KD, P),
                                   (KD * P, w1[:, :, D_FF + j * P:D_FF + (j + 1) * P], KD, P)], SLOT))
        for half in range(2):
            k0 = 0
            for nk in [2, 4, 4, 4, 4, 4]:
                token_major(f"down{l}", w["ffn_w2"][l], half * 512, k0, nk)
                k0 += nk

    we = w["even_w_in"][0]
    for stage, n0 in (("a_f", 512), ("a_q", 0)):
        for i in range(2):
            feature_major(stage, we, n0 + 256 * i)
    columns("a_i", we, 1024)
    for stage, n0 in (("b_q", 2048), ("b_k", 2560)):
        for i in range(2):
            feature_major(stage, we, n0 + 256 * i)
    columns("b_v", we, 3072)
    columns("a_g", we, 1536)
    tail(0, w["even_w_out"][0])
    wf = w["fox_w_in"][0]
    for name, i in FOX_ORDER:
        n0 = "qkvg".index(name) * D
        if name in "qk":
            token_major(f"fox{name}{i}", wf, n0 + 256 * i, 0, KD, 256)
        else:
            columns(f"fox{name}{i}", wf, n0 + 512 * i)
        if (name, i) == FOX_ORDER[0]:
            token_major("fox_f", wf, 4 * D, 0, KD, FH)
    tail(1, w["fox_w_out"][0])
    return out


def build(nc, w, out):
    chunks = weight_chunks(w)
    stage_chunks = {}
    for c, (stage, _, _) in enumerate(chunks):
        stage_chunks.setdefault(stage, []).append(c)

    with ExitStack() as ctx:
        top = [-(-nc.sbuf_base // 32) * 32]

        def at(name, shape, dt, offset):
            return nc.alloc_sbuf_tensor_at(name, shape, dt, offset=offset)

        def place(name, free, dt, size):
            t = at(name, [P, *free], dt, top[0])
            n = size
            for f in free:
                n *= f
            top[0] += -(-n // 32) * 32
            return t

        x_res = place("x_res", [NT, D], F32, 4)
        xT_hi = place("xT_hi", [KD, TS], F32R, 4)
        xT_lo = place("xT_lo", [KD, TS], F32R, 4)
        w_raw = [place(f"w_raw{i}", [SLOT], F32, 4) for i in range(RAW)]
        w_hi = [place(f"w_hi{i}", [SLOT], F32R, 4) for i in range(RING)]
        w_lo = [place(f"w_lo{i}", [SLOT], F32R, 4) for i in range(RING)]
        ident = place("ident", [P], F32, 4)
        ident_bf = place("ident_bf", [P], BF16, 2)
        fox_mask = place("fox_mask", [P], BF16, 2)
        diff_mask = place("diff_mask", [P], BF16, 2)
        level_mask = place("level_mask", [len(LEVELS), P], BF16, 2)
        ln_rows = place("ln_rows", [D], F32, 4)
        stats = place("stats", [NT, 20], F32, 4)
        small = place("small", [48], F32, 4)
        gains = place("gains", [12], F32, 4)
        arena = top[0]

        def take(name, free, dt, at_el):
            t = at(name, [P, *free], dt, arena + 4 * at_el)
            n = 1
            for f in free:
                n *= f
            return t, at_el + n

        hT_hi, e = take("hT_hi", [NF, TS], F32R, 0)
        hT_lo, _ = take("hT_lo", [NF, TS], F32R, e)
        silu_g = at("silu_g", [P, NF, TS], F32, arena + 4 * NF * TS)
        qT, e = take("qT", [AH, TS], F32, 0)
        kT, e = take("kT", [AH, TS], F32, e)
        lfT, e = take("lfT", [AH, TS], F32, e)
        q_dec, e = take("q_dec", [TS], F32, e)
        k_dec, e = take("k_dec", [TS], F32, e)
        k_dec2, e = take("k_dec2", [3, P], F32, e)
        scT, e = take("scT", [2, 10, P], F32, e)
        iv, e = take("iv", [NT, 512], F32, e)
        bqT, e = take("bqT", [AH, TS], F32, e)
        bkT, e = take("bkT", [AH, TS], F32, e)
        bv, e = take("bv", [NT, 512], F32, e)
        o_even, e = take("o_even", [NT, D], F32, e)
        spans = bv[:, :, :].rearrange("p t n -> p (t n)")[:, 0:(len(LEVELS) + 2) * P].rearrange("p (m n) -> p m n", n=P)
        lam_rows = bv[:, 3, 0:4 * HD]
        assert (len(LEVELS) + 2) * P <= 3 * 512
        junk, e = take("junk", [P], F32, e)
        assert e <= 2 * NF * TS, e
        p_map, e2 = take("p_map", [3, 2, TS], F32, 0)
        pT_diff, e2 = take("pT_diff", [2, TS], F32, e2)
        a_gate, e2 = take("a_gate", [NT, 512], F32, e2)
        assert e2 <= 3 * AH * TS
        rows_even, e2 = take("rows_even", [2, D], F32, 3 * AH * TS)
        rows_fox, _ = take("rows_fox", [2, D], F32, 0)
        assert 2 * D <= 4 * TS and e2 <= 3 * AH * TS + 2 * TS + 3 * P + 20 * P
        mixer_rows = [rows_even, rows_fox]
        qA, e = take("qA", [2, 4, TS], F32, 0)
        kA, e = take("kA", [2, 4, TS], F32, e)
        v_all, e = take("v_all", [NT, D], F32, e)
        o_fox, e = take("o_fox", [NT, D], F32, e)
        p_fox, e = take("p_fox", [3, TS], F32, e)
        pT_fox, e = take("pT_fox", [2, TS], F32, e)
        qn, e = take("qn", [2, 4, HA], F32, e)
        sq, e = take("sq", [2, 256], F32, e)
        gate_T, e = take("gate_T", [2, TS], F32, e)
        cum, e = take("cum", [2, NT, FH], F32, e)
        fox_ms, e = take("fox_ms", [2, 3, 4], F32, e)
        assert e <= 2 * NF * TS, e
        top[0] = arena + 2 * NF * TS * 4
        assert top[0] <= nc.sbuf_top, (top[0], nc.sbuf_top)

        banks = ctx.enter_context(nc.psum_tensor("banks", [P, 8, 512], F32))
        psum = [banks[:, b, :] for b in range(8)]

        def sem(name):
            return ctx.enter_context(nc.semaphore(name))

        w_loaded = [sem(f"w_loaded{i}") for i in range(RAW)]
        hi_ready, lo_ready, w_used = sem("hi_ready"), sem("lo_ready"), sem("w_used")
        consts_in, out_done = sem("consts_in"), sem("out_done")
        rows_in = [sem(f"norm{l}_rows_in") for l in range(DEPTH)]
        x_in = [sem(f"x{t}_in") for t in range(NT)]
        lam_in, ident_in = sem("lam_in"), sem("ident_in")
        bank_full = [sem(f"bank{b}_full") for b in range(8)]
        freed = {"act": [sem(f"bank{b}_read_act") for b in range(8)],
                 "dve": [sem(f"bank{b}_read_dve") for b in range(8)]}
        act_step, dve_step = sem("act_step"), sem("dve_step")
        T_hi, T_lo = sem("T_hi"), sem("T_lo")
        S = {}

        def named(*names):
            for n in names:
                S[n] = sem(n)

        named("norm_done", "o_ready", "var_ready", "root_ready", "silu_done", "h_hi", "h_lo", "h_mul",
              "sig_done", "q_done", "gate_done", "i_done", "bq_done", "bk_done", "bv_done", "ln_arg",
              "ln_done", "lf_done", "lfT_done", "e_done", "dec_done", "merge_done", "ms_done", "max_done",
              "exp_done", "mix_done", "pT_done", "lam_arg", "lam_exp", "f_arg", "f_ln", "logf_done",
              "sq_done", "qvar", "qroot", "qn_done", "qA_done", "v_done", "g_done", "act_free", "gated",
              "fmax", "fexp", "fpT", "ffin")

        chunk_used = {}
        PAIR = {(t, t): t for t in range(NT)} | {(0, 1): 4, (1, 2): 5, (2, 3): 6, (0, 2): 7, (1, 3): 8, (0, 3): 9}

        uses, bank_count, last = {}, [0] * 8, [None] * 8
        read_count = {"act": [0] * 8, "dve": [0] * 8}

        rows = [w[n][l:l + 1, :] for l in range(DEPTH) for n in ("ln2_g", "ln2_b")]
        n_masks = 2 + len(LEVELS)
        masks_f32 = bkT[:, :, :].rearrange("p h n -> p (h n)")[:, 0:n_masks * P].rearrange("p (m n) -> p m n", n=P)
        consts = [(masks_f32, w["c_masks"]),
                  (gains[:, 0:1], w["hgrn_norm_g"].rearrange("o d -> d o")),
                  (gains[:, 1:2], w["diff_norm_g"].rearrange("o d -> d o")),
                  (gains[0:HD, 4:5], w["fox_qnorm_g"].rearrange("o d -> d o")),
                  (gains[0:HD, 5:6], w["fox_knorm_g"].rearrange("o d -> d o")),
                  (gains[0:FH, 6:7], w["fox_b_f"].rearrange("o d -> d o")),
                  (gains[HD:P, 4:6], w["c_ones"][HD:P, :]), (gains[0:FH, 2:4], w["c_ones"][0:FH, :]),
                  ]
        consts += [(gains[:, 8 + h:9 + h], w["hgrn_lb_logits"][:, h * P:(h + 1) * P].rearrange("o d -> d o"))
                   for h in range(AH)]
        consts += [(ln_rows[i:i + 1, :], row) for i, row in enumerate(rows)]
        lam_loads = [(spans, w["c_spans"])]
        lam_loads += [(lam_rows[:, i * HD:(i + 1) * HD], w[n][0:1, :].to_broadcast([P, HD]))
                     for i, n in enumerate(("diff_lq1", "diff_lk1", "diff_lq2", "diff_lk2"))]
        N_CONSTS = len(consts)

        block = ctx.enter_context(nc.Block())

        def chunk_at(stage, i=0):
            return stage_chunks[stage][i]

        def hi(c, a, n):
            return w_hi[c % RING][:, a:a + n]

        def lo(c, a, n):
            return w_lo[c % RING][:, a:a + n]

        units = []
        for h in range(AH):
            units += [("diag", h, 0)] + [("level", h, n) for n in range(len(LEVELS))]
            units += [("qdec", h, 0), ("kdec", h, 0), ("kdec2", h, 0)]
            if h:
                units.insert(len(units) - 7, ("value", h - 1, 0))
        units += [("none", 0, 0)] * 3 + [("value", AH - 1, 0)] + [("none", 0, 0)] * 5
        mixed = [(c, p) for s in ("a_i", "b_q", "b_k", "b_v") for c in stage_chunks[s] for p in range(PIECES)]
        even_seq = [("turn", 0, 0)]
        n = 0
        for i, (c, p) in enumerate(mixed):
            even_seq.append(("piece", c, p))
            if i < AH - 1:
                even_seq.append(("turn", i + 1, 0))
            if i == AH - 2:
                even_seq.append(("lead", 0, 0))
            if i >= AH - 2:
                for _ in range(2):
                    if n < len(units):
                        even_seq.append(("unit", n, 0))
                        n += 1
        bv_at = even_seq.index(("piece", stage_chunks["b_v"][1], 0))
        assert even_seq.index(("unit", max(u for u, x in enumerate(units) if x[0] == "kdec") - 1, 0)) < bv_at
        for u in range(n, len(units)):
            even_seq.append(("unit", u, 0))

        D_UNITS = AH * NT
        gate_pieces = [(c, p) for c in stage_chunks["a_g"] for p in range(PIECES)]
        GATE_AT = len(gate_pieces) + 1
        TURN_AT = GATE_AT + 4
        ROOT_LAG = 2

        def fox_pieces(j):
            return [(c, p) for name, i in FOX_PARTS[j] for c in stage_chunks[f"fox{name}{i}"] for p in range(PIECES)]

        fox_slots = [(piece, None) for piece in fox_pieces(0)]
        F_UNITS = 4 * QUARTER
        for j in range(4):
            between = fox_pieces(j + 1)
            places = [n if len(between) == QUARTER else 3 * n // 2 if j < 3 else 2 * n for n in range(len(between))]
            for i in range(QUARTER):
                fox_slots.append((between[places.index(i)] if i in places else None, QUARTER * j + i))
        fox_slots += [(None, F_UNITS + i) for i in range(3)]

        def heads_at(i):
            if not 0 <= i < len(fox_slots) or fox_slots[i][0] is None:
                return None
            c, p = fox_slots[i][0]
            stage = chunks[c][0]
            if stage[3] not in "qk":
                return None
            part, j = "qk".index(stage[3]), int(stage[4])
            return part, j, p, (2 * j + part) * NT + p

        def group_at(i):
            if not 0 <= i < len(fox_slots) or fox_slots[i][0] is None:
                return None
            c, p = fox_slots[i][0]
            stage = chunks[c][0]
            return (stage, p) if stage[3] in "vg" and stage_chunks[stage][1] == c else None

        def nth(kinds, u):
            return sum(1 for k, _, _ in units[:u] if k in kinds)

        MM = ("diag", "level", "kdec", "kdec2")
        EXP = ("level", "qdec", "kdec")
        DEC = ("level", "qdec", "kdec", "kdec2")

        def groups_of(c):
            stage = chunks[c][0]
            i = stage_chunks[stage].index(c)
            if stage in ("a_f", "a_q", "b_q", "b_k"):
                return [(stage, 2 * i), (stage, 2 * i + 1)]
            if i % 2 == 1:
                return [(stage, t) for t in range(NT)]
            return []

        def dec_buf(n):
            return o_even[:, 2 + n % 2, 512:D]

        def targets(ap, b):
            return ap.rearrange("p t (n two b) -> p t n two b", two=2, b=b)[:, :, :, 1, :]

        def lf_buf(h):
            return o_even[:, h, 512:D]

        def exp_buf(n):
            return o_even[:, n % 2, 512:D]

        def halves(ap, b):
            return ap.rearrange("p (n two b) -> p n two b", two=2, b=b)

        def fox_gate(half, t):
            return v_all[:, t, 0:512] if half == 0 else o_fox[:, t, 512:D]

        def silu_buf(j):
            return silu_g[:, j, :]

        def h_buf(j):
            return psum[4 + j % 2]

        @block.tensor
        def _(pe):
            mm = nc.tensor.matmul

            def open_bank(key, bank, reader):
                if last[bank]:
                    who, count = last[bank]
                    pe.wait_ge(freed[who][bank], count)
                read_count[reader][bank] += 1
                bank_count[bank] += 1
                last[bank] = (reader, read_count[reader][bank])
                uses[key] = (bank, bank_count[bank], reader)
                return psum[bank]

            def close_bank(key, ins):
                ins.then_inc(bank_full[uses[key][0]], 1)

            def used_with_bank(c, key):
                chunk_used[c] = (bank_full[uses[key][0]], uses[key][1])

            alone = [0]

            def used_alone(c, ins):
                ins.then_inc(w_used, 1)
                alone[0] += 1
                chunk_used[c] = (w_used, alone[0])

            gid = [0]

            def next_gemm_bank():
                gid[0] += 1
                return (gid[0] - 1) % 4

            def products(acc, l_hi, l_lo, r_hi, r_lo, first, final):
                mm(acc, l_hi, r_lo, start=first, stop=False)
                mm(acc, l_lo, r_hi, start=False, stop=False)
                return mm(acc, l_hi, r_hi, start=False, stop=final)

            def weights_in(c):
                pe.wait_ge(hi_ready, c + 1)
                pe.wait_ge(lo_ready, c + 1)

            def feature_chunk(c, reader):
                stage, _, _ = chunks[c]
                weights_in(c)
                for j, key in enumerate(groups_of(c)):
                    acc = open_bank(key, next_gemm_bank(), reader)
                    for k in range(KD):
                        a = k * 256 + j * P
                        ins = products(acc[:, :], hi(c, a, P), lo(c, a, P), xT_hi[:, k, :], xT_lo[:, k, :],
                                       k == 0, k == KD - 1)
                        if k == KD // 2 - 1:
                            yield
                    close_bank(key, ins)
                    if j == 1:
                        used_with_bank(c, key)
                    yield

            def token_chunk(c, reader, src_hi, src_lo, k_base, first, final, width=512):
                stage, _, size = chunks[c]
                nk = size // width
                weights_in(c)
                for t in range(NT):
                    key = (stage, t) if not isinstance(final, tuple) else (*final, t)
                    if first:
                        open_bank((stage, "acc", t, c), next_gemm_bank(), reader)
                        acc_bank[t] = uses[(stage, "acc", t, c)]
                    acc = psum[acc_bank[t][0]][:, 0:width]
                    for k in range(nk):
                        tok = slice(t * P, (t + 1) * P)
                        ins = products(acc, src_hi[:, k_base + k, tok], src_lo[:, k_base + k, tok],
                                       hi(c, k * width, width), lo(c, k * width, width),
                                       first and k == 0, bool(final) and k == nk - 1)
                    if final:
                        uses[key] = acc_bank[t]
                        close_bank(key, ins)
                    if t == NT - 1:
                        if final:
                            used_with_bank(c, key)
                        else:
                            used_alone(c, ins)
                    yield

            acc_bank = [None] * NT

            def columns(stage, reader, src_hi=xT_hi, src_lo=xT_lo):
                a, b = stage_chunks[stage]
                yield from token_chunk(a, reader, src_hi, src_lo, 0, True, False)
                yield from token_chunk(b, reader, src_hi, src_lo, 4, False, True)

            def drain(pieces):
                for _ in pieces:
                    pass

            def turn_tile(tag, t, src, ready, first_bank, rounds=(0, 1)):
                for r in rounds:
                    if r == rounds[0]:
                        ready()
                    key = (tag, t, r)
                    acc = open_bank(key, first_bank + r - rounds[0], "dve")
                    for j in range(4):
                        f = (4 * r + j) * P
                        ins = nc.tensor.transpose(acc[:, j * P:(j + 1) * P], src[:, t, f:f + P], ident[:, :])
                    close_bank(key, ins)

            def wait_tiles(n):
                pe.wait_ge(T_hi, 2 * n)
                pe.wait_ge(T_lo, 2 * n)

            pe.wait_ge(ident_in, 16)

            for t in range(NT):
                turn_tile("x", t, x_res, lambda: pe.wait_ge(x_in[t], 16), 2 * t)
            turned_tiles = [NT]

            def norm_tail(tag, step, src_tiles, lag, early):
                def turn(t):
                    turn_tile(tag, t, x_res, lambda: pe.wait_ge(S["norm_done"], step * NT + t + 1),
                              (0, 0, 2, 4)[t] if step % 2 else 4 + 2 * (t % 2))

                for t in range(NT):
                    src_tiles(t)
                    if early and t >= lag:
                        turn(t - lag)
                if early:
                    for t in range(NT - lag, NT - 1):
                        turn(t)
                    early(0)
                    turn(NT - 1)
                    early(1)
                    turned_tiles[0] += NT

            def mixer_out(l):
                o = o_even if l == 0 else o_fox
                for t in range(NT):
                    ready = lambda: pe.wait_ge(S["o_ready"], l * NT + t + 1)
                    if l == 0:
                        turn_tile("o0", t, o, ready, 4 + t, (1,))
                    else:
                        turn_tile("o1", t, o, ready, 2 * (t % 2))
                turned_tiles[0] += NT
                wait_tiles(turned_tiles[0])
                a, b, c2, d2 = stage_chunks[f"out{l}"]
                drain(first_out if l == 0 else token_chunk(a, "dve", xT_hi, xT_lo, 0, True, False))
                drain(token_chunk(b, "dve", xT_hi, xT_lo, 4, False, (f"out{l}", 0)))
                tail_products((f"out{l}", 1), [(c2, 0), (d2, 4)], xT_hi, xT_lo, f"n1_{l}", 2 * l, 2,
                              lambda i: up_product(l, i, 0))

            def tail_products(name, parts, src_hi, src_lo, tag, step, lag, early, acc_open=False):
                def tile(t):
                    key = (*name, t)
                    if not acc_open:
                        open_bank((*name, "acc", t), next_gemm_bank(), "dve")
                        acc_bank[t] = uses[(*name, "acc", t)]
                    acc = psum[acc_bank[t][0]][:, :]
                    tok = slice(t * P, (t + 1) * P)
                    for n, (c, k0) in enumerate(parts):
                        if t == 0:
                            weights_in(c)
                        nk = chunks[c][2] // 512
                        for k in range(nk):
                            ins = products(acc, src_hi[:, k0 + k, tok], src_lo[:, k0 + k, tok],
                                           hi(c, k * 512, 512), lo(c, k * 512, 512),
                                           not acc_open and n == 0 and k == 0,
                                           n == len(parts) - 1 and k == nk - 1)
                        if t == NT - 1:
                            if n < len(parts) - 1:
                                used_alone(c, ins)
                            else:
                                uses[key] = acc_bank[t]
                                close_bank(key, ins)
                                used_with_bank(c, key)
                        elif n == len(parts) - 1:
                            uses[key] = acc_bank[t]
                            close_bank(key, ins)

                norm_tail(tag, step, tile, lag, early)

            def up_product(l, j, half):
                c = chunk_at(f"up{l}", j)
                weights_in(c)
                if half == 0:
                    wait_tiles(turned_tiles[0] + NT // 2)
                tok = slice(half * (TS // 2), (half + 1) * (TS // 2))
                for part in range(2):
                    key = (f"up{l}", j, part)
                    if half == 0:
                        open_bank(key, next_gemm_bank(), "act" if part == 0 else "dve")
                    acc = psum[uses[key][0]][:, tok]
                    for k in range(KD):
                        a = part * KD * P + k * P
                        ins = products(acc, hi(c, a, P), lo(c, a, P), xT_hi[:, k, tok], xT_lo[:, k, tok],
                                       k == 0, k == KD - 1)
                    if half == 1:
                        close_bank(key, ins)
                if half == 1:
                    used_with_bank(c, key)

            def swiglu(l):
                wait_tiles(turned_tiles[0])
                for j in range(2):
                    up_product(l, j, 1)
                for j, c in enumerate(stage_chunks[f"up{l}"]):
                    if j < 2:
                        continue
                    weights_in(c)
                    for part in range(2):
                        key = (f"up{l}", j, part)
                        acc = open_bank(key, next_gemm_bank(), "act" if part == 0 else "dve")
                        for k in range(KD):
                            a = part * KD * P + k * P
                            ins = products(acc[:, :], hi(c, a, P), lo(c, a, P), xT_hi[:, k, :],
                                           xT_lo[:, k, :], k == 0, k == KD - 1)
                        close_bank(key, ins)
                    used_with_bank(c, key)
                cs = stage_chunks[f"down{l}"]
                k0 = 0
                for i in range(6):
                    pe.wait_ge(S["h_lo"], l * NF + k0 + chunks[cs[i]][2] // 512)
                    drain(token_chunk(cs[i], "dve", hT_hi, hT_lo, k0, i == 0, (f"down{l}", 0) if i == 5 else False))
                    k0 += chunks[cs[i]][2] // 512
                spread_rows(l)
                k0 = 0
                for i in range(6, 9):
                    drain(token_chunk(cs[i], "dve", hT_hi, hT_lo, k0, i == 6, False))
                    k0 += chunks[cs[i]][2] // 512
                parts = []
                for i in range(9, 12):
                    parts.append((cs[i], k0))
                    k0 += chunks[cs[i]][2] // 512
                tail_products((f"down{l}", 1), parts, hT_hi, hT_lo, f"n2_{l}", 2 * l + 1, 1,
                              fox_start if l == 0 else None, acc_open=True)

            running = {}

            def fox_start(i):
                c = chunk_at("fox_f")
                if i == 0:
                    wait_tiles(turned_tiles[0] + NT // 2)
                    q0, = stage_chunks["foxq0"]
                    running["foxq0"] = token_chunk(q0, "dve", xT_hi, xT_lo, 0, True, True, 256)
                    next(running["foxq0"])
                    next(running["foxq0"])
                    return
                weights_in(c)
                acc = open_bank("fox_f", 6, "dve")
                for half in range(2):
                    if half == 1:
                        wait_tiles(turned_tiles[0] + NT)
                    tok = slice(half * (TS // 2), (half + 1) * (TS // 2))
                    for k in range(KD):
                        ins = products(acc[0:FH, tok], hi(c, k * FH, FH), lo(c, k * FH, FH), xT_hi[:, k, tok],
                                       xT_lo[:, k, tok], k == 0, k == KD - 1)
                close_bank("fox_f", ins)
                used_with_bank(c, "fox_f")

            def spread_rows(l):
                for i in range(4):
                    key = ("rows", l, i)
                    acc = open_bank(key, 4 + i, "dve")
                    row = 2 * l + i // 2
                    sel = ident[0:2 * DEPTH, row:row + 1].to_broadcast([2 * DEPTH, P])
                    close_bank(key, mm(acc[:, :], sel, ln_rows[0:2 * DEPTH, (i % 2) * 512:(i % 2) * 512 + 512],
                                       start=True, stop=True))

            wait_tiles(NT)
            for c in stage_chunks["a_f"] + stage_chunks["a_q"]:
                drain(feature_chunk(c, "act"))

            def turn_ln(h):
                acc = open_bank(("turn", h), 4 + h, "act")
                pe.wait_ge(S["lf_done"], h + 1)
                for t in range(NT):
                    ins = nc.tensor.transpose(acc[:, t * P:(t + 1) * P], lf_buf(h)[:, t * P:(t + 1) * P], ident[:, :])
                close_bank(("turn", h), ins)

            def decay_sums(u):
                if u >= len(units) or units[u][0] not in EXP:
                    return
                kind, h, n = units[u]
                acc = open_bank(("arg", u), 6 + nth(EXP, u) % 2, "act")
                pe.wait_ge(S["lfT_done"], h + 1)
                m = {"level": n, "qdec": len(LEVELS), "kdec": len(LEVELS) + 1}[kind]
                for t in range(NT):
                    ins = mm(acc[:, t * P:(t + 1) * P], lfT[:, h, t * P:(t + 1) * P], spans[:, m, :],
                             start=True, stop=True)
                close_bank(("arg", u), ins)

            def unit_products(u):
                decay_sums(u + 2)
                kind, h, n = units[u]
                if kind in MM:
                    acc = open_bank(("unit", u), 4 + nth((*MM, "value"), u) % 2, "dve")
                if kind == "diag":
                    for t in range(NT):
                        ins = mm(acc[:, t * P:(t + 1) * P], kT[:, h, t * P:(t + 1) * P],
                                 qT[:, h, t * P:(t + 1) * P], start=True, stop=True)
                if kind == "level":
                    pe.wait_ge(S["dec_done"], nth(DEC, u) + 1)
                    d = dec_buf(nth(("level",), u))
                    for t in range(NT):
                        tile = d[:, t * P:(t + 1) * P]
                        ins = mm(halves(acc[:, t * P:(t + 1) * P], LEVELS[n])[:, :, 1, :], tile,
                                 halves(tile, LEVELS[n])[:, :, 1, :], start=True, stop=True)
                if kind == "kdec":
                    pe.wait_ge(S["dec_done"], nth(DEC, u) + 1)
                    for i in range(3):
                        ins = mm(acc[:, i * P:(i + 1) * P], k_dec[:, i * P:(i + 1) * P],
                                 q_dec[:, (i + 1) * P:(i + 2) * P], start=True, stop=True)
                if kind == "kdec2":
                    pe.wait_ge(S["dec_done"], nth(DEC, u) + 1)
                    for i, t in enumerate((2, 3, 3)):
                        ins = mm(acc[:, i * P:(i + 1) * P], k_dec2[:, i, :], q_dec[:, t * P:(t + 1) * P],
                                 start=True, stop=True)
                if kind in MM:
                    close_bank(("unit", u), ins)
                if kind == "value":
                    acc = open_bank(("value", h), 4 + nth((*MM, "value"), u) % 2, "act")
                    pe.wait_ge(S["merge_done"], 10 * (h + 1))
                    pe.wait_ge(S["i_done"], NT)
                    for t in range(NT):
                        for s in range(t + 1):
                            ins = mm(acc[:, t * P:(t + 1) * P], scT[:, h % 2, PAIR[(s, t)], :],
                                     iv[:, s, h * P:(h + 1) * P], start=s == 0, stop=s == t)
                    close_bank(("value", h), ins)

            pieces = {}
            for kind, a, b in even_seq:
                if kind == "unit":
                    unit_products(a)
                    continue
                if kind == "turn":
                    turn_ln(a)
                    continue
                if kind == "lead":
                    pe.wait_ge(consts_in, 16 * N_CONSTS)
                    pe.wait_ge(lam_in, 16 * len(lam_loads))
                    pe.wait_ge(S["q_done"], 1)
                    decay_sums(0)
                    decay_sums(1)
                    continue
                stage = chunks[a][0]
                if stage not in pieces:
                    if stage in ("a_i", "b_v"):
                        pieces[stage] = columns(stage, "act")
                    else:
                        x0, x1 = stage_chunks[stage]
                        pieces[stage] = (y for c in (x0, x1) for y in feature_chunk(c, "act"))
                next(pieces[stage], None)
            for stage in ("a_i", "b_q", "b_k", "b_v"):
                drain(pieces[stage])

            pe.wait_ge(S["bq_done"], 4)
            pe.wait_ge(S["bk_done"], 4)
            pe.wait_ge(S["bv_done"], 4)
            N = D_UNITS
            gen = columns("a_g", "act")
            first_out = token_chunk(chunk_at("out0"), "dve", xT_hi, xT_lo, 0, True, False)
            for s in range(N + 3):
                if s < len(gate_pieces):
                    next(gen)
                if s == GATE_AT - 1:
                    drain(gen)
                wide = GATE_AT <= s < TURN_AT
                if TURN_AT <= s < TURN_AT + 2:
                    for t in (2 * (s - TURN_AT), 2 * (s - TURN_AT) + 1):
                        turn_tile("o0", t, o_even, lambda: pe.wait_ge(S["gated"], t + 1), t, (0,))
                if TURN_AT + 2 <= s < TURN_AT + 2 + NT:
                    t = s - TURN_AT - 2
                    pe.wait_ge(T_hi, 2 * NT + t + 1)
                    pe.wait_ge(T_lo, 2 * NT + t + 1)
                    next(first_out)
                if s < N:
                    h, i = s // NT, s % NT
                    for m in range(2):
                        key = ("score", s, m)
                        acc = open_bank(key, (0 if wide and s % 2 else 4) + m, "act")
                        n = (i + 1) * P
                        rows = slice(m * HD, (m + 1) * HD)
                        mm(acc[:, 0:n], bqT[rows, h, i * P:(i + 1) * P], bkT[rows, h, 0:n], start=True, stop=False)
                        close_bank(key, mm(acc[:, n - P:n], ident_bf[:, :], diff_mask[:, :], start=False, stop=True))
                if 2 <= s < N + 2:
                    u = s - 2
                    i = u % NT
                    pe.wait_ge(S["mix_done"], u + 1)
                    acc = open_bank(("pT", u), 2 if wide and u % 2 else 6, "act")
                    for j in range(i + 1):
                        ins = nc.tensor.transpose(acc[:, j * P:(j + 1) * P], p_map[:, u % 3, 0, j * P:(j + 1) * P],
                                                  ident[:, :])
                    close_bank(("pT", u), ins)
                if s >= 3:
                    u = s - 3
                    h, i = u // NT, u % NT
                    pe.wait_ge(S["pT_done"], u + 1)
                    acc = open_bank(("diff", u), 3 if wide and u % 2 else 7, "dve")
                    for j in range(i + 1):
                        ins = mm(acc[:, 0:P], pT_diff[:, u % 2, j * P:(j + 1) * P], bv[:, j, h * P:(h + 1) * P],
                                 start=j == 0, stop=j == i)
                    close_bank(("diff", u), ins)

            mixer_out(0)
            swiglu(0)

            def turn_heads(part, j, t, n):
                pe.wait_ge(S["qn_done"], n + 1)
                key = ("heads", n)
                acc = open_bank(key, 7, "act")
                for i in range(4):
                    ins = nc.tensor.transpose(acc[0:HA, i * P:(i + 1) * P], qn[:, n % 2, i, :], ident[:, :])
                close_bank(key, ins)

            def gates():
                acc = open_bank("cum", 6, "dve")
                pe.wait_ge(S["logf_done"], 1)
                for t in range(NT):
                    ins = nc.tensor.transpose(acc[:, t * FH:(t + 1) * FH], gate_T[0:FH, 0, t * P:(t + 1) * P],
                                              ident[0:FH, 0:FH])
                close_bank("cum", ins)

            for i, (piece, s) in enumerate(fox_slots):
                if piece and i >= 2:
                    stage = chunks[piece[0]][0]
                    if stage not in running:
                        if stage[3] in "qk":
                            running[stage] = token_chunk(piece[0], "dve", xT_hi, xT_lo, 0, True, True, 256)
                        else:
                            running[stage] = columns(stage, "act")
                    next(running[stage])
                if i == 3:
                    gates()
                if heads_at(i - 3):
                    turn_heads(*heads_at(i - 3))
                if s is None:
                    continue
                if s < F_UNITS:
                    h, i = s // NT, s % NT
                    n = (i + 1) * P
                    j = s // QUARTER
                    if s % QUARTER == 0:
                        pe.wait_ge(S["qA_done"], 2 * NT * (j + 1))
                        pe.wait_ge(S["v_done"], NT * (j // 2 + 1))
                    acc = open_bank(("fs", s), 7 if s > 3 * QUARTER and s % 2 else 4, "act")
                    mm(acc[:, 0:n], qA[0:HA, j % 2, h % 4, i * P:(i + 1) * P], kA[0:HA, j % 2, h % 4, 0:n],
                       start=True, stop=False)
                    close_bank(("fs", s), mm(acc[:, n - P:n], ident_bf[:, :], fox_mask[:, :], start=False, stop=True))
                if 2 <= s < F_UNITS + 2:
                    u = s - 2
                    i = u % NT
                    pe.wait_ge(S["fexp"], u + 1)
                    acc = open_bank(("fT", u), 5, "act")
                    for j in range(i + 1):
                        ins = nc.tensor.transpose(acc[:, j * P:(j + 1) * P], p_fox[:, u % 3, j * P:(j + 1) * P],
                                                  ident[:, :])
                    close_bank(("fT", u), ins)
                if s >= 3:
                    u = s - 3
                    h, i = u // NT, u % NT
                    pe.wait_ge(S["fpT"], u + 1)
                    acc = open_bank(("fv", u), 6, "dve")
                    for j in range(i + 1):
                        ins = mm(acc[:, 0:HD], pT_fox[:, u % 2, j * P:(j + 1) * P], v_all[:, j, h * HD:(h + 1) * HD],
                                 start=j == 0, stop=j == i)
                    close_bank(("fv", u), ins)
            for gen in running.values():
                drain(gen)
            mixer_out(1)
            swiglu(1)

        @block.sync
        def _(sp):
            def load(c):
                if c >= RAW:
                    sp.wait_ge(lo_ready, c - RAW + 1)
                for off, src, a, b in chunks[c][1]:
                    dst = w_raw[c % RAW][:, off:off + a * b].rearrange("p (a b) -> p a b", a=a)
                    sp.dma_start(dst, src).then_inc(w_loaded[c % RAW], 16)

            sp.dma_start(ident[:, :], w["c_ident"]).then_inc(ident_in, 16)
            x = w["x"][0].rearrange("(t p) d -> p t d", p=P)
            for t in range(NT):
                sp.dma_start(x_res[:, t, :], x[:, t, :]).then_inc(x_in[t], 16)
                if t == 0:
                    load(0)
            load(1)
            for dst, src in consts:
                sp.dma_start(dst, src).then_inc(consts_in, 16)
            for dst, src in lam_loads:
                sp.dma_start(dst, src).then_inc(lam_in, 16)
            for c in range(2, len(chunks)):
                for l in range(DEPTH):
                    if c == chunk_at(f"out{l}"):
                        if l == 0:
                            sp.wait_ge(S["act_free"], 1)
                        else:
                            sp.wait_ge(S["fexp"], 3 * QUARTER)
                        for i, name in enumerate(("ln1_g", "ln1_b")):
                            sp.dma_start(mixer_rows[l][:, i, :], w[name][l:l + 1, :].to_broadcast([P, D])
                                         ).then_inc(rows_in[l], 16)
                load(c)
            o = out[0].rearrange("(t p) d -> p t d", p=P)
            for t in range(NT):
                sp.wait_ge(S["norm_done"], 3 * NT + t + 1)
                sp.dma_start(o[:, t, :], x_res[:, t, :]).then_inc(out_done, 16)
            sp.wait_ge(out_done, 16 * NT)

        @block.gpsimd
        def _(pool):
            for c, (_, _, size) in enumerate(chunks):
                pool.wait_ge(hi_ready, c + 1)
                if c >= RING:
                    pool.wait_ge(*chunk_used[c - RING])
                for a in range(0, size, 1024):
                    n = min(1024, size - a)
                    ins = nc.gpsimd.tensor_tensor(w_lo[c % RING][:, a:a + n], w_raw[c % RAW][:, a:a + n],
                                                  w_hi[c % RING][:, a:a + n].bitcast(F32), ALU.subtract)
                ins.then_inc(lo_ready, 1)

        def reader_of(eng, counts):
            def full(key):
                bank, n, _ = uses[key]
                eng.wait_ge(bank_full[bank], n)
                return psum[bank]

            def chain(ins, s):
                ins.then_inc(s, 1)
                counts[id(s)] = counts.get(id(s), 0) + 1
                eng.wait_ge(s, counts[id(s)])

            return full, chain

        @block.scalar
        def _(act):
            counts = {}
            full, chain = reader_of(act, counts)
            step = lambda ins: chain(ins, act_step)
            release = lambda ins, key: chain(ins, freed["act"][uses[key][0]])
            fn = nc.scalar.activation
            rounded = [0]
            loaded = {0: 0, 1: 0}
            need = []
            for c, (_, loads, _) in enumerate(chunks):
                loaded[c % RAW] += 16 * len(loads)
                need.append(loaded[c % RAW])

            def hi_upto(n):
                while rounded[0] < min(n, len(chunks)):
                    c = rounded[0]
                    act.wait_ge(w_loaded[c % RAW], need[c])
                    if c >= RING:
                        act.wait_ge(*chunk_used[c - RING])
                    size = chunks[c][2]
                    chain(fn(w_hi[c % RING][:, 0:size], w_raw[c % RAW][:, 0:size], ACT.Copy), hi_ready)
                    rounded[0] += 1

            def split_hi(tag, t, rounds=(0, 1)):
                for r in rounds:
                    acc = full((tag, t, r))
                    dst = xT_hi[:, 4 * r:4 * r + 4, t * P:(t + 1) * P]
                    src = acc[:, :].rearrange("p (k n) -> p k n", k=4)
                    if tag == "o0":
                        chain(fn(dst, src, ACT.Copy, scale=gains[:, r:r + 1]), T_hi)
                    else:
                        chain(fn(dst, src, ACT.Copy), T_hi)

            def root(dst, src, arg_sem, n, done):
                act.wait_ge(arg_sem, n)
                step(fn(dst, src, ACT.Ln))
                chain(fn(dst, dst, ACT.Exp, scale=-0.5), done)

            def evac(key, dst, src_fn, func=ACT.Copy):
                acc = full(key)
                release(fn(dst, src_fn(acc), func), key)

            whole = lambda acc: acc[:, :]

            hi_upto(1)
            for t in range(NT):
                split_hi("x", t)
            hi_upto(3)
            act.wait_ge(S["lam_arg"], 1)
            chain(fn(small[:, 0:2], small[:, 0:2], ACT.Exp), S["lam_exp"])
            chain(fn(small[:, 16:20], small[:, 16:20], ACT.Exp), S["lam_exp"])
            def projected(stage, dst, func):
                for h in range(AH):
                    hi_upto(stage_chunks[stage][h // 2] + 3)
                    evac((stage, h), dst[:, h, :], whole, func)

            projected("a_f", kT, ACT.Sigmoid)
            act.sem_inc(S["sig_done"], 1)
            nc.scalar.preload_act_table_set("natural_log")
            for h in range(AH):
                act.wait_ge(S["ln_arg"], h + 1)
                step(fn(q_dec[:, :], q_dec[:, :], ACT.Ln))
                chain(fn(k_dec[:, :], k_dec[:, :], ACT.Ln), S["ln_done"])
                if h == 1:
                    hi_upto(stage_chunks["a_q"][0] + 3)
            projected("a_q", qT, ACT.Silu)
            act.sem_inc(S["q_done"], 1)
            nc.scalar.preload_act_table_set(LN_EXP)

            def decay(u):
                if u >= len(units) or units[u][0] not in EXP:
                    return
                acc = full(("arg", u))
                x = nth(EXP, u)
                if x >= 2:
                    act.wait_ge(S["dec_done"], nth(DEC, u) - 1)
                release(fn(exp_buf(x), acc[:, :], ACT.Exp), ("arg", u))
                act.sem_inc(S["e_done"], 1)

            def unit_act(u):
                if u >= 5 and units[u - 5][0] == "value":
                    h = units[u - 5][1]
                    root(stats[:, :, 8 + h], stats[:, :, 4 + h], S["var_ready"], h + 1, S["root_ready"])
                decay(u + 1)
                kind, h, n = units[u]
                if kind == "value":
                    acc = full(("value", h))
                    release(fn(o_even[:, :, h * P:(h + 1) * P], acc[:, :].rearrange("p (t n) -> p t n", t=NT),
                               ACT.Copy), ("value", h))
                    for t in range(NT):
                        chain(fn(junk[:, :], o_even[:, t, h * P:(h + 1) * P], ACT.Square,
                                 accum_out=stats[:, t, h:h + 1]), S["ms_done"] if t == NT - 1 else act_step)

            due = []
            for kind, a, b in even_seq:
                if kind == "unit":
                    unit_act(a)
                    continue
                if kind == "turn":
                    evac(("turn", a), lfT[:, a, :], whole)
                    act.sem_inc(S["lfT_done"], 1)
                    continue
                if kind == "lead":
                    decay(0)
                    continue
                for key in due:
                    dst = {"a_i": iv, "b_v": bv, "b_q": bqT, "b_k": bkT}[key[0]]
                    if key[0] == "b_v" and key[1] == 0:
                        act.wait_ge(S["lam_arg"], 1)
                    release(fn(dst[:, key[1], :], full(key), ACT.Copy, scale=HD ** -0.5 if key[0] == "b_q" else 1.0), key)
                    act.sem_inc(S[{"a_i": "i_done", "b_v": "bv_done", "b_q": "bq_done", "b_k": "bk_done"}[key[0]]], 1)
                due = []
                hi_upto(a + 2 if b < 2 else a + 3) if b == 1 or b == 3 else None
                g = groups_of(a)
                if len(g) == 2:
                    due = [g[0]] if b == 1 else [g[1]] if b == 3 else []
                elif g:
                    due = [g[b]]
            for key in due:
                evac(key, bv[:, key[1], :], whole)
                act.sem_inc(S["bv_done"], 1)

            N = D_UNITS
            for s in range(N + 4 + ROOT_LAG):
                if 4 <= s < N + 4:
                    u = s - 4
                    acc = full(("diff", u))
                    chain(fn(junk[:, :], acc[:, 0:P], ACT.Square, scale=stats[:, u % NT, 13:14],
                             accum_out=stats[:, u % NT, u // NT:u // NT + 1]), S["ms_done"])
                u = s - 4 - ROOT_LAG + 1
                if u >= 0 and u % NT == NT - 1:
                    h = u // NT
                    root(stats[:, :, 8 + h], stats[:, :, 4 + h], S["var_ready"], AH + h + 1, S["root_ready"])
                if TURN_AT + 1 <= s < TURN_AT + 3:
                    for t in (2 * (s - TURN_AT - 1), 2 * (s - TURN_AT - 1) + 1):
                        split_hi("o0", t, (0,))
                if s == GATE_AT:
                    for t in range(NT):
                        evac(("a_g", t), a_gate[:, t, :], whole, ACT.Silu)
                    act.sem_inc(S["gate_done"], 1)
                    nc.scalar.preload_act_table_set(LN_EXP)
                if s in (1, 5, 9):
                    hi_upto(stage_chunks["a_g"][0] + 2 + s // 4)
                if s < N:
                    i = s % NT
                    n = (i + 1) * P
                    if s == 0:
                        act.wait_ge(S["act_free"], 1)
                    if s >= 2:
                        act.wait_ge(S["mix_done"], s - 1)
                    if s >= 3:
                        bank, cnt, _ = uses[("pT", s - 3)]
                        act.wait_ge(bank_full[bank], cnt)
                    for m in range(2):
                        act.wait_ge(S["max_done"], s + 1)
                        key = ("score", s, m)
                        acc = full(key)
                        c = 24 + 4 * (s % 2) + m
                        ins = fn(p_map[:, s % 3, m, 0:n], acc[:, 0:n], ACT.Exp, bias=small[:, c:c + 1],
                                 accum_out=small[:, c + 2:c + 3])
                        release(ins, key)
                    act.sem_inc(S["exp_done"], 1)
                if 2 <= s < N + 2:
                    u = s - 2
                    n = (u % NT + 1) * P
                    acc = full(("pT", u))
                    if u >= 2:
                        bank, cnt, _ = uses[("diff", u - 2)]
                        act.wait_ge(bank_full[bank], cnt)
                    release(fn(pT_diff[:, u % 2, 0:n], acc[:, 0:n], ACT.Copy), ("pT", u))
                    act.sem_inc(S["pT_done"], 1)

            def mixer_tail(l):
                for t in range(NT):
                    split_hi(f"o{l}", t, (1,) if l == 0 else (0, 1))
                hi_upto(stage_chunks[f"out{l}"][0] + 3)
                hi_upto(stage_chunks[f"out{l}"][2] + 2)
                hi_upto(stage_chunks[f"up{l}"][0] + 1)
                norm_act(f"n1_{l}", 2 * l, stage_chunks[f"up{l}"][0], 2)

            def norm_act(tag, step_n, after, lag=1):
                nc.scalar.preload_act_table_set(LN_EXP)
                for t in range(NT):
                    root(stats[:, t, 14:15], stats[:, t, 13:14], S["ln_arg"], AH + step_n * NT + t + 1, S["ln_done"])
                    if t == NT - 2 and lag == 2:
                        hi_upto(after + 2)
                    if t >= 1 and tag != "n2_1":
                        split_hi(tag, t - 1)
                    if t == NT - 2 and lag == 1:
                        hi_upto(after + 2)
                if tag != "n2_1":
                    split_hi(tag, NT - 1)
                hi_upto(after + 3)

            def swiglu_act(l):
                for j, c in enumerate(stage_chunks[f"up{l}"]):
                    hi_upto(c + 2)
                    acc = full((f"up{l}", j, 0))
                    release(fn(silu_buf(j), acc[:, :], ACT.Silu), (f"up{l}", j, 0))
                    act.sem_inc(S["silu_done"], 1)
                    hi_upto(c + 3)
                    if j >= 1:
                        act.wait_ge(S["h_mul"], l * NF + j)
                        chain(fn(hT_hi[:, j - 1, :], h_buf(j - 1), ACT.Copy), S["h_hi"])
                act.wait_ge(S["h_mul"], l * NF + NF)
                chain(fn(hT_hi[:, NF - 1, :], h_buf(NF - 1), ACT.Copy), S["h_hi"])
                cs = stage_chunks[f"down{l}"]
                hi_upto(cs[-1] + 1)
                norm_act(f"n2_{l}", 2 * l + 1, cs[-1] + 1)

            mixer_tail(0)
            swiglu_act(0)

            def fox_gates(half):
                for t in range(NT):
                    evac((f"foxg{half}", t), fox_gate(half, t), whole, ACT.Sigmoid)
                    act.sem_inc(S["g_done"], 1)

            for i, (piece, s) in enumerate(fox_slots):
                if i == 0:
                    continue
                if i == 2:
                    act.wait_ge(S["f_arg"], 1)
                    step(fn(gate_T[0:FH, 1, :], gate_T[0:FH, 1, :], ACT.Exp))
                    nc.scalar.preload_act_table_set("natural_log")
                    chain(fn(gate_T[0:FH, 1, :], gate_T[0:FH, 1, :], ACT.Ln, bias=gains[0:FH, 2:3]), S["f_ln"])
                    nc.scalar.preload_act_table_set(LN_EXP)
                if piece and piece[1] == 1:
                    hi_upto(piece[0] + 3)
                if group_at(i - 1):
                    stage, t = group_at(i - 1)
                    if stage[3] == "v":
                        half = int(stage[4])
                        evac((stage, t), v_all[:, t, 512 * half:512 * half + 512], whole)
                        act.sem_inc(S["v_done"], 1)
                    elif t == NT - 1 and stage == "foxg1":
                        fox_gates(1)
                        nc.scalar.preload_act_table_set(LN_EXP)
                if heads_at(i - 1):
                    part, j, t, n = heads_at(i - 1)
                    acc = full((f"fox{'qk'[part]}{j}", t))
                    if n >= 2:
                        act.wait_ge(S["qvar"], n - 1)
                    chain(fn(sq[:, n % 2, :], acc[:, 0:256], ACT.Square), S["sq_done"])
                    root(fox_ms[:, n % 2, 1, :], fox_ms[:, n % 2, 0, :], S["qvar"], n + 1, S["qroot"])
                if s is not None and s < F_UNITS:
                    n = (s % NT + 1) * P
                    act.wait_ge(S["fmax"], s + 1)
                    if s >= 3:
                        full(("fT", s - 3))
                    if s >= 4:
                        act.wait_ge(S["ffin"], s - 3)
                    key = ("fs", s)
                    ins = fn(p_fox[:, s % 3, 0:n], full(key)[:, 0:n], ACT.Exp, bias=small[:, 32 + s % 4:33 + s % 4],
                             accum_out=small[:, 36 + s % 4:37 + s % 4])
                    release(ins, key)
                    act.sem_inc(S["fexp"], 1)
                if s is not None and 2 <= s < F_UNITS + 2:
                    u = s - 2
                    n = (u % NT + 1) * P
                    key = ("fT", u)
                    acc = full(key)
                    if u >= 2:
                        full(("fv", u - 2))
                    release(fn(pT_fox[:, u % 2, 0:n], acc[:, 0:n], ACT.Copy), key)
                    act.sem_inc(S["fpT"], 1)
                if s == F_UNITS:
                    nc.scalar.preload_act_table_set("sigmoid_and_others")
                if heads_at(i - 3):
                    part, j, t, n = heads_at(i - 3)
                    acc = full(("heads", n))
                    dst = (qA, kA)[part][0:HA, j % 2, :, t * P:(t + 1) * P]
                    src = acc[0:HA, :].rearrange("p (k n) -> p k n", k=4)
                    release(fn(dst, src, ACT.Copy, scale=gains[0:HA, 4 + part:5 + part]), ("heads", n))
                    act.sem_inc(S["qA_done"], 1)
            fox_gates(0)
            hi_upto(stage_chunks["out1"][0] + 2)
            mixer_tail(1)
            swiglu_act(1)

        @block.vector
        def _(dve):
            counts = {}
            full, chain = reader_of(dve, counts)
            step = lambda ins: chain(ins, dve_step)
            release = lambda ins, key: chain(ins, freed["dve"][uses[key][0]])
            v = nc.vector
            tt, ts, stt = v.tensor_tensor, v.tensor_scalar, v.scalar_tensor_tensor
            split = [0]

            def split_lo(tag, t, rounds=(0, 1)):
                for r in rounds:
                    split[0] += 1
                    acc = full((tag, t, r))
                    dve.wait_ge(T_hi, split[0])
                    tok = slice(t * P, (t + 1) * P)
                    dst = xT_lo[:, 4 * r:4 * r + 4, tok]
                    high = xT_hi[:, 4 * r:4 * r + 4, tok].bitcast(F32)
                    src = acc[:, :].rearrange("p (k n) -> p k n", k=4)
                    if tag == "o0":
                        ins = stt(dst, src, gains[:, r:r + 1], high, ALU.mult, ALU.subtract)
                    else:
                        ins = tt(dst, src, high, ALU.subtract)
                    release(ins, (tag, t, r))
                    dve.sem_inc(T_lo, 1)

            def free_now(key):
                s = freed["dve"][uses[key][0]]
                counts[id(s)] = counts.get(id(s), 0) + 1
                dve.sem_inc(s, 1)

            def refine(r, var, tmp):
                step(tt(tmp, r, r, ALU.mult))
                step(tt(tmp, tmp, var, ALU.mult))
                step(ts(tmp, tmp, -0.5, 1.5, ALU.mult, ALU.add))
                step(tt(r, r, tmp, ALU.mult))

            for t in range(NT):
                split_lo("x", t)
            dve.wait_ge(ident_in, 16)
            dve.wait_ge(consts_in, 16 * N_CONSTS)
            dve.wait_ge(lam_in, 16 * len(lam_loads))
            step(v.tensor_copy(ident_bf[:, :], ident[:, :]))
            step(v.tensor_copy(fox_mask[:, :], masks_f32[:, 0, :]))
            step(v.tensor_copy(diff_mask[:, :], masks_f32[:, 1, :]))
            step(v.tensor_copy(level_mask[:, :, :], masks_f32[:, 2:n_masks, :]))
            lam4 = lam_rows.rearrange("p (a b) -> p a b", a=4)
            for m in range(2):
                dots = bv[:, 3, (4 + m) * HD:(5 + m) * HD]
                step(tt(dots, lam4[:, 2 * m, :], lam4[:, 2 * m + 1, :], ALU.mult))
                step(v.tensor_reduce(small[:, m:m + 1], dots, AX_X, ALU.add))
            lg = gains[:, 8:12]
            step(tt(small[:, 16:20], lg, lg, ALU.subtract))
            step(ts(gains[:, 1:2], gains[:, 1:2], 1.0 - LAM_INIT, None, ALU.mult))
            step(ts(gains[0:HD, 4:5], gains[0:HD, 4:5], HD ** -0.5, None, ALU.mult))
            dve.sem_inc(S["lam_arg"], 1)

            dve.wait_ge(S["lam_exp"], 2)
            step(tt(small[:, 2:3], small[:, 1:2], small[:, 0:1], ALU.subtract))
            step(ts(small[:, 2:3], small[:, 2:3], -LAM_INIT, None, ALU.add))
            step(v.reciprocal(small[:, 20:24], small[:, 16:20]))
            step(tt(small[:, 16:20], small[:, 16:20], small[:, 20:24], ALU.mult))
            step(tt(small[:, 8:12], small[:, 16:20], small[:, 16:20], ALU.subtract))
            step(ts(small[:, 12:16], small[:, 8:12], -1.0, 1.0, ALU.mult, ALU.add))
            dve.wait_ge(S["sig_done"], 1)
            for h in range(AH):
                k = kT[:, h, :]
                step(ts(k, k, small[:, 12 + h:13 + h], small[:, 8 + h:9 + h], ALU.mult, ALU.add))
                step(ts(q_dec[:, :], k, TINY, None, ALU.max))
                step(ts(k_dec[:, :], k, 1.0 / TINY, 1.0, ALU.mult, ALU.min))
                chain(ts(k, k, -1.0, 1.0, ALU.mult, ALU.add), S["ln_arg"])
                dve.wait_ge(S["ln_done"], h + 1)
                chain(tt(lf_buf(h), q_dec[:, :], k_dec[:, :], ALU.add), S["lf_done"])
            dve.wait_ge(S["q_done"], 1)

            def after(u):
                kind, h, n = units[u]
                if kind in EXP:
                    dve.wait_ge(S["e_done"], nth(EXP, u) + 1)
                    buf = exp_buf(nth(EXP, u))
                if kind == "level":
                    m = nth(("level",), u)
                    if m >= 2:
                        prev = [x for x in range(u) if units[x][0] == "level"][-2]
                        bank, cnt, _ = uses[("unit", prev)]
                        dve.wait_ge(bank_full[bank], cnt)
                    z = LEVELS[n]
                    d, ee = halves(dec_buf(m), z), halves(buf, z)
                    qq, kk = halves(qT[:, h, :], z), halves(kT[:, h, :], z)
                    step(tt(d[:, :, 1, :], qq[:, :, 1, :], ee[:, :, 1, :], ALU.mult))
                    chain(tt(d[:, :, 0, :], kk[:, :, 0, :], ee[:, :, 0, :], ALU.mult), S["dec_done"])
                if kind in ("qdec", "kdec") and h:
                    prev = [x for x in range(u) if units[x][0] == "kdec2"][-1]
                    bank, cnt, _ = uses[("unit", prev)]
                    dve.wait_ge(bank_full[bank], cnt)
                if kind == "qdec":
                    step(v.tensor_copy(small[:, 3:7], buf.rearrange("p (t n) -> p t n", t=NT)[:, :, P - 1]))
                    chain(tt(q_dec[:, :], qT[:, h, :], buf, ALU.mult), S["dec_done"])
                if kind == "kdec":
                    chain(tt(k_dec[:, :], kT[:, h, :], buf, ALU.mult), S["dec_done"])
                if kind == "kdec2":
                    step(ts(k_dec2[:, 0, :], k_dec[:, 0:P], small[:, 4:5], None, ALU.mult))
                    step(ts(k_dec2[:, 1, :], k_dec[:, P:2 * P], small[:, 5:6], None, ALU.mult))
                    chain(ts(k_dec2[:, 2, :], k_dec2[:, 0, :], small[:, 5:6], None, ALU.mult), S["dec_done"])

            def merge(u):
                kind, h, n = units[u]
                if kind in MM:
                    acc = full(("unit", u))
                    dst = scT[:, h % 2, 0:4, :]
                    src = acc[:, :].rearrange("p (t n) -> p t n", t=NT)
                    if kind == "diag":
                        if h >= 2:
                            bank, cnt, _ = uses[("value", h - 2)]
                            dve.wait_ge(bank_full[bank], cnt)
                        ins = tt(dst, src, ident[:, None, :].to_broadcast([P, NT, P]), ALU.mult)
                    elif kind == "level":
                        z = LEVELS[n]
                        mask = level_mask[:, n:n + 1, :].bitcast(U16).to_broadcast([P, NT, P])
                        ins = v.copy_predicated(targets(dst, z), targets(mask, z), targets(src, z))
                    else:
                        o = 4 if kind == "kdec" else 7
                        ins = v.tensor_copy(scT[:, h % 2, o:o + 3, :], src[:, 0:3, :])
                    release(ins, ("unit", u))
                    dve.sem_inc(S["merge_done"], 1)
                if kind == "value":
                    norm_var(h, 0)

            def norm_var(h, part):
                dve.wait_ge(S["ms_done"], h + 1 if part == 0 else AH + NT * (h + 1))
                chain(ts(stats[:, :, 4 + h], stats[:, :, h], 1.0 / P, 1e-6, ALU.mult, ALU.add), S["var_ready"])

            def norm_head(h, part):
                dve.wait_ge(S["root_ready"], part * AH + h + 1)
                r = stats[:, :, 8 + h]
                refine(r, stats[:, :, 4 + h], stats[:, :, 12])
                for t in range(NT):
                    o = o_even[:, t, part * 512 + h * P:part * 512 + (h + 1) * P]
                    step(ts(o, o, r[:, t:t + 1], None, ALU.mult))

            U = len(units)
            for u in range(U + 3):
                if 0 <= u - 3 < U:
                    merge(u - 3)
                if u >= 6 and units[u - 6][0] == "value":
                    norm_head(units[u - 6][1], 0)
                if 0 <= u - 1 < U:
                    after(u - 1)
            dve.sem_inc(S["act_free"], 1)

            N = D_UNITS
            for s in range(N + 4 + ROOT_LAG):
                if TURN_AT + 1 <= s < TURN_AT + 3:
                    for t in (2 * (s - TURN_AT - 1), 2 * (s - TURN_AT - 1) + 1):
                        split_lo("o0", t, (0,))
                u = s - 4
                if 0 <= u < N:
                    h, i = u // NT, u % NT
                    dve.wait_ge(S["ms_done"], AH + u + 1)
                    key = ("diff", u)
                    o = o_even[:, i, 512 + h * P:512 + (h + 1) * P]
                    release(ts(o, full(key)[:, 0:P], stats[:, i, 13:14], None, ALU.mult), key)
                    if i == NT - 1:
                        norm_var(h, 1)
                if s < N:
                    n = (s % NT + 1) * P
                    if s >= 2:
                        dve.wait_ge(S["exp_done"], s - 1)
                    for m in range(2):
                        full(("score", s, m))
                    c, b = 24 + 4 * (s % 2), uses[("score", s, 0)][0]
                    chain(v.tensor_reduce(small[:, c:c + 2], banks[:, b:b + 2, 0:n], AX_X, ALU.max, negate=True),
                          S["max_done"])
                if 1 <= s <= N:
                    u = s - 1
                    n = (u % NT + 1) * P
                    c = 26 + 4 * (u % 2)
                    dve.wait_ge(S["exp_done"], u + 1)
                    inv, part = stats[:, u % NT, 13:15], stats[:, u % NT, 15:16]
                    step(v.reciprocal(inv, small[:, c:c + 2]))
                    step(stt(part, inv[:, 1:2], small[:, 2:3], small[:, c:c + 1], ALU.mult, ALU.mult))
                    a, b = p_map[:, u % 3, 0, 0:n], p_map[:, u % 3, 1, 0:n]
                    chain(stt(a, b, part, a, ALU.mult, ALU.add), S["mix_done"])
                u = s - 4 - ROOT_LAG
                if u >= 0 and u % NT == NT - 1:
                    norm_head(u // NT, 1)
                if GATE_AT + 1 <= s <= GATE_AT + NT:
                    t = s - GATE_AT - 1
                    dve.wait_ge(S["gate_done"], 1)
                    chain(tt(o_even[:, t, 0:512], o_even[:, t, 0:512], a_gate[:, t, :], ALU.mult), S["gated"])
            dve.sem_inc(S["o_ready"], NT)

            def add_left(key, t, half):
                xs = x_res[:, t, half * 512:(half + 1) * 512]
                release(stt(xs, xs, ALPHA, full(key)[:, :], ALU.mult, ALU.add), key)
                step(v.bn_stats(stats[:, t, 6 * half:6 * half + 6], xs))

            def norm(tag, name, n):
                for t in range(NT):
                    add_left((*name, 1, t), t, 1)
                    st = stats[:, t, :]
                    step(v.bn_aggr(st[:, 12:14], st[:, 0:12]))
                    chain(ts(st[:, 13:14], st[:, 13:14], 1e-5, None, ALU.add), S["ln_arg"])
                    dve.wait_ge(S["ln_done"], AH + n * NT + t + 1)
                    r, tmp = st[:, 14:15], st[:, 15:16]
                    step(stt(tmp, r, r, st[:, 13:14], ALU.mult, ALU.mult))
                    step(ts(tmp, tmp, -0.5, 1.5, ALU.mult, ALU.add))
                    step(tt(r, r, tmp, ALU.mult))
                    if n % 2:
                        for i in range(4):
                            full(("rows", n // 2, i))
                        gain, bias = banks[:, 4:6, :], banks[:, 6:8, :]
                    else:
                        dve.wait_ge(rows_in[n // 2], 32)
                        gain, bias = (mixer_rows[n // 2][:, i, :].rearrange("p (a b) -> p a b", a=2) for i in range(2))
                    xs = x_res[:, t, :].rearrange("p (a b) -> p a b", a=2)
                    step(stt(xs, xs, st[:, 12:13], gain, ALU.subtract, ALU.mult))
                    chain(stt(xs, xs, r, bias, ALU.mult, ALU.add), S["norm_done"])
                    if t == NT - 1 and n % 2:
                        for i in range(4):
                            free_now(("rows", n // 2, i))
                    if t >= 1 and tag != "n2_1":
                        split_lo(tag, t - 1)
                if tag != "n2_1":
                    split_lo(tag, NT - 1)

            def mixer_tail(l):
                for t in range(NT):
                    split_lo(f"o{l}", t, (1,) if l == 0 else (0, 1))
                for t in range(NT):
                    add_left((f"out{l}", 0, t), t, 0)
                norm(f"n1_{l}", (f"out{l}",), 2 * l)

            def swiglu_dve(l):
                for j in range(NF):
                    dve.wait_ge(S["silu_done"], l * NF + j + 1)
                    if j >= 2:
                        dve.wait_ge(S["h_hi"], l * NF + j - 1)
                    acc = full((f"up{l}", j, 1))
                    release(tt(h_buf(j), silu_buf(j), acc[:, :], ALU.mult), (f"up{l}", j, 1))
                    dve.sem_inc(S["h_mul"], 1)
                    if j >= 1:
                        lo_h(l, j - 1)
                lo_h(l, NF - 1)
                for t in range(NT):
                    add_left((f"down{l}", 0, t), t, 0)
                norm(f"n2_{l}", (f"down{l}",), 2 * l + 1)

            def lo_h(l, j):
                dve.wait_ge(S["h_hi"], l * NF + j + 1)
                chain(tt(hT_lo[:, j, :], h_buf(j), hT_hi[:, j, :].bitcast(F32), ALU.subtract), S["h_lo"])

            mixer_tail(0)
            swiglu_dve(0)

            step(v.memset(qn[:, :, :, HD:HA], 1.0))

            def square_sums(part, j, t, n):
                dve.wait_ge(S["sq_done"], n + 1)
                m = fox_ms[:, n % 2, :, :]
                step(v.tensor_reduce(m[:, 0, :], sq[:, n % 2, :].rearrange("p (h d) -> p h d", h=4), AX_X, ALU.add))
                chain(ts(m[:, 0, :], m[:, 0, :], 1.0 / HD, 1e-6, ALU.mult, ALU.add), S["qvar"])

            def fox_heads(part, j, t, n):
                key = (f"fox{'qk'[part]}{j}", t)
                m = fox_ms[:, n % 2, :, :]
                dve.wait_ge(S["qroot"], n + 1)
                refine(m[:, 1, :], m[:, 0, :], m[:, 2, :])
                if n >= 2:
                    full(("heads", n - 2))
                q = qn[:, n % 2, :, :]
                release(tt(q[:, :, 0:HD], full(key)[:, 0:256].rearrange("p (h d) -> p h d", h=4),
                           m[:, 1, :].unsqueeze(2).to_broadcast([P, 4, HD]), ALU.mult), key)
                if n == 0:
                    sums = full("cum")[:, 0:NT * FH].rearrange("p (t h) -> p t h", t=NT)
                    step(v.tensor_copy(cum[:, 0, :, :], sums))
                    release(ts(cum[:, 1, :, :], sums, -1.0, None, ALU.mult), "cum")
                hs = slice(4 * j, 4 * j + 4)
                step(v.tensor_copy(q[:, :, HD + part], cum[:, part, t, hs]))
                chain(v.memset(q[:, :, HD + 1 - part], 1.0), S["qn_done"])

            for i, (piece, s) in enumerate(fox_slots):
                if i == 2:
                    z, e = gate_T[0:FH, 0, :], gate_T[0:FH, 1, :]
                    release(ts(z, full("fox_f")[0:FH, :], gains[0:FH, 6:7], None, ALU.add), "fox_f")
                    chain(stt(e, z, -1.0, z, ALU.mult, ALU.min), S["f_arg"])
                    step(ts(z, z, 0.0, None, ALU.min))
                    dve.wait_ge(S["f_ln"], 1)
                    chain(v.tensor_tensor_scan(z, z, e, 0.0, ALU.add, ALU.subtract), S["logf_done"])
                if heads_at(i - 2):
                    fox_heads(*heads_at(i - 2))
                if heads_at(i - 1):
                    square_sums(*heads_at(i - 1))
                if s is not None and s < F_UNITS:
                    n = (s % NT + 1) * P
                    c = 32 + s % 4
                    if s >= 4:
                        dve.wait_ge(S["fexp"], s - 3)
                    chain(v.tensor_reduce(small[:, c:c + 1], full(("fs", s))[:, 0:n], AX_X, ALU.max, negate=True),
                          S["fmax"])
                if s is not None and s >= 3:
                    u = s - 3
                    h, i = u // NT, u % NT
                    key = ("fv", u)
                    acc = full(key)
                    step(v.reciprocal(small[:, 40:41], small[:, 36 + u % 4:37 + u % 4]))
                    o = o_fox[:, i, h * HD:(h + 1) * HD]
                    if h < 8:
                        release(ts(o, acc[:, 0:HD], small[:, 40:41], None, ALU.mult), key)
                    else:
                        dve.wait_ge(S["g_done"], i + 1)
                        release(stt(o, acc[:, 0:HD], small[:, 40:41], o, ALU.mult, ALU.mult), key)
                    dve.sem_inc(S["ffin"], 1)
            for t in range(NT):
                dve.wait_ge(S["g_done"], NT + t + 1)
                o = o_fox[:, t, 0:512]
                chain(tt(o, o, fox_gate(0, t), ALU.mult), S["o_ready"])
            mixer_tail(1)
            swiglu_dve(1)


_INS = ["x", "even_w_in", "even_w_out", "hgrn_lb_logits", "diff_lq1", "diff_lk1", "diff_lq2", "diff_lk2",
        "hgrn_norm_g", "diff_norm_g", "fox_w_in", "fox_w_out", "fox_b_f", "fox_qnorm_g", "fox_knorm_g",
        "ffn_w1", "ffn_w2", "ln1_g", "ln1_b", "ln2_g", "ln2_b"]


def _constants():
    import numpy as np

    i = np.arange(P)
    masks = np.zeros((P, 2 + len(LEVELS), P), np.float32)
    masks[:, 0, :] = np.where(i[None, :] > i[:, None], -1e30, 0.0)
    masks[:, 1, :] = np.where(i[None, :] // CHUNK > i[:, None] // CHUNK, -1e30, 0.0)
    for n, z in enumerate(LEVELS):
        same = i[:, None] // (2 * z) == i[None, :] // (2 * z)
        masks[:, 2 + n, :] = same & (i[:, None] % (2 * z) < z) & (i[None, :] % (2 * z) >= z)
    s, t = i[:, None], i[None, :]
    spans = np.zeros((P, len(LEVELS) + 2, P), np.float32)
    for n, z in enumerate(LEVELS):
        same = s // (2 * z) == t // (2 * z)
        spans[:, n, :] = same & np.where(t % (2 * z) < z, (s > t) & (s % (2 * z) < z), (s <= t) & (s % (2 * z) >= z))
    spans[:, len(LEVELS), :] = s <= t
    spans[:, len(LEVELS) + 1, :] = s > t
    return {
        "c_ident": np.eye(P, dtype=np.float32),
        "c_masks": masks,
        "c_spans": spans,
        "c_ones": np.ones((P, 2), np.float32),
    }


def kernel(**inputs):
    import numpy as _np
    import concourse.bacc as _bacc
    from concourse import mybir as _mybir
    from concourse.bass_utils import run_bass_kernel_spmd as _run

    nc = _bacc.Bacc("TRN2", target_bir_lowering=False, num_devices=1)
    arrays, args = {}, {}
    for name, a in [(n, inputs[n]) for n in _INS] + list(_constants().items()):
        a = _np.ascontiguousarray(a)
        arrays[f"in_{name}_dram"] = a
        args[name] = nc.dram_tensor(f"in_{name}_dram", a.shape, _mybir.dt.from_np(a.dtype),
                                    kind="ExternalInput").ap()
    out = nc.dram_tensor("out_0_dram", (1, TS, D), F32, kind="ExternalOutput").ap()
    build(nc, args, out)
    r = _run(nc, [arrays], core_ids=[0])
    return r.results[0]["out_0_dram"]
```
